# Optimizing a Trainium2 kernel written in Bass

```python
import math
import jax, jax.numpy as jnp
from jax import lax
import numpy as np

D_MODEL = 1024
BATCH = 1
SEQ = 512
DEPTH = 2
DEC_BATCH = 8
DEC_SEQ = 1
PAST_LEN = 2048
PAGE_SIZE = 128

EPS = 1e-5
ROPE_THETA = 10000.0
A_HEADS = 8
A_HEAD_DIM = 64
A_WIDTH = A_HEADS * A_HEAD_DIM
A_BRANCHES = ((128, 1), (512, 4), (2048, 16))
A_BUF = 2048
A_QBLOCK = 128
B_HEADS = 4
B_KEY_DIM = 64
B_VAL_DIM = 128
B_QK_WIDTH = B_HEADS * B_KEY_DIM
B_V_WIDTH = B_HEADS * B_VAL_DIM
B_GATE_RANK = 16
B_GATE_TAU = 16.0
B_CHUNK = 64
L0_SPLITS = (A_WIDTH, A_WIDTH, A_WIDTH, B_QK_WIDTH, B_QK_WIDTH, B_V_WIDTH, B_GATE_RANK, B_V_WIDTH)
L0_IN = A_WIDTH * 3 + B_QK_WIDTH * 2 + B_V_WIDTH * 2 + B_GATE_RANK
L0_MIX = A_WIDTH + B_V_WIDTH
C_INNER = 2 * D_MODEL
C_HEAD_DIM = 64
C_HEADS = C_INNER // C_HEAD_DIM
C_GROUPS = 8
C_STATE = 128
C_CONV = 4
C_CONV_DIM = C_INNER + 2 * C_GROUPS * C_STATE
C_CHUNK = 128
L1_IN = C_INNER + C_CONV_DIM + C_HEADS
DT_MIN = 1e-3
DT_MAX = 1e-1
D_FF = 4 * D_MODEL

kernel_name = 'dilated_gla_ssd_hybrid_step'

def split_cols(x, sizes):
    return jnp.split(x, np.cumsum(sizes)[:-1].tolist(), axis=-1)

def rms_norm(x, w):
    xf = x.astype(jnp.float32)
    y = xf * lax.rsqrt(jnp.mean(xf * xf, axis=-1, keepdims=True) + EPS)
    return (y * w.astype(jnp.float32)).astype(x.dtype)

def rope(x, pos):
    half = x.shape[-1] // 2
    inv_freq = ROPE_THETA ** (-jnp.arange(half, dtype=jnp.float32) / half)
    ang = pos.astype(jnp.float32)[:, None] * inv_freq[None, :]
    cos = jnp.cos(ang)[None, :, None, :]
    sin = jnp.sin(ang)[None, :, None, :]
    xf = x.astype(jnp.float32)
    x1, x2 = xf[..., :half], xf[..., half:]
    return jnp.concatenate([x1 * cos - x2 * sin, x2 * cos + x1 * sin], axis=-1).astype(x.dtype)

def dilated_window_attention(q, k_all, v_all):
    bsz, t_len, n_h, hd = q.shape
    prefix = k_all.shape[1] - t_len
    pad = ((0, 0), (A_BUF, 0), (0, 0), (0, 0))
    k_pad = jnp.pad(k_all, pad).astype(jnp.float32)
    v_pad = jnp.pad(v_all, pad).astype(jnp.float32)
    qb = A_QBLOCK if t_len % A_QBLOCK == 0 else t_len
    n_blk = t_len // qb
    q_blocks = jnp.moveaxis(q.astype(jnp.float32).reshape(bsz, n_blk, qb, n_h, hd), 1, 0) * (hd ** -0.5)
    starts = jnp.arange(n_blk, dtype=jnp.int32) * qb

    def block(args):
        q_blk, start = args
        q_idx = A_BUF + prefix + start + jnp.arange(qb, dtype=jnp.int32)
        lses, outs = [], []
        for window, dil in A_BRANCHES:
            offs = dil * jnp.arange(window // dil + 1, dtype=jnp.int32)
            k_idx = q_idx[:, None] - offs[None, :]
            valid = k_idx >= A_BUF
            k_g = k_pad[:, k_idx]
            v_g = v_pad[:, k_idx]
            s = jnp.einsum('bqhd,bqkhd->bhqk', q_blk, k_g)
            s = jnp.where(valid[None, None], s, -jnp.inf)
            lse = jax.nn.logsumexp(s, axis=-1)
            p = jnp.exp(s - lse[..., None])
            outs.append(jnp.einsum('bhqk,bqkhd->bhqd', p, v_g))
            lses.append(lse)
        w = jax.nn.softmax(jnp.stack(lses), axis=0)
        o = jnp.sum(w[..., None] * jnp.stack(outs), axis=0)
        return jnp.transpose(o, (0, 2, 1, 3))

    out = lax.map(block, (q_blocks, starts))
    return jnp.moveaxis(out, 0, 1).reshape(bsz, t_len, n_h, hd).astype(q.dtype)

def gla_chunked(q, k, v, log_a, s0):
    bsz, t_len, n_h, dk = q.shape
    dv = v.shape[-1]
    c = B_CHUNK if t_len % B_CHUNK == 0 else t_len
    n = t_len // c
    f32 = jnp.float32
    q, k, v, g = (t.astype(f32).reshape(bsz, n, c, n_h, t.shape[-1]) for t in (q, k, v, log_a))
    b = jnp.cumsum(g, axis=2)
    b_end = b[:, :, -1:]
    q_dec = q * jnp.exp(b)
    k_dec = k * jnp.exp(-b)
    k_end = k * jnp.exp(b_end - b)
    causal = jnp.tril(jnp.ones((c, c), dtype=bool))
    att = jnp.where(causal, jnp.einsum('bnqhd,bnkhd->bnhqk', q_dec, k_dec), 0.0)
    o_intra = jnp.einsum('bnhqk,bnkhe->bnqhe', att, v)
    u = jnp.einsum('bnkhd,bnkhe->nbhde', k_end, v)
    decay = jnp.moveaxis(jnp.exp(b_end[:, :, 0]), 1, 0)

    def step(s, inp):
        u_c, d_c = inp
        return d_c[..., None] * s + u_c, s

    s_fin, s_start = lax.scan(step, s0.astype(f32), (u, decay))
    o_inter = jnp.einsum('bnqhd,nbhde->bnqhe', q_dec, s_start)
    return (o_intra + o_inter).reshape(bsz, t_len, n_h, dv), s_fin

def ssd_chunked(x, dt, a_neg, bm, cm, s0):
    bsz, t_len, n_h, hp = x.shape
    n_g, n_s = bm.shape[2], bm.shape[3]
    hpg = n_h // n_g
    q_len = C_CHUNK if t_len % C_CHUNK == 0 else t_len
    n = t_len // q_len
    f32 = jnp.float32
    xdt = (x.astype(f32) * dt[..., None]).reshape(bsz, n, q_len, n_g, hpg, hp)
    cum = jnp.cumsum((dt * a_neg).reshape(bsz, n, q_len, n_g, hpg), axis=2)
    bm = bm.astype(f32).reshape(bsz, n, q_len, n_g, n_s)
    cm = cm.astype(f32).reshape(bsz, n, q_len, n_g, n_s)
    causal = jnp.tril(jnp.ones((q_len, q_len), dtype=bool))
    cum_t = jnp.moveaxis(cum, 2, -1)
    seg = jnp.exp(jnp.where(causal, cum_t[..., :, None] - cum_t[..., None, :], -jnp.inf))
    cb = jnp.einsum('bntgk,bnsgk->bngts', cm, bm)
    y_intra = jnp.einsum('bngts,bngjts,bnsgjp->bntgjp', cb, seg, xdt)
    to_end = jnp.exp(cum[:, :, -1:] - cum)
    u = jnp.einsum('bnsgk,bnsgj,bnsgjp->nbgjpk', bm, to_end, xdt)
    chunk_decay = jnp.moveaxis(jnp.exp(cum[:, :, -1]), 1, 0)

    def step(s, inp):
        u_c, d_c = inp
        return d_c[..., None, None] * s + u_c, s

    s_init = s0.astype(f32).reshape(bsz, n_g, hpg, hp, n_s)
    s_fin, s_start = lax.scan(step, s_init, (u, chunk_decay))
    y_inter = jnp.einsum('bntgk,nbgjpk,bntgj->bntgjp', cm, s_start, jnp.exp(cum))
    y = (y_intra + y_inter).reshape(bsz, t_len, n_h, hp)
    return y, s_fin.reshape(bsz, n_h, hp, n_s)

def attn_gla_mixer(h, pos, win_k, win_v, gla_state, w_in, w_gate, b_gate, w_onorm, w_out):
    bsz, t_len, _ = h.shape
    q_a, k_a, v_a, q_b, k_b, v_b, g_low, r_b = split_cols(h @ w_in, L0_SPLITS)
    q_a = rope(q_a.reshape(bsz, t_len, A_HEADS, A_HEAD_DIM), pos)
    k_a = rope(k_a.reshape(bsz, t_len, A_HEADS, A_HEAD_DIM), pos)
    k_all = jnp.concatenate([win_k.astype(h.dtype), k_a], axis=1)
    v_all = jnp.concatenate([win_v.astype(h.dtype), v_a.reshape(bsz, t_len, A_HEADS, A_HEAD_DIM)], axis=1)
    o_a = dilated_window_attention(q_a, k_all, v_all).reshape(bsz, t_len, A_WIDTH)
    keep = min(A_BUF, k_all.shape[1])
    log_a = jax.nn.log_sigmoid((g_low @ w_gate + b_gate).astype(jnp.float32)) / B_GATE_TAU
    heads_k = lambda t: t.reshape(bsz, t_len, B_HEADS, B_KEY_DIM)
    o_b, gla_new = gla_chunked(heads_k(q_b) * (B_KEY_DIM ** -0.5), heads_k(k_b),
                               v_b.reshape(bsz, t_len, B_HEADS, B_VAL_DIM), heads_k(log_a), gla_state)
    o_b = rms_norm(o_b, w_onorm) * jax.nn.silu(r_b.astype(jnp.float32).reshape(bsz, t_len, B_HEADS, B_VAL_DIM))
    mix = jnp.concatenate([o_a, o_b.reshape(bsz, t_len, B_V_WIDTH).astype(h.dtype)], axis=-1)
    return mix @ w_out, k_all[:, -keep:], v_all[:, -keep:], gla_new

def ssd_mixer(h, conv_state, ssm_state, w_in, conv_w, conv_b, dt_bias, a_log, d_skip, w_gnorm, w_out):
    bsz, t_len, _ = h.shape
    f32 = jnp.float32
    z, xbc, dt = split_cols(h @ w_in, (C_INNER, C_CONV_DIM, C_HEADS))
    xbc_ext = jnp.concatenate([conv_state.astype(h.dtype), xbc], axis=1)
    conv = lax.conv_general_dilated(xbc_ext, conv_w[:, None, :].astype(h.dtype), (1,), 'VALID',
                                    dimension_numbers=('NWC', 'WIO', 'NWC'),
                                    feature_group_count=C_CONV_DIM)
    xbc_c = jax.nn.silu(conv + conv_b)
    xs, bm, cm = split_cols(xbc_c, (C_INNER, C_GROUPS * C_STATE, C_GROUPS * C_STATE))
    xs = xs.reshape(bsz, t_len, C_HEADS, C_HEAD_DIM)
    dt = jax.nn.softplus(dt.astype(f32) + dt_bias.astype(f32))
    y, ssm_new = ssd_chunked(xs, dt, -jnp.exp(a_log.astype(f32)),
                             bm.reshape(bsz, t_len, C_GROUPS, C_STATE),
                             cm.reshape(bsz, t_len, C_GROUPS, C_STATE), ssm_state)
    y = y + d_skip.astype(f32)[:, None] * xs.astype(f32)
    y = y.reshape(bsz, t_len, C_INNER) * jax.nn.silu(z.astype(f32))
    y = rms_norm(y.reshape(bsz, t_len, C_GROUPS, C_INNER // C_GROUPS),
                 w_gnorm.reshape(C_GROUPS, C_INNER // C_GROUPS)).reshape(bsz, t_len, C_INNER)
    return y.astype(h.dtype) @ w_out, xbc_ext[:, -(C_CONV - 1):], ssm_new

def sq_relu_mlp(h, w_up, w_down):
    u = jnp.maximum(h @ w_up, 0)
    return (u * u) @ w_down

def trunk(x, pos0, states, p):
    bsz, t_len, _ = x.shape
    pos = pos0 + jnp.arange(t_len, dtype=jnp.int32)
    h = x
    new_k, new_v, new_gla, new_conv, new_ssm = [], [], [], [], []
    for layer in range(DEPTH):
        i = layer // 2
        hn = rms_norm(h, p['norm_mix'][layer])
        if layer % 2 == 0:
            if states is None:
                ck = jnp.zeros((bsz, 0, A_HEADS, A_HEAD_DIM), x.dtype)
                cv = ck
                gs = jnp.zeros((bsz, B_HEADS, B_KEY_DIM, B_VAL_DIM), jnp.float32)
            else:
                ck, cv, gs = states[0][i], states[1][i], states[2][i]
            out, k_i, v_i, g_i = attn_gla_mixer(hn, pos, ck, cv, gs, p['w_in_ab'][i], p['w_gate_b'][i],
                                                p['b_gate_b'][i], p['w_onorm_b'][i], p['w_out_ab'][i])
            new_k.append(k_i)
            new_v.append(v_i)
            new_gla.append(g_i)
        else:
            if states is None:
                cs = jnp.zeros((bsz, C_CONV - 1, C_CONV_DIM), x.dtype)
                ss = jnp.zeros((bsz, C_HEADS, C_HEAD_DIM, C_STATE), jnp.float32)
            else:
                cs, ss = states[3][i], states[4][i]
            out, c_i, s_i = ssd_mixer(hn, cs, ss, p['w_in_c'][i], p['conv_w'][i], p['conv_b'][i],
                                      p['dt_bias'][i], p['a_log'][i], p['d_skip'][i],
                                      p['w_gnorm_c'][i], p['w_out_c'][i])
            new_conv.append(c_i)
            new_ssm.append(s_i)
        h = h + out
        h = h + sq_relu_mlp(rms_norm(h, p['norm_mlp'][layer]), p['w_up'][layer], p['w_down'][layer])
    y = rms_norm(h, p['norm_final'])
    return (y, jnp.stack(new_k), jnp.stack(new_v), jnp.stack(new_gla), jnp.stack(new_conv), jnp.stack(new_ssm))

def setup_inputs(seed: int = 0) -> dict:
    key = jax.random.key(seed)
    keys = iter(jax.random.split(key, 32))

    def nrm(shape, scale):
        return jax.random.normal(next(keys), shape, jnp.float32) * scale

    n_even = (DEPTH + 1) // 2
    n_odd = DEPTH // 2
    win_len = min(A_BUF, PAST_LEN)
    dt_init = jnp.exp(jax.random.uniform(next(keys), (n_odd, C_HEADS), jnp.float32,
                                         math.log(DT_MIN), math.log(DT_MAX)))
    a_init = jax.random.uniform(next(keys), (n_odd, C_HEADS), jnp.float32, 1.0, 16.0)
    return {
        'x_prompt': nrm((BATCH, SEQ, D_MODEL), 1.0),
        'x_sample': nrm((DEC_BATCH, DEC_SEQ, D_MODEL), 1.0),
        'cache_win_k': nrm((n_even, DEC_BATCH, win_len, A_HEADS, A_HEAD_DIM), 1.0),
        'cache_win_v': nrm((n_even, DEC_BATCH, win_len, A_HEADS, A_HEAD_DIM), 1.0),
        'state_gla': nrm((n_even, DEC_BATCH, B_HEADS, B_KEY_DIM, B_VAL_DIM), 1.0),
        'state_conv': nrm((n_odd, DEC_BATCH, C_CONV - 1, C_CONV_DIM), 1.0),
        'state_ssm': nrm((n_odd, DEC_BATCH, C_HEADS, C_HEAD_DIM, C_STATE), 0.1),
        'norm_mix': 1.0 + nrm((DEPTH, D_MODEL), 0.02),
        'norm_mlp': 1.0 + nrm((DEPTH, D_MODEL), 0.02),
        'norm_final': 1.0 + nrm((D_MODEL,), 0.02),
        'w_in_ab': nrm((n_even, D_MODEL, L0_IN), D_MODEL ** -0.5),
        'w_gate_b': nrm((n_even, B_GATE_RANK, B_QK_WIDTH), B_GATE_RANK ** -0.5),
        'b_gate_b': nrm((n_even, B_QK_WIDTH), 0.1),
        'w_onorm_b': 1.0 + nrm((n_even, B_VAL_DIM), 0.02),
        'w_out_ab': nrm((n_even, L0_MIX, D_MODEL), L0_MIX ** -0.5),
        'w_in_c': nrm((n_odd, D_MODEL, L1_IN), D_MODEL ** -0.5),
        'conv_w': nrm((n_odd, C_CONV, C_CONV_DIM), C_CONV ** -0.5),
        'conv_b': nrm((n_odd, C_CONV_DIM), 0.02),
        'dt_bias': dt_init + jnp.log(-jnp.expm1(-dt_init)),
        'a_log': jnp.log(a_init),
        'd_skip': 1.0 + nrm((n_odd, C_HEADS), 0.02),
        'w_gnorm_c': 1.0 + nrm((n_odd, C_INNER), 0.02),
        'w_out_c': nrm((n_odd, C_INNER, D_MODEL), C_INNER ** -0.5),
        'w_up': nrm((DEPTH, D_MODEL, D_FF), D_MODEL ** -0.5),
        'w_down': nrm((DEPTH, D_FF, D_MODEL), D_FF ** -0.5),
    }

def reference(x_prompt, x_sample, cache_win_k, cache_win_v, state_gla, state_conv, state_ssm,
              norm_mix, norm_mlp, norm_final, w_in_ab, w_gate_b, b_gate_b, w_onorm_b, w_out_ab,
              w_in_c, conv_w, conv_b, dt_bias, a_log, d_skip, w_gnorm_c, w_out_c, w_up, w_down):
    p = {'norm_mix': norm_mix, 'norm_mlp': norm_mlp, 'norm_final': norm_final,
         'w_in_ab': w_in_ab, 'w_gate_b': w_gate_b, 'b_gate_b': b_gate_b, 'w_onorm_b': w_onorm_b,
         'w_out_ab': w_out_ab, 'w_in_c': w_in_c, 'conv_w': conv_w, 'conv_b': conv_b,
         'dt_bias': dt_bias, 'a_log': a_log, 'd_skip': d_skip, 'w_gnorm_c': w_gnorm_c,
         'w_out_c': w_out_c, 'w_up': w_up, 'w_down': w_down}
    y_prompt, p_k, p_v, p_gla, p_conv, p_ssm = trunk(x_prompt, 0, None, p)
    y_sample, s_k, s_v, s_gla, s_conv, s_ssm = trunk(
        x_sample, PAST_LEN, (cache_win_k, cache_win_v, state_gla, state_conv, state_ssm), p)
    return (y_prompt, y_sample, p_k, p_v, p_gla, p_conv, p_ssm, s_k, s_v, s_gla, s_conv, s_ssm)


_drawn_inputs = setup_inputs


def setup_inputs(seed=0):
    import zlib

    import numpy as np

    out = dict(_drawn_inputs(seed))
    spreads = {}
    factors = {'norm_final': 7.946,
     'w_onorm_b': 4.232,
     'd_skip': 35.432,
     'w_gnorm_c': 14.783,
     'norm_mlp': 3.238}
    for name, (base, spread) in spreads.items():
        noise = np.random.default_rng([zlib.crc32(name.encode()), seed]).standard_normal(out[name].shape)
        drawn = base * np.exp(spread * noise) if base else spread * noise
        out[name] = __import__('jax').numpy.asarray(drawn.astype(out[name].dtype))
    for name, factor in factors.items():
        out[name] = (out[name] * factor).astype(out[name].dtype)
    return out
```

```python
from contextlib import ExitStack

import numpy as np

import concourse.bass as bass
from concourse import mybir

F32 = mybir.dt.float32
U32 = mybir.dt.uint32
ALU = mybir.AluOpType
ACT = mybir.ActivationFunctionType
AX = mybir.AxisListType.X

P = 128
D = 1024
DC = D // P
TP = 512
NB = 8
T = TP + NB
LO, HI = 256, T - 256
NT = TP // P
EPS = 1e-5

AH, AD = 8, 64
AW = AH * AD
HP = AW // P
WIN = 2048
BRANCHES = ((128, 1), (512, 4), (2048, 16))
NBR = len(BRANCHES)
BH, BK, BV = 4, 64, 128
GP = BH // 2
RANK, TAU, CH = 16, 16.0, 64
NCH = TP // CH
FF = 4096
FC = FF // P

CI = 2048
CG, CHD, CN = 8, 64, 128
CJ = 4
CH_ALL = CG * CJ
TAPS = 4
GW = CI // CG
SCALE = AD ** -0.5

RING = 8
SLOTS = 2
SSD_UNITS = 6
U_ATT = 0
U_GLA = U_ATT + 3 * HP
U_OUT0 = U_GLA + 6 * GP
U_UP0 = U_OUT0 + DC
U_DOWN0 = U_UP0 + FC
U_SSD = U_DOWN0 + DC * (FF // D)
U_OUT1 = U_SSD + SSD_UNITS * CG
U_UP1 = U_OUT1 + DC * (CI // D)
U_DOWN1 = U_UP1 + FC
N_UNITS = U_DOWN1 + DC * (FF // D)
T_NORM0 = 0
T_ATT = 1
T_GATE = T_ATT + 3 * HP
T_GLA = T_GATE + 1
T_OUT0 = T_GLA + 6 * GP
T_OUT0B = T_OUT0 + DC
T_NORM1 = T_OUT0B + DC
T_UP0 = T_NORM1 + 1
T_DOWN0 = T_UP0 + FC
T_NORM2 = T_DOWN0 + DC
T_DT = T_NORM2 + 1
T_SSD = T_DT + 1
T_OUT1 = T_SSD + SSD_UNITS * CG
T_NORM3 = T_OUT1 + DC
T_UP1 = T_NORM3 + 1
T_DOWN1 = T_UP1 + FC
T_NORM4 = T_DOWN1 + DC

PW = 120
LEAST = -3.0e38
NEVER = -1.0e30
LOG1P = [1.0 / n for n in (15, 13, 11, 9, 7, 5, 3)]
COPIES = [("k", b) for b in range(NB)] + [("v", b) for b in range(NB)]


class Tally:

    def __init__(self, eng):
        self.eng, self.total, self.round, self.per, self.here = eng, {}, None, {}, {}

    def start(self, name, i):
        self.name, self.round, self.here = name, i, {}

    def end(self):
        known = self.per.setdefault(self.name, dict(self.here))
        assert known == self.here
        self.round = None

    def done(self, ins, sem):
        self.mark(ins, sem)
        if self.round is None:
            self.eng.wait_ge(sem, self.total[id(sem)])
        else:
            n = self.here[id(sem)]
            per = self.per.get(self.name)
            self.eng.wait_ge(sem, n if per is None else self.round * per[id(sem)] + n)

    def mark(self, ins, sem):
        ins.then_inc(sem, 1)
        where = self.total if self.round is None else self.here
        where[id(sem)] = where.get(id(sem), 0) + 1


def build(nc, A):
    ctx = ExitStack()
    with ctx:
        sems = {}

        def sem(name):
            if name not in sems:
                sems[name] = ctx.enter_context(nc.semaphore(name))
            return sems[name]

        def sb(name, shape, dt=F32, stack=ctx):
            return stack.enter_context(nc.sbuf_tensor(name, shape, dt))

        def flat(ap):
            names = "abcd"[:len(ap.shape) - 1]
            return ap.rearrange(f"p {' '.join(names)} -> p ({' '.join(names)})")

        B = [ctx.enter_context(nc.psum_tensor(f"bank{i}", [P, 512], F32)) for i in range(8)]

        ring = sb("ring", [P, RING, DC, P])
        h = sb("h", [P, DC, T])
        hn = sb("hn", [P, DC, T])
        std = sb("std", [P, T])
        rstd = sb("rstd", [P, T])
        ident = sb("ident", [P, P])
        ones = sb("ones", [P, P])
        tri = sb("tri", [P, P])
        norms = sb("norms", [P, 5, DC])
        eps = sb("eps", [P, 1])

        wdt = sb("wdt", [P, DC, CH_ALL])
        dtb = sb("dtb", [P, CH_ALL])
        nega = sb("nega", [P, CH_ALL])
        parm = sb("parm", [P, CG, PW])
        deltac = sb("deltac", [NB, NB])

        a = ExitStack()
        rotm = sb("rotm", [P, P], stack=a)
        cos = sb("cos", [P, T], stack=a)
        sin = sb("sin", [P, T], stack=a)
        lncount = sb("lncount", [P, TP], stack=a)
        selb = sb("selb", [NB, NB, P], stack=a)
        rep = sb("rep", [NB, NB * AH], stack=a)
        ownhead = sb("ownhead", [NB * AH, AW], stack=a)
        delta = sb("delta", [NB, NB], stack=a)
        tri64 = sb("tri64", [P, P], stack=a)
        mask64 = sb("mask64", [P, P], U32, stack=a)
        wglow = sb("wglow", [P, DC, RANK], stack=a)
        wgate = sb("wgate", [RANK, BH * BK], stack=a)
        bgate = sb("bgate", [P, GP], stack=a)
        wonorm = sb("wonorm", [P, 1], stack=a)
        mixT = sb("mixT", [P, DC, T], stack=a)
        samp = sb("samp", [NB, 3, AW], stack=a)
        gath = sb("gath", [P, SLOTS, NBR, AW], stack=a)
        gprod = sb("gprod", [P, NBR, AW], stack=a)
        s3 = sb("s3", [P, NBR, NB * AH], stack=a)
        krep = gprod[0:NB * AH, 0]
        kscr = gprod[0:NB * AH, 1]
        vrep = gprod[0:NB * AH, 2]
        sexp = sb("sexp", [NB * AH, NBR, P], stack=a)
        sst = sb("sst", [NB * AH, 10], stack=a)
        sdiag = sb("sdiag", [NB * AH, NB * AH], stack=a)
        spt = sb("spt", [P, NBR, NB * AH], stack=a)
        glow = sb("glow", [RANK, T], stack=a)
        qg = sb("qg", [P, GP, T], stack=a)
        kg = sb("kg", [P, GP, T], stack=a)
        vg = sb("vg", [P, BH, T], stack=a)
        rg = sb("rg", [P, BH, T], stack=a)
        b0 = ExitStack()
        qraw = sb("qraw", [P, T], stack=b0)
        kraw = sb("kraw", [P, T], stack=b0)
        vraw = sb("vraw", [P, T], stack=b0)
        qr = sb("qr", [P, T], stack=b0)
        kr = sb("kr", [P, T], stack=b0)
        rt = sb("rt", [P, 2, T], stack=b0)
        vtok = sb("vtok", [P, NT, P], stack=b0)
        probs = sb("probs", [P, NT, TP], stack=b0)
        pstat = sb("pstat", [P, 4, NT], stack=b0)
        pt = sb("pt", [P, 2, TP], stack=b0)
        b0.close()
        b1 = ExitStack()
        gt = sb("gt", [P, 6, T], stack=b1)
        vdiag = gt[0:NB, 2:6].rearrange("p i t -> p (i t)")[:, 0:2 * NB * P].rearrange(
            "p (e b v) -> p e b v", e=2, b=NB)
        loga = sb("loga", [P, GP, T], stack=b1)
        latok = sb("latok", [P, NT, P], stack=b1)
        bT = sb("bT", [P, NCH, CH], stack=b1)
        eb = sb("eb", [P, GP, NCH, CH], stack=b1)
        enb = sb("enb", [P, GP, NCH, CH], stack=b1)
        ee = sb("ee", [P, GP, NCH, CH], stack=b1)
        sdec = sb("sdec", [P, GP, NB], stack=b1)
        rows_left = flat(gath[:])
        gst = rows_left[:, 0:(NCH + 1) * P].rearrange("p (c v) -> p c v", v=P)
        ketok = rows_left[:, (NCH + 1) * P:(NCH + 1) * P + TP].rearrange("p (t k) -> p t k", k=P)
        gvtok = rows_left[:, (NCH + 1) * P + TP:(NCH + 1) * P + 3 * TP].rearrange("p (e t v) -> p e t v", e=2, v=P)
        gsamp = sb("gsamp", [NB, 3, P], stack=b1)
        att = sb("att", [P, 2, NT, P], stack=b1)
        gs0 = sb("gs0", [P, NB, P], stack=b1)
        b1.close()
        a.close()

        m = ExitStack()
        hid = sb("hid", [P, FC, T], stack=m)
        m.close()

        c = ExitStack()
        pg = sb("pg", [P, 2, 24], stack=c)
        dts = sb("dts", [P, 8, NT + 1, CH_ALL], stack=c)
        dtg = sb("dtg", [P, 2, NT + 1, CJ], stack=c)
        dag = sb("dag", [P, 2, NT + 1, CJ], stack=c)
        xe = sb("xe", [P, 4, TAPS - 1 + TP], stack=c)
        xs = sb("xs", [P, 4, TAPS, NB], stack=c)
        xsp = sb("xsp", [P, 4, TAPS, NB], stack=c)
        conv = sb("conv", [P, 2, 4, T], stack=c)
        th = sb("th", [P, 2, T], stack=c)
        gz = sb("gz", [P, 2, 2, T], stack=c)
        ths = sb("ths", [P, 4, NB], stack=c)
        ystd = sb("ystd", [P, T], stack=c)
        yrstd = sb("yrstd", [P, T], stack=c)
        cum = sb("cum", [P, 2, NT, CJ], stack=c)
        dec = sb("dec", [P, NT, CJ], stack=c)
        toend = sb("toend", [P, NT, CJ], stack=c)
        xdt = sb("xdt", [P, NT, CJ, CHD], stack=c)
        btok = sb("btok", [P, NT, P], stack=c)
        cbm = sb("cbm", [P, NT, P], stack=c)
        seg = sb("seg", [P, CJ, NT, P], stack=c)
        st = sb("st", [P, NT - 1, CJ, CHD], stack=c)
        std1 = sb("std1", [P, CJ, CHD], stack=c)
        turns3 = sb("turns3", [P, 2 * T], stack=c)
        xde = turns3[:, 0:NT * GW].rearrange("p (t j q) -> p t j q", j=CJ, q=CHD)
        ytmp = turns3[:, 0:2 * (TP - P)].rearrange("p (i t) -> p i t", i=2)
        ysq = turns3[:].rearrange("p (i t) -> p i t", i=2)
        efeat = sb("efeat", [P, 2, TP - P], stack=c)
        yT = sb("yT", [P, 2, T], stack=c)
        ssamp = sb("ssamp", [NB, 3, P], stack=c)
        sxdt = sb("sxdt", [NB, CJ, CHD], stack=c)
        sadg = sb("sadg", [NB, 2, NB, CJ], stack=c)
        sadec = sb("sadec", [P, NB, CJ], stack=c)
        sxdiag = seg[0:NB].rearrange("k j t q -> k (j t q)").rearrange("k (b c) -> k b c", b=NB)
        ss0 = sb("ss0", [P, NB, CJ, CHD], stack=c)
        yout = sb("yout", [P, 2 * CG, T], stack=c)
        pconv = sb("pconv", [P, CG, 4, TAPS - 1], stack=c)
        sconv = sb("sconv", [P, CG, 4, TAPS - 1, NB], stack=c)
        pssm = sb("pssm", [P, CJ, CHD], stack=c)
        c.close()

        x_in = [sem(f"x_in{i}") for i in range(DC // 2)]
        norm_consts_in = sem("norm_consts_in")
        consts_in = sem("consts_in")
        late_consts_in = sem("late_consts_in")
        units_multiplied = sem("units_multiplied")
        copied = [sem("pair0_copied"), sem("pair1_copied")]
        ring_in = [sem(f"ring{s}_in") for s in range(RING)]
        squares = sem("squares")
        squares_added = sem("squares_added")
        norm_summed = sem("norm_summed")
        std_ready = sem("std_ready")
        hn_ready = sem("hn_ready")
        hidden = sem("hidden")
        caches_written = sem("caches_written")

        def lo(n):
            return B[2 * (n % 2)][:, 0:LO]

        def hi(n):
            return B[2 * (n % 2) + 1][:, 0:HI]

        def turns_before(n):
            return n // 2

        MATMULS = [(slice(0, LO), lo), (slice(LO, T), hi)]

        NORM_CONSTS = ("ones", "norms", "eps")
        FIRST_CONSTS = ("ident", "rotm", "cos", "sin", "lncount")
        LATE_CONSTS = [n for n in A["consts"] if n not in NORM_CONSTS + FIRST_CONSTS]
        const_tiles = dict(ident=ident, ones=ones, tri=tri, norms=norms, eps=eps, rotm=rotm, cos=cos, sin=sin,
                           lncount=lncount, selb=selb, rep=rep, ownhead=ownhead, delta=delta, tri64=tri64,
                           mask64=mask64, wglow=wglow, wgate=wgate, bgate=bgate, wonorm=wonorm, wdt=wdt,
                           dtb=dtb, nega=nega, parm=parm, deltac=deltac)
        block = ctx.enter_context(nc.Block())

        @block.sync
        def _(sp):
            for i in (0, 2):
                sp.dma_start(h[:, 2 * i:2 * i + 2], A["xT"][:, 2 * i:2 * i + 2]).then_inc(x_in[i], 16)

            def load(w, s):
                sp.dma_start(flat(ring[:, s]), A["units"][w]).then_inc(ring_in[s], 16)

            for s in range(RING):
                load(s, s)
                if s == 1:
                    for name in FIRST_CONSTS:
                        sp.dma_start(const_tiles[name][:], A["consts"][name]).then_inc(consts_in, 16)
            for name in LATE_CONSTS:
                sp.dma_start(const_tiles[name][:], A["consts"][name]).then_inc(late_consts_in, 16)
            with sp.Fori(1, U_SSD // RING) as i:
                for s in range(RING):
                    sp.wait_ge(units_multiplied, i * RING + (s + 1 - RING))
                    load(i * RING + s, s)
            for s in range(SSD_UNITS):
                sp.wait_ge(units_multiplied, U_SSD - RING + s + 1)
                load(U_SSD + s, s)
            with sp.Fori(1, CG) as g:
                for s in range(SSD_UNITS):
                    sp.wait_ge(units_multiplied, g * SSD_UNITS + (U_SSD - SSD_UNITS + s + 1))
                    load(g * SSD_UNITS + (U_SSD + s), s)
            for s in range(RING):
                if s < SSD_UNITS:
                    sp.wait_ge(units_multiplied, U_OUT1 - SSD_UNITS + s + 1)
                load(U_OUT1 + s, s)
            with sp.Fori(1, (N_UNITS - U_OUT1) // RING) as i:
                for s in range(RING):
                    sp.wait_ge(units_multiplied, i * RING + (U_OUT1 - RING + s + 1))
                    load(i * RING + (U_OUT1 + s), s)
            for k in range(DC):
                sp.wait_ge(hn_ready, 2 * DC * 4 + DC + k + 1)
                sp.dma_start(A["y"][:, k], hn[:, k]).then_inc(sem("y_written"), 16)
            sp.wait_ge(sem("y_written"), 16 * DC)

        @block.gpsimd
        def _(pool):
            copy_sent = [0]

            def cache_copy(units_done):
                kind, b = COPIES[copy_sent[0]]
                copy_sent[0] += 1
                if units_done:
                    pool.wait_ge(units_multiplied, units_done)
                src = A["cache_" + kind][b, 1:WIN].rearrange("t d -> (t d)")
                dst = A["win_" + kind][b, 0:WIN - 1].rearrange("t d -> (t d)")
                pool.dma_start(dst, src).then_inc(caches_written, 16)

            def gather(n):
                kind, b = COPIES[n]
                if n >= SLOTS:
                    if n - SLOTS < NB:
                        pool.wait_ge(sem("keys_scored"), n - SLOTS + 1)
                    else:
                        pool.wait_ge(sem("values_mixed"), n - SLOTS + 1 - NB)
                for i, (w, d) in enumerate(BRANCHES):
                    pool.dma_start(gath[:, n % SLOTS, i], A["cache_" + kind][b, WIN - w:WIN:d]).then_inc(
                        sem(f"gathered{n % SLOTS}"), 16)

            gather(0)
            gather(1)
            for hp in range(HP):
                pool.wait_ge(sem("rope_done"), 2 * hp + 2)
                pool.dma_start(A["pk"][hp], kr[:, 0:TP]).then_inc(sem("k_written"), 16)
                pool.wait_ge(copied[(T_ATT + 3 * hp + 2) % 2], turns_before(T_ATT + 3 * hp + 2) + 1)
                pool.dma_start(A["pv"][hp], vraw[:, 0:TP]).then_inc(sem("v_written"), 16)
            pool.wait_ge(sem("samp_ready"), HP)
            pool.dma_start(A["win_k"][:, WIN - 1, :], samp[:, 1, :]).then_inc(sem("samp_written"), 16)
            pool.dma_start(A["win_v"][:, WIN - 1, :], samp[:, 2, :]).then_inc(sem("samp_written"), 16)
            for n in range(SLOTS, 2 * NB):
                gather(n)
            for gp in range(GP):
                if gp:
                    pool.wait_ge(sem("gla_state_out"), 16)
                    pool.wait_ge(sem("gla_sample_out"), gp)
                else:
                    pool.wait_ge(sem("o_copied"), AH)
                    pool.wait_ge(sem("v_written"), 16 * HP)
                    pool.wait_ge(sem("k_written"), 16 * HP)
                pool.dma_start(gs0[:], A["gla0"][gp]).then_inc(sem("gla_state_in"), 16)
                pool.wait_ge(sem("gla_stepped"), gp + 1)
                pool.dma_start(A["gla1"][gp], gs0[:]).then_inc(sem("gla_state_out"), 16)
                pool.wait_ge(sem("gla_chained"), gp + 1)
                pool.dma_start(A["pgla"][gp], gst[:, NCH]).then_inc(sem("gla_prompt_out"), 16)
            for n in range(2 * NB - 4):
                cache_copy(U_UP0 + 5 * n)
            pool.wait_ge(units_multiplied, U_SSD)

            def states(g):
                pool.dma_start(flat(ss0[:]), A["ssm0"][g]).then_inc(sem("ssm_in"), 16)
                pool.wait_ge(sem("ssm_in"), g * 16 + 16)
                pool.wait_ge(sem("sadec_ready"), g + 1)
                for half in (slice(0, NB // 2), slice(NB // 2, NB)):
                    s = ss0[:, half].rearrange("p b j q -> p (b j) q")
                    decays = sadec[:, half].rearrange("p b j -> p (b j)").unsqueeze(2)
                    nc.gpsimd.tensor_tensor(s, s, decays.to_broadcast((P, NB // 2 * CJ, CHD)), ALU.mult).then_inc(
                        sem("ssm_decayed"), 1)
                pool.wait_ge(sem("ssm_read"), g + 1)
                pool.dma_start(A["ssm1"][g], flat(ss0[:])).then_inc(sem("ssm_out"), 16)
                pool.wait_ge(sem("states_kept"), g + 1)
                pool.dma_start(A["pssm"][g], flat(pssm[:])).then_inc(sem("pssm_out"), 16)
                pool.wait_ge(sem("ssm_out"), g * 16 + 16)

            for g in range(CG):
                states(g)
            pool.wait_ge(sem("conv_kept"), 2 * CG)
            pool.dma_start(A["pconv"], flat(pconv[:])).then_inc(sem("layer1_out"), 16)
            pool.dma_start(A["sconv"], flat(sconv[:])).then_inc(sem("layer1_out"), 16)
            for n in range(4):
                cache_copy(U_UP1 + 4 * n)
            pool.wait_ge(caches_written, 16 * len(COPIES))
            pool.wait_ge(sem("layer1_out"), 32)
            pool.wait_ge(sem("gla_prompt_out"), 16 * GP)
            pool.wait_ge(sem("gla_state_out"), 16 * GP)

        @block.tensor
        def _(pe):
            mm = nc.tensor.matmul

            def unit(w, n, s, count, src, first=0, last=True, start=True, ready=None, blocks=range(DC), used=True):
                pe.wait_ge(ring_in[s], count * 16)
                for cols, half in MATMULS:
                    for k in blocks:
                        if ready is not None:
                            pe.wait_ge(*ready(k, cols.start > 0))
                        x = mm(half(n), ring[:, s, k], src[:, first + k, cols],
                               start=start and k == blocks[0], stop=last and k == blocks[-1])
                x.then_inc(units_multiplied if used else sem("parts_multiplied"), 1)

            def bank_free(n, more=0):
                if n >= 2:
                    pe.wait_ge(copied[n % 2], turns_before(n) + more)

            def norm(r, n):
                bank_free(n)
                pe.wait_ge(squares_added, (r + 1) * DC)
                for cols, half in MATMULS:
                    mm(half(n), ones[:], rstd[:, cols], start=True, stop=True).then_inc(norm_summed, 1)

            def normed(r):
                return lambda k, high: (hn_ready, 2 * DC * r + DC * high + k + 1)

            pe.wait_ge(norm_consts_in, 16 * len(NORM_CONSTS))
            norm(0, T_NORM0)

            at = [0]

            def project():
                w = at[0]
                if w >= U_OUT0:
                    return
                at[0] += 1
                n = T_ATT + w if w < U_GLA else T_GLA + w - U_GLA
                if w == U_GLA:
                    gates()
                bank_free(n)
                unit(w, n, w % RING, w // RING + 1, hn,
                     ready=normed(0) if w == 0 else None)

            def gates():
                n = T_GATE
                bank_free(n)
                pe.wait_ge(late_consts_in, 16 * len(LATE_CONSTS))
                for cols, half in MATMULS:
                    for k in range(DC):
                        x = mm(half(n)[0:RANK], wglow[:, k], hn[:, k, cols], start=k == 0, stop=k == DC - 1)
                x.then_inc(sem("glow_summed"), 1)

            def rotate(hp):
                for i, (raw, n) in enumerate(((qraw, T_ATT + 3 * hp), (kraw, T_ATT + 3 * hp + 1))):
                    pe.wait_ge(copied[n % 2], turns_before(n) + 1)
                    if hp and not i:
                        pe.wait_ge(sem("o_copied"), 2 * hp)
                        pe.wait_ge(sem("pt_copied"), 2 * hp * NT)
                    for j, cols in enumerate((slice(0, LO), slice(LO, T))):
                        x = mm(B[4 + 2 * i + j][:, 0:cols.stop - cols.start], rotm[:], raw[:, cols],
                               start=True, stop=True)
                    x.then_inc(sem("rotated"), 1)

            def to_tokens(hp):
                pe.wait_ge(sem("rope_done"), 2 * hp + 2)
                n = T_ATT + 3 * hp + 2
                pe.wait_ge(copied[n % 2], turns_before(n) + 1)
                for t in range(NT):
                    pe.transpose(B[4][:, t * P:(t + 1) * P], vraw[:, t * P:(t + 1) * P], ident[:])
                for i, src in enumerate((qr, kr, vraw)):
                    x = pe.transpose(B[5][0:NB, i * P:(i + 1) * P], src[:, TP:T], ident[:])
                x.then_inc(sem("v_turned"), 1)

            def scores(hp, e):
                hd = 2 * hp + e
                if e == 0:
                    pe.wait_ge(sem("samp_ready"), hp + 1)
                else:
                    pe.wait_ge(sem("pt_copied"), hd * NT)
                    pe.wait_ge(sem("o_copied"), hd)
                rows = slice(AD * e, AD * e + AD)
                for j in range(NT):
                    mm(B[4 + j][:, 0:(j + 1) * P], qr[rows, j * P:(j + 1) * P], kr[rows, 0:(j + 1) * P],
                       start=True, stop=True).then_inc(sem("scored"), 1)

            def mix_values(hp, e):
                hd = 2 * hp + e
                pe.wait_ge(sem("p_ready"), (hd + 1) * NT)

                def turn(kt):
                    if kt == 3:
                        pe.wait_ge(sem("pt_copied"), hd * NT + 1)
                    for j in range(kt, NT):
                        x = pe.transpose(B[4 + kt % 3][:, (j - kt) * P:(j - kt + 1) * P],
                                         probs[:, j, kt * P:(kt + 1) * P], ident[:])
                    x.then_inc(sem("p_turned"), 1)

                turn(0)
                turn(1)
                for kt in range(NT):
                    if kt + 2 < NT:
                        turn(kt + 2)
                    pe.wait_ge(sem("pt_copied"), hd * NT + kt + 1)
                    mm(B[7][AD * e:AD * e + AD, kt * P:TP], vtok[:, kt, AD * e:AD * e + AD],
                       pt[:, kt % 2, 0:TP - kt * P], start=kt == 0, stop=kt == NT - 1,
                       skip_group_check=True).then_inc(sem("pv_done"), 1)

            def sample_q(b):
                if b < 2:
                    pe.wait_ge(sem("o_copied"), AH)
                    pe.wait_ge(sem("pt_copied"), AH * NT)
                    pe.wait_ge(sem("samp_ready"), HP)
                else:
                    pe.wait_ge(sem("keys_scored"), b - 1)
                mm(B[4 + b % 2][:, 0:AW], selb[:, b, :], samp[:, 0, :], start=True, stop=True).then_inc(
                    sem("sample_q_spread"), 1)

            def sample_rows():
                pe.wait_ge(sem("keys_scored"), NB)
                for i in range(NBR):
                    pe.transpose(B[6][0:NB * AH, i * P:(i + 1) * P], s3[:, i, :], ident[:])
                for i, bank in enumerate((4, 5, 7)):
                    x = mm(B[bank][0:NB * AH, 0:AW], rep[:], samp[:, i, :], start=True, stop=True)
                x.then_inc(sem("sample_rows_ready"), 1)

            def sample_cols():
                pe.wait_ge(sem("sample_probs"), 1)
                for i in range(NBR):
                    x = pe.transpose(B[4][:, i * NB * AH:(i + 1) * NB * AH], sexp[:, i, :],
                                     ident[0:NB * AH, 0:NB * AH])
                x.then_inc(sem("sample_probs_turned"), 1)

            def sample_mix():
                pe.wait_ge(sem("spt_copied"), 1)
                out = B[5][:, 0:HP * NB * 2].rearrange("p (a b e) -> p a b e", a=HP, b=NB)
                for b in range(NB):
                    n = NB + b
                    pe.wait_ge(sem(f"gathered{n % SLOTS}"), 16 * NBR * (n // SLOTS + 1))
                    for hp in range(HP):
                        for i in range(NBR):
                            x = mm(out[:, hp, b, :], gath[:, n % SLOTS, i, hp * P:(hp + 1) * P],
                                   spt[:, i, b * AH + 2 * hp:b * AH + 2 * hp + 2],
                                   start=b == 0 and hp == 0 and i == 0, stop=False, skip_group_check=True)
                    x.then_inc(sem("values_mixed"), 1)
                own = sdiag[:].rearrange("r (b k) -> r b k", b=NB)
                for hp in range(HP):
                    x = mm(out[:, hp, :, :], vrep[:, hp * P:(hp + 1) * P], own[:, :, 2 * hp:2 * hp + 2],
                           start=False, stop=hp == HP - 1, skip_group_check=True)
                x.then_inc(sem("sample_mixed"), 1)

            def gate_logits(gp):
                if gp == 0:
                    pe.wait_ge(copied[T_GATE % 2], turns_before(T_GATE) + 1)
                    pe.wait_ge(sem("pt_copied"), AH * NT)
                    pe.wait_ge(sem("o_copied"), AH)
                else:
                    pe.wait_ge(sem("gate_folded"), gp)
                for j, cols in enumerate((slice(0, LO), slice(LO, T))):
                    x = mm(B[6 + j][:, 0:cols.stop - cols.start], wgate[:, gp * P:(gp + 1) * P], glow[:, cols],
                           start=True, stop=True)
                x.then_inc(sem("gate_logits"), 1)

            def gate_turn(gp):
                pe.wait_ge(sem("loga_ready"), gp + 1)
                pe.wait_ge(sem("gate_folded"), GP)
                for t in range(NT):
                    x = pe.transpose(B[6][:, t * P:(t + 1) * P], loga[:, gp, t * P:(t + 1) * P], ident[:])
                x.then_inc(sem("loga_turned"), 1)

            def gate_sums(gp):
                pe.wait_ge(sem("latok_ready"), gp + 1)
                if gp:
                    pe.wait_ge(sem("sums_copied"), gp)
                for t in range(NT):
                    x = mm(B[7][:, t * P:(t + 1) * P], latok[:, t, :], tri64[:], start=True, stop=True)
                x.then_inc(sem("gates_summed"), 1)

            def gla_tokens(gp):
                if gp == 0:
                    pe.wait_ge(sem("sample_out"), 2)
                else:
                    pe.wait_ge(sem("gla_std"), 2 * gp)
                pe.wait_ge(sem("k_end_ready"), gp + 1)
                for i in range(2):
                    n = T_GLA + 6 * gp + 2 + i
                    pe.wait_ge(copied[n % 2], turns_before(n) + 1)
                for t in range(NT):
                    pe.transpose(B[6][:, t * P:(t + 1) * P], flat(ee[:, gp])[:, t * P:(t + 1) * P], ident[:])
                    pe.transpose(B[7][:, t * P:(t + 1) * P], vg[:, 2 * gp, t * P:(t + 1) * P], ident[:])
                    pe.transpose(B[4][:, t * P:(t + 1) * P], vg[:, 2 * gp + 1, t * P:(t + 1) * P], ident[:])
                for i, src in enumerate((kg[:, gp], vg[:, 2 * gp], vg[:, 2 * gp + 1])):
                    x = pe.transpose(B[5][0:NB, i * P:(i + 1) * P], src[:, TP:T], ident[:])
                x.then_inc(sem("gla_turned"), 1)

            def gla_att(gp):
                pe.wait_ge(sem("gla_tokens_ready"), gp + 1)
                for e in range(2):
                    rows = slice(BK * e, BK * e + BK)
                    for t in range(NT):
                        x = mm(B[6 + e][:, t * P:(t + 1) * P], gt[rows, 1, t * P:(t + 1) * P],
                               gt[rows, 0, t * P:(t + 1) * P], start=True, stop=True)
                x.then_inc(sem("gla_att"), 1)
                for ch in range(NCH):
                    for e in range(2):
                        rows = slice(CH * (ch % 2), CH * (ch % 2) + CH)
                        x = mm(B[4 + ch % 2][BK * e:BK * e + BK, (ch // 2) * P:(ch // 2 + 1) * P],
                               ketok[rows, ch // 2, BK * e:BK * e + BK], gvtok[rows, e, ch // 2, :],
                               start=True, stop=True, skip_group_check=True)
                x.then_inc(sem("gla_added"), 1)

            def gla_out(gp):
                pe.wait_ge(sem("gla_masked"), gp + 1)
                pe.wait_ge(sem("gla_chained"), gp + 1)
                for e in range(2):
                    rows = slice(BK * e, BK * e + BK)
                    for t in range(NT):
                        mm(B[6 + e][:, t * P:(t + 1) * P], gvtok[:, e, t, :], att[:, e, t, :],
                           start=True, stop=False, skip_group_check=True)
                        for ch in (2 * t, 2 * t + 1):
                            if ch:
                                x = mm(B[6 + e][:, ch * CH:(ch + 1) * CH], gst[rows, ch, :],
                                       gt[rows, 0, ch * CH:(ch + 1) * CH], start=False, stop=ch % 2 == 1,
                                       skip_group_check=True)
                x.then_inc(sem("gla_out"), 1)
                for bh in range(2):
                    for e in range(2):
                        x = mm(B[4 + bh][BK * e:BK * e + BK, :], gsamp[:, 0, BK * e:BK * e + BK],
                               vdiag[:, e, 4 * bh:4 * bh + 4, :].rearrange("k b v -> k (b v)"), start=True, stop=True,
                               skip_group_check=True)
                x.then_inc(sem("gla_sample_kv"), 1)

            def gla_sample_out(gp):
                pe.wait_ge(sem("gla_stepped"), gp + 1)
                for e in range(2):
                    rows = slice(BK * e, BK * e + BK)
                    for b in range(NB):
                        x = mm(B[4 + e][:, b:b + 1], gs0[rows, b, :], qg[rows, gp, TP + b:TP + b + 1],
                               start=True, stop=True, skip_group_check=True)
                x.then_inc(sem("gla_sample_out"), 1)

            def gla_norm(gp):
                pe.wait_ge(sem("gla_squares"), 2 * gp + 2)
                for e in range(2):
                    for j, cols in enumerate((slice(0, LO), slice(LO, T))):
                        x = mm(B[4 + 2 * e + j][:, 0:cols.stop - cols.start], ones[:], gt[:, 2 + e, cols],
                               start=True, stop=True)
                x.then_inc(sem("gla_squares_summed"), 1)

            for _ in range(3):
                project()
            pe.wait_ge(consts_in, 16 * len(FIRST_CONSTS))
            for hp in range(HP):
                rotate(hp)
                project()
                to_tokens(hp)
                scores(hp, 0)
                project()
                mix_values(hp, 0)
                scores(hp, 1)
                project()
                mix_values(hp, 1)
            for b in range(NB):
                sample_q(b)
                if b == 1:
                    gate_logits(0)
                elif b == 3:
                    gate_logits(1)
                elif b == 4:
                    gate_turn(0)
                elif b == 5:
                    gate_sums(0)
                elif b == 7:
                    gate_sums(1)
                if b % 2:
                    project()
                if b == 5:
                    gate_turn(1)
            sample_rows()
            project()
            sample_cols()
            sample_mix()
            def out_half(j, part):
                n, w = (T_OUT0, T_OUT0B)[part] + j, U_OUT0 + j
                bank_free(n)
                unit(w, n, w % RING, w // RING + 1, mixT, blocks=range(part * HP, (part + 1) * HP), used=part == 1)

            gla_tokens(0)
            project()
            gla_att(0)
            project()
            gla_out(0)
            project()
            gla_sample_out(0)
            project()
            gla_norm(0)
            out_half(0, 0)
            out_half(1, 0)
            gla_tokens(1)
            out_half(2, 0)
            gla_att(1)
            out_half(3, 0)
            out_half(4, 0)
            gla_out(1)
            out_half(5, 0)
            gla_sample_out(1)
            out_half(6, 0)
            gla_norm(1)
            out_half(7, 0)
            pe.wait_ge(sem("gla_mixed"), BH)
            for j in range(DC):
                out_half(j, 1)

            def mlp(layer, r, t_norm, t_up, t_down, u_up, u_down, load_up):
                norm(r, t_norm)

                def up(i):
                    for s in range(RING):
                        bank_free(t_up + s, i * (RING // 2))
                        unit(i * RING + (u_up + s), t_up + s, s, i + (load_up[s] + 1), hn,
                             ready=normed(r) if isinstance(i, int) and s == 0 else None)

                up(0)
                with pe.Fori(1, FC // RING) as i:
                    up(i)
                with pe.Fori(0, DC // 2) as i:
                    for s in range(RING):
                        part = s % (FF // D)
                        n = t_down + s // (FF // D)
                        if part == 0:
                            bank_free(n, i)
                        pe.wait_ge(hidden, layer * FC + (part + 1) * DC)
                        unit(None, n, s, i + (load_up[s] + FC // RING + 1), hid, first=part * DC,
                             start=part == 0, last=part == FF // D - 1)

            mlp(0, 1, T_NORM1, T_UP0, T_DOWN0, U_UP0, U_DOWN0, [U_UP0 // RING] * RING)

            norm(2, T_NORM2)
            n = T_DT
            bank_free(n)
            for t in range(NT + 1):
                if t in (0, LO // P):
                    pe.wait_ge(*normed(2)(DC - 1, t > 0))
                cols = slice(t * P, (t + 1) * P) if t < NT else slice(TP, T)
                out = B[2 * (n % 2)][0:cols.stop - cols.start, t * CH_ALL:(t + 1) * CH_ALL]
                for k in range(DC):
                    x = mm(out, hn[:, k, cols], wdt[:, k, :], start=k == 0, stop=k == DC - 1)
            x.then_inc(sem("dt_summed"), 1)

            def ssd_project(g, j):
                n = T_SSD + j
                bank_free(n, g * (SSD_UNITS // 2))
                unit(None, n, j, g + (U_SSD // RING + 1), hn)

            def ssd_tokens(g, d):
                pe.wait_ge(sem("conv_ready"), g + 1)
                for i in range(2):
                    for t in range(NT):
                        pe.transpose(B[4 + t // 2][:, (t % 2) * GW + i * P:(t % 2) * GW + (i + 1) * P],
                                     conv[:, d, i, t * P:(t + 1) * P], ident[:])
                for t in range(NT):
                    pe.transpose(B[6][:, t * P:(t + 1) * P], conv[:, d, 2, t * P:(t + 1) * P], ident[:])
                for i in range(3):
                    pe.transpose(B[7][0:NB, 32 + i * P:32 + (i + 1) * P], conv[:, d, i, TP:T], ident[:])
                mm(B[7][:, 0:16], tri[:], flat(dag[:, d, 0:NT]), start=True, stop=True)
                mm(B[7][:, 16:32], ones[:], flat(dag[:, d, 0:NT]), start=True, stop=True)
                mm(B[7][:, 416:448], ones[0:NB], flat(sadg[:, d]), start=True, stop=True).then_inc(
                    sem("ssd_turned"), 1)

            def sample_outer(g, half):
                if half == 0:
                    pe.wait_ge(sem("xdt_ready"), g + 1)
                    pe.wait_ge(sem("sxdiag_ready"), g + 1)
                else:
                    pe.wait_ge(sem("ssm_stepped"), g * 2 + 1)
                for j in range(2):
                    b = 4 * half + 2 * j
                    x = mm(B[4 + j][:], ssamp[:, 2, :], sxdiag[:, b:b + 2, :].rearrange("k b c -> k (b c)"), start=True, stop=True)
                x.then_inc(sem("ssm_outer"), 1)

            def ssd_cb(g, d):
                pe.wait_ge(sem("btok_ready"), g + 1)
                for t in range(NT):
                    x = mm(B[6][:, t * P:(t + 1) * P], conv[:, d, 2, t * P:(t + 1) * P],
                           conv[:, d, 3, t * P:(t + 1) * P], start=True, stop=True)
                x.then_inc(sem("cb_ready"), 1)

            def ssd_spread(g, d, heads):
                for j in heads:
                    if j == 2:
                        pe.wait_ge(sem("cbm_ready"), g + 1)
                    if j == 3:
                        for read in ("small_read", "ssamp_read", "sadec_ready"):
                            pe.wait_ge(sem(read), g + 1)
                    if j == 0:
                        pe.wait_ge(sem("ssm_stepped"), g * 2 + 2)
                    for t in range(NT):
                        x = mm(B[4 + j][:, t * P:(t + 1) * P], dag[:, d, t, j:j + 1].to_broadcast((P, P)), tri[:],
                               start=True, stop=True)
                    x.then_inc(sem("decays_spread"), 1)

            def sample_y(g, d):
                pe.wait_ge(sem("decays_featured"), g * 4 + 1)
                pe.wait_ge(sem("ssm_stepped"), g * 2 + 2)
                for i in range(2):
                    for b in range(NB):
                        x = mm(B[6][:, i * NB + b:i * NB + b + 1], flat(ss0[:, b, 2 * i:2 * i + 2, :]),
                               conv[:, d, 3, TP + b:TP + b + 1], start=True, stop=True, skip_group_check=True)
                x.then_inc(sem("ssm_read"), 1)

            def ssd_intra(g):
                pe.wait_ge(sem("seg_ready"), g * 4 + 4)
                pe.wait_ge(sem("decays_featured"), g * 4 + 4)
                pe.wait_ge(sem("sample_y_read"), g + 1)
                for t in range(NT):
                    for j in range(CJ):
                        x = mm(B[6 + j // 2][CHD * (j % 2):CHD * (j % 2) + CHD, t * P:(t + 1) * P], xdt[:, t, j, :],
                               seg[:, j, t, :], start=True, stop=True, skip_group_check=True)
                x.then_inc(sem("y_intra"), 1)
                pe.wait_ge(sem("xde_ready"), g + 1)
                for t in range(NT):
                    x = mm(B[4 + t // 2][:, (t % 2) * GW:(t % 2 + 1) * GW], btok[:, t, :], xde[:, t].rearrange("p j q -> p (j q)"),
                           start=True, stop=True)
                x.then_inc(sem("ssd_added"), 1)

            def ssd_inter(g, d):
                pe.wait_ge(sem("states_kept"), g + 1)
                for t in range(1, NT):
                    for i in range(2):
                        x = mm(B[4 + i][:, t * P:(t + 1) * P], flat(st[:, t - 1, 2 * i:2 * i + 2]),
                               conv[:, d, 3, t * P:(t + 1) * P], start=True, stop=True)
                x.then_inc(sem("y_inter"), 1)

            def ssd_norm(g):
                pe.wait_ge(sem("ysq_ready"), g + 1)
                for j, cols in enumerate((slice(0, LO), slice(LO, T))):
                    x = mm(B[4 + j][:, 0:cols.stop - cols.start], ones[:], ysq[:, 0, cols], start=True, stop=True)
                x.then_inc(sem("ysq_summed"), 1)

            def ssd_mix(g, d, project):
                if not isinstance(g, int) or g > 0:
                    pe.wait_ge(sem("y_std"), g)
                    pe.wait_ge(sem("y_read"), g)
                ssd_tokens(g, d)
                project(0)
                sample_outer(g, 0)
                ssd_cb(g, d)
                project(1)
                sample_outer(g, 1)
                ssd_spread(g, d, (2, 3))
                project(2)
                ssd_spread(g, d, (0, 1))
                sample_y(g, d)
                project(3)
                ssd_intra(g)
                project(4)
                ssd_inter(g, d)
                project(5)
                ssd_norm(g)

            for j in range(SSD_UNITS):
                ssd_project(0, j)
            ssd_mix(0, 0, lambda j: ssd_project(1, j))
            with pe.Fori(0, (CG - 2) // 2) as i:
                ssd_mix(i * 2 + 1, 1, lambda j: ssd_project(i * 2 + 2, j))
                ssd_mix(i * 2 + 2, 0, lambda j: ssd_project(i * 2 + 3, j))

            def out_start(step):
                if step >= 4:
                    return
                j, part = step % 2, step // 2
                n, s = T_OUT1 + j, 2 * j + part
                if part == 0:
                    bank_free(n)
                else:
                    pe.wait_ge(sem("yout_ready"), CG - 1)
                pe.wait_ge(ring_in[s], 16 * (U_SSD // RING + CG + 1))
                for cols, bank in MATMULS:
                    for k in range(DC if part == 0 else DC - 2):
                        x = mm(bank(n), ring[:, s, k], yout[:, part * DC + k, cols], start=part == 0 and k == 0,
                               stop=False, skip_group_check=True)
                if step == 0:
                    x.then_inc(units_multiplied, 1)

            ssd_mix(CG - 1, 1, out_start)
            pe.wait_ge(sem("yout_ready"), CG)
            for j in range(2):
                for cols, bank in MATMULS:
                    for k in (DC - 2, DC - 1):
                        x = mm(bank(T_OUT1 + j), ring[:, 2 * j + 1, k], yout[:, DC + k, cols], start=False,
                               stop=k == DC - 1, skip_group_check=True)
                x.then_inc(units_multiplied, 2 - j)
            for j in range(2, DC):
                n = T_OUT1 + j
                bank_free(n)
                for part in range(CI // D):
                    w = U_OUT1 + 2 * j + part
                    s = (2 * j + part) % RING
                    load = U_SSD // RING + (CG if s < SSD_UNITS else 0)
                    unit(w, n, s, load + (2 * j + part) // RING + 1, yout, first=part * DC, start=part == 0,
                         last=part == 1)
            mlp(1, 3, T_NORM3, T_UP1, T_DOWN1, U_UP1, U_DOWN1,
                [U_SSD // RING + (CG if s < SSD_UNITS else 0) + (U_UP1 - U_OUT1) // RING for s in range(RING)])
            norm(4, T_NORM4)

        @block.scalar
        def _(act):
            run = nc.scalar.activation
            tally = Tally(act)
            step = sem("act_step")
            for name in NORM_CONSTS:
                act.dma_start(const_tiles[name][:], A["consts"][name]).then_inc(norm_consts_in, 16)
            for i in (1, 3):
                act.dma_start(h[:, 2 * i:2 * i + 2], A["xT"][:, 2 * i:2 * i + 2]).then_inc(x_in[i], 16)

            def norm(r, n, t_written):
                for k in range(DC):
                    if r == 0:
                        act.wait_ge(x_in[k // 2], 16)
                    else:
                        act.wait_ge(copied[(t_written + k) % 2], turns_before(t_written + k) + 1)
                    run(hn[:, k], h[:, k], ACT.Square).then_inc(squares, 1)
                if r == 0:
                    act.wait_ge(norm_consts_in, 16 * len(NORM_CONSTS))
                act.wait_ge(norm_summed, 2 * r + 1)
                run(std[:, 0:LO], lo(n), ACT.Sqrt, bias=eps[:, 0:1], scale=1.0 / D).then_inc(std_ready, 1)
                act.wait_ge(norm_summed, 2 * r + 2)
                run(std[:, LO:T], hi(n), ACT.Sqrt, bias=eps[:, 0:1], scale=1.0 / D).then_inc(copied[n % 2], 1)

            def copy_turn(n, dst, units=None, scale=1.0):
                if units is not None:
                    act.wait_ge(units_multiplied, units)
                run(dst[:, 0:LO], lo(n), ACT.Copy, scale=scale).then_inc(step, 1)
                run(dst[:, LO:T], hi(n), ACT.Copy, scale=scale).then_inc(copied[n % 2], 1)
                tally.total[id(step)] = tally.total.get(id(step), 0) + 1

            norm(0, T_NORM0, None)
            at = [0]

            def copy_next():
                w = at[0]
                if w >= U_OUT0:
                    return
                at[0] += 1
                if w < U_GLA:
                    n, hp, i = T_ATT + w, w // 3, w % 3
                    if hp:
                        if i < 2:
                            act.wait_ge(sem("rotated"), 2 * hp)
                            act.wait_ge(sem("rope_done"), 2 * hp)
                        else:
                            act.wait_ge(sem("v_turned"), hp)
                            act.wait_ge(sem("v_written"), 16 * hp)
                    copy_turn(n, (qraw, kraw, vraw)[i], w + 1, SCALE if i == 0 else 1.0)
                    return
                n, gp, i = T_GLA + w - U_GLA, (w - U_GLA) // 6, (w - U_GLA) % 6
                if w == U_GLA:
                    act.wait_ge(sem("glow_summed"), 1)
                    run(glow[:, 0:LO], lo(T_GATE)[0:RANK], ACT.Copy).then_inc(step, 1)
                    tally.total[id(step)] += 1
                    run(glow[:, LO:T], hi(T_GATE)[0:RANK], ACT.Copy).then_inc(copied[T_GATE % 2], 1)
                if i < 4:
                    copy_turn(n, (qg[:, gp], kg[:, gp], vg[:, 2 * gp], vg[:, 2 * gp + 1])[i], w + 1,
                              BK ** -0.5 if i == 0 else 1.0)
                else:
                    act.wait_ge(units_multiplied, w + 1)
                    run(rg[:, 2 * gp + i - 4, 0:LO], lo(n), ACT.Tanh, scale=0.5).then_inc(step, 1)
                    tally.total[id(step)] += 1
                    run(rg[:, 2 * gp + i - 4, LO:T], hi(n), ACT.Tanh, scale=0.5).then_inc(sem("r_tanh"), 1)

            def exps(hd):
                for j in range(NT):
                    act.wait_ge(sem("masked"), hd * NT + j + 1)
                    run(probs[:, j, 0:(j + 1) * P], probs[:, j, 0:(j + 1) * P], ACT.Exp, bias=pstat[:, 1, j:j + 1],
                        accum_out=pstat[:, 2, j:j + 1]).then_inc(sem("expd"), 1)

            def pt_copies(hd):
                for kt in range(NT):
                    act.wait_ge(sem("p_turned"), hd * NT + kt + 1)
                    if hd * NT + kt >= 2:
                        act.wait_ge(sem("pv_done"), hd * NT + kt - 1)
                    run(pt[:, kt % 2, 0:TP - kt * P], B[4 + kt % 3][:, 0:TP - kt * P], ACT.Copy).then_inc(
                        sem("pt_copied"), 1)

            for _ in range(3):
                copy_next()
            for hp in range(HP):
                copy_next()
                exps(2 * hp)
                copy_next()
                pt_copies(2 * hp)
                exps(2 * hp + 1)
                copy_next()
                pt_copies(2 * hp + 1)

            def gate_exp(gp):
                act.wait_ge(sem("gate_folded"), gp + 1)
                run(gt[:, 1, :], gt[:, 1, :], ACT.Exp).then_inc(sem("gate_expd"), 1)

            def gate_tokens(gp):
                act.wait_ge(sem("loga_turned"), gp + 1)
                run(flat(latok[:]), B[6][:], ACT.Copy).then_inc(sem("latok_ready"), 1)

            def gate_decays(gp):
                act.wait_ge(sem("sums_copied"), gp + 1)
                tally.done(run(flat(eb[:, gp]), flat(bT[:]), ACT.Exp), step)
                tally.done(run(flat(enb[:, gp]), flat(bT[:]), ACT.Exp, scale=-1.0), step)
                tally.done(run(sdec[:, gp], loga[:, gp, TP:T], ACT.Exp), step)
                act.wait_ge(sem("gate_left"), gp + 1)
                run(flat(ee[:, gp]), flat(ee[:, gp]), ACT.Exp).then_inc(sem("decays_ready"), 1)

            gate_exp(0)
            copy_next()
            gate_exp(1)
            copy_next()
            gate_tokens(0)
            copy_next()
            gate_decays(0)
            gate_tokens(1)
            copy_next()
            gate_decays(1)
            copy_next()
            act.wait_ge(sem("sample_max"), 1)
            tally.done(run(flat(sexp[:]), B[6][0:NB * AH, 0:NBR * P], ACT.Exp, bias=sst[:, 2:3],
                           accum_out=sst[:, 3:4]), step)
            run(sst[:, 4:5], sst[:, 1:2], ACT.Exp, bias=sst[:, 2:3]).then_inc(sem("sample_expd"), 1)

            def gla(gp):
                act.wait_ge(sem("gla_turned"), gp + 1)
                tally.done(run(flat(ketok), B[6][:], ACT.Copy), step)
                run(flat(gvtok[:, 0]), B[7][:], ACT.Copy).then_inc(sem("gla_tok_act"), 1)
                copy_next()
                copy_next()
                act.wait_ge(sem("gla_sample_kv"), gp + 1)
                for e in range(2):
                    run(gt[:, 4 + e, 0:TP], B[6 + e][:], ACT.Copy).then_inc(sem("gla_o_copied"), 1)
                copy_next()
                act.wait_ge(sem("gla_sample_out"), gp + 1)
                for e in range(2):
                    tally.done(run(gt[:, 4 + e, TP:T], B[4 + e][:, 0:NB], ACT.Copy), step)
                act.wait_ge(sem("gla_o_copied"), 2 * gp + 2)
                for e in range(2):
                    run(gt[:, 2 + e, :], gt[:, 4 + e, :], ACT.Square).then_inc(sem("gla_squares"), 1)
                copy_next()
                act.wait_ge(sem("gla_squares_summed"), gp + 1)
                for e in range(2):
                    tally.done(run(gt[:, 2 + e, 0:LO], B[4 + 2 * e][:, 0:LO], ACT.Sqrt, bias=eps[:, 0:1],
                                   scale=1.0 / BV), step)
                    run(gt[:, 2 + e, LO:T], B[5 + 2 * e][:, 0:HI], ACT.Sqrt, bias=eps[:, 0:1],
                        scale=1.0 / BV).then_inc(sem("gla_std"), 1)

            for gp in range(GP):
                gla(gp)

            def mlp_up(t_up, u_up, p=0):
                with act.Fori(0, FC // RING) as i:
                    for s in range(RING):
                        act.wait_ge(units_multiplied, i * RING + (u_up + s + 1))
                        run(hid[:, i * RING + s, 0:LO], lo(t_up + s), ACT.Relu).then_inc(sem("relu_low"), 1)
                        run(hid[:, i * RING + s, LO:T], hi(t_up + s), ACT.Relu).then_inc(
                            copied[(t_up + s) % 2], 1)

            norm(1, T_NORM1, T_OUT0B)
            act.wait_ge(sem("gla_prompt_out"), 16 * GP)
            act.wait_ge(sem("gla_state_out"), 16 * GP)
            act.wait_ge(sem("samp_written"), 32)
            mlp_up(T_UP0, U_UP0)

            norm(2, T_NORM2, T_DOWN0)
            act.wait_ge(sem("dt_folded"), 1)
            tally.done(run(nega[:], nega[:], ACT.Exp), step)
            run(flat(dts[:, 2]), flat(dts[:, 1]), ACT.Exp).then_inc(sem("dt_expd"), 1)

            ct = Tally(act)
            cstep, mstep = sem("act_conv_step"), sem("act_ssd_step")

            def conv_in(g, j):
                n = T_SSD + j
                act.wait_ge(units_multiplied, g * SSD_UNITS + (U_SSD + j + 1))
                if not (isinstance(g, int) and g == 0):
                    act.wait_ge(sem("conv_ready"), g)
                else:
                    act.wait_ge(sem("pads_ready"), 1)
                run(xe[:, j, 3:3 + LO], lo(n), ACT.Copy).then_inc(cstep, 1)
                run(xe[:, j, 3 + LO:3 + TP], hi(n)[:, 0:LO], ACT.Copy).then_inc(cstep, 1)
                run(xs[:, j, 3, :], hi(n)[:, LO:HI], ACT.Copy).then_inc(copied[n % 2], 1)

            def conv_tanh(g, d, j):
                act.wait_ge(sem("taps_done"), g * 4 + (j + 1))
                if not (isinstance(g, int) and g == 0 and j < 2):
                    act.wait_ge(sem("tanh_used"), g * 4 + (j - 1))
                run(th[:, j % 2, 0:TP], conv[:, d, j, 0:TP], ACT.Tanh).then_inc(sem("conv_tanh"), 1)

            def conv_tanh_samples(g, d):
                act.wait_ge(sem("sample_taps_done"), g + 1)
                run(ths[:], conv[:, d, :, TP:T], ACT.Tanh).then_inc(sem("sample_conv_tanh"), 1)

            def gate(g, d, i):
                n = T_SSD + 4 + i
                act.wait_ge(units_multiplied, g * SSD_UNITS + (U_SSD + 4 + i + 1))
                run(gz[:, d, i, 0:LO], lo(n), ACT.Tanh, scale=0.5).then_inc(cstep, 1)
                run(gz[:, d, i, LO:T], hi(n), ACT.Tanh, scale=0.5).then_inc(sem("z_tanh"), 1)

            def mix(g, d, nxt):
                act.wait_ge(sem("ssd_turned"), g + 1)
                if not (isinstance(g, int) and g == 0):
                    act.wait_ge(sem("ssm_decayed"), g * 2)
                    act.wait_ge(sem("states_kept"), g)
                    act.wait_ge(sem("y_scaled"), g)
                act.wait_ge(sem("ssamp_read"), g + 1)
                run(flat(sadec[:]), B[7][:, 416:448], ACT.Exp).then_inc(sem("sadec_ready"), 1)
                run(flat(btok[:]), B[6][:], ACT.Copy).then_inc(sem("btok_ready"), 1)
                act.wait_ge(sem("cum_left"), g + 1)
                run(flat(dec[:]), flat(cum[:, 1]), ACT.Exp).then_inc(mstep, 1)
                run(flat(toend[:]), flat(toend[:]), ACT.Exp).then_inc(sem("decay_exps"), 1)
                if nxt is not None:
                    conv_in(nxt, 0)
                    conv_tanh(nxt, 1 - d, 0)
                    conv_in(nxt, 1)
                    conv_tanh(nxt, 1 - d, 1)
                for i, j in enumerate((2, 3, 0, 1)):
                    act.wait_ge(sem("decays_read"), g * 4 + (i + 1))
                    rows = slice(CHD * (j % 2), CHD * (j % 2) + CHD)
                    run(efeat[rows, j // 2, :], B[4 + j][rows, P:TP], ACT.Exp).then_inc(sem("decays_featured"), 1)
                    run(flat(seg[:, j]), flat(seg[:, j]), ACT.Exp).then_inc(sem("seg_expd"), 1)
                    if i == 1 and nxt is not None:
                        conv_in(nxt, 2)
                        conv_tanh(nxt, 1 - d, 2)
                if nxt is not None:
                    conv_in(nxt, 3)
                    conv_tanh(nxt, 1 - d, 3)
                    conv_tanh_samples(nxt, 1 - d)
                    gate(nxt, 1 - d, 0)
                act.wait_ge(sem("y_gated"), g + 1)
                run(ysq[:, 0], yT[:, 0], ACT.Square).then_inc(mstep, 1)
                run(ysq[:, 1], yT[:, 1], ACT.Square).then_inc(sem("y_squared"), 1)
                if nxt is not None:
                    gate(nxt, 1 - d, 1)
                act.wait_ge(sem("ysq_summed"), g + 1)
                run(ystd[:, 0:LO], B[4][:, 0:LO], ACT.Sqrt, bias=eps[:, 0:1], scale=1.0 / GW).then_inc(mstep, 1)
                run(ystd[:, LO:T], B[5][:, 0:HI], ACT.Sqrt, bias=eps[:, 0:1], scale=1.0 / GW).then_inc(
                    sem("y_std"), 1)

            conv_in(0, 0)
            for j in range(4):
                if j:
                    conv_in(0, j)
                conv_tanh(0, 0, j)
            conv_tanh_samples(0, 0)
            gate(0, 0, 0)
            gate(0, 0, 1)
            mix(0, 0, 1)
            with act.Fori(0, (CG - 2) // 2) as i:
                mix(i * 2 + 1, 1, i * 2 + 2)
                mix(i * 2 + 2, 0, i * 2 + 3)
            mix(CG - 1, 1, None)
            norm(3, T_NORM3, T_OUT1)
            act.wait_ge(sem("layer1_out"), 32)
            act.wait_ge(sem("pssm_out"), 16 * CG)
            act.wait_ge(sem("ssm_out"), 16 * CG)
            mlp_up(T_UP1, U_UP1)
            norm(4, T_NORM4, T_DOWN1)

        @block.vector
        def _(dve):
            V = nc.vector
            tally = Tally(dve)
            step = sem("vec_step")
            do = lambda ins, name=None: tally.done(ins, step if name is None else sem(name))

            def add_square(r, k):
                dve.wait_ge(squares, k + (r * DC + 1))
                if not (r == 0 and isinstance(k, int) and k == 0):
                    dve.wait_ge(squares_added, k + r * DC)
                V.tensor_tensor(rstd[:], rstd[:], hn[:, k], ALU.add).then_inc(squares_added, 1)

            def norm(r, n):
                if r == 0:
                    dve.wait_ge(norm_consts_in, 16 * len(NORM_CONSTS))
                    for i in range(DC // 2):
                        dve.wait_ge(x_in[i], 16)
                for cols, _ in MATMULS:
                    if cols.start == 0:
                        dve.wait_ge(std_ready, r + 1)
                    else:
                        dve.wait_ge(copied[n % 2], turns_before(n) + 1)
                    do(V.reciprocal(rstd[:, cols], std[:, cols]))
                    for k in range(DC):
                        V.scalar_tensor_tensor(hn[:, k, cols], h[:, k, cols], norms[:, r, k:k + 1], rstd[:, cols],
                                               ALU.mult, ALU.mult).then_inc(hn_ready, 1)

            def log1p_tail(e, s, s2, p, den):
                do(V.tensor_scalar(den, e, 2.0, None, ALU.add))
                do(V.reciprocal(den, den))
                do(V.tensor_tensor(s, e, den, ALU.mult))
                do(V.tensor_tensor(s2, s, s, ALU.mult))
                do(V.tensor_scalar(p, s2, LOG1P[0], None, ALU.mult))
                for coefficient in LOG1P[1:]:
                    do(V.scalar_tensor_tensor(p, p, coefficient, s2, ALU.add, ALU.mult))
                do(V.scalar_tensor_tensor(p, p, 1.0, s, ALU.add, ALU.mult))

            do(V.memset(rstd[:], 0.0))
            for k in range(DC):
                add_square(0, k)
            norm(0, T_NORM0)
            at = [3]

            def next_gate():
                w = at[0]
                if w >= U_OUT0:
                    return
                at[0] += 1
                i = (w - U_GLA) % 6
                if w < U_GLA or i < 4:
                    return
                n, tile = T_GLA + w - U_GLA, (w - U_GLA) // 6 * 2 + i - 4
                dve.wait_ge(sem("r_tanh"), tile + 1)
                V.scalar_tensor_tensor(rg[:, tile, 0:LO], rg[:, tile, 0:LO], 1.0, lo(n), ALU.add,
                                       ALU.mult).then_inc(sem("r_gated"), 1)
                V.scalar_tensor_tensor(rg[:, tile, LO:T], rg[:, tile, LO:T], 1.0, hi(n), ALU.add,
                                       ALU.mult).then_inc(copied[n % 2], 1)

            def rope(hp):
                if hp:
                    dve.wait_ge(sem("k_written"), 16 * hp)
                for i, (raw, out) in enumerate(((qraw, qr), (kraw, kr))):
                    dve.wait_ge(sem("rotated"), 2 * hp + i + 1)
                    V.tensor_tensor(rt[:, 0, 0:LO], B[4 + 2 * i][:, 0:LO], sin[:, 0:LO], ALU.mult).then_inc(
                        sem("rope_part"), 1)
                    V.tensor_tensor(rt[:, 0, LO:T], B[5 + 2 * i][:, 0:HI], sin[:, LO:T], ALU.mult).then_inc(
                        sem("rope_part"), 1)
                    do(V.tensor_tensor(rt[:, 1], raw[:], cos[:], ALU.mult))
                    do(V.tensor_tensor(out[:], rt[:, 0], rt[:, 1], ALU.add), "rope_done")

            def tokens(hp):
                dve.wait_ge(sem("v_turned"), hp + 1)
                if hp:
                    dve.wait_ge(sem("pv_done"), 2 * hp * NT)
                do(V.tensor_copy(flat(vtok[:]), B[4][:]))
                do(V.tensor_copy(samp[:, :, hp * P:(hp + 1) * P],
                                 B[5][0:NB, 0:3 * P].rearrange("b (i d) -> b i d", i=3)), "samp_ready")

            def mask(hd):
                if hd:
                    dve.wait_ge(sem("p_turned"), hd * NT)
                for j in range(NT):
                    w = (j + 1) * P
                    dve.wait_ge(sem("scored"), hd * NT + j + 1)
                    do(V.tensor_tensor_reduce(probs[:, j, 0:w], B[4 + j][:, 0:w], lncount[:, TP - w:TP], 1.0,
                                              LEAST, ALU.add, ALU.max, pstat[:, 0, j:j + 1]))
                    do(V.tensor_scalar(pstat[:, 1, j:j + 1], pstat[:, 0, j:j + 1], -1.0, None, ALU.mult), "masked")

            def normalise(hd):
                for j in range(NT):
                    dve.wait_ge(sem("expd"), hd * NT + j + 1)
                    do(V.reciprocal(pstat[:, 3, j:j + 1], pstat[:, 2, j:j + 1]))
                    do(V.tensor_scalar(probs[:, j, 0:(j + 1) * P], probs[:, j, 0:(j + 1) * P],
                                       pstat[:, 3, j:j + 1], None, ALU.mult), "p_ready")

            def take_out(hp, e):
                dve.wait_ge(sem("pv_done"), (2 * hp + e + 1) * NT)
                rows = slice(AD * e, AD * e + AD)
                do(V.tensor_copy(mixT[rows, hp, 0:TP], B[7][rows, :]), "o_copied")

            dve.wait_ge(consts_in, 16 * len(FIRST_CONSTS))
            for hp in range(HP):
                rope(hp)
                next_gate()
                tokens(hp)
                mask(2 * hp)
                normalise(2 * hp)
                next_gate()
                take_out(hp, 0)
                mask(2 * hp + 1)
                normalise(2 * hp + 1)
                next_gate()
                take_out(hp, 1)

            def fold_gate(gp):
                dve.wait_ge(sem("gate_logits"), gp + 1)
                x, e = gt[:, 0], gt[:, 1]
                do(V.tensor_scalar(x[:, 0:LO], B[6][:, 0:LO], bgate[:, gp:gp + 1], None, ALU.add))
                do(V.tensor_scalar(x[:, LO:T], B[7][:, 0:HI], bgate[:, gp:gp + 1], None, ALU.add))
                do(V.scalar_tensor_tensor(e, x, -1.0, x, ALU.mult, ALU.min), "gate_folded")

            def log_gate(gp):
                x, e, s, s2, p, t = (gt[:, i] for i in range(6))
                dve.wait_ge(sem("gate_expd"), gp + 1)
                log1p_tail(e, s, s2, p, t)
                do(V.tensor_scalar(x, x, 0.0, 1.0 / TAU, ALU.min, ALU.mult))
                do(V.scalar_tensor_tensor(loga[:, gp], p, -2.0 / TAU, x, ALU.mult, ALU.add), "loga_ready")

            def gate_decays(gp):
                dve.wait_ge(sem("gates_summed"), gp + 1)
                if gp:
                    dve.wait_ge(sem("decays_ready"), gp)
                do(V.tensor_copy(flat(bT[:]), B[7][:]), "sums_copied")
                do(V.tensor_tensor(ee[:, gp], bT[:, :, CH - 1:CH].to_broadcast((P, NCH, CH)), bT[:], ALU.subtract),
                   "gate_left")

            dve.wait_ge(late_consts_in, 16 * len(LATE_CONSTS))
            for b in range(NB):
                dve.wait_ge(sem("sample_q_spread"), b + 1)
                dve.wait_ge(sem(f"gathered{b % SLOTS}"), 16 * NBR * (b // SLOTS + 1))
                do(V.tensor_tensor(gprod[:], gath[:, b % SLOTS], B[4 + b % 2][:].unsqueeze(1).to_broadcast((P, NBR, AW)),
                                   ALU.mult))
                do(V.tensor_reduce(s3[:, :, b * AH:(b + 1) * AH],
                                   gprod[:].rearrange("p i (k d) -> p i k d", k=AH), AX, ALU.add), "keys_scored")
                if b == 1:
                    dve.wait_ge(sem("v_written"), 16 * HP)
                    dve.wait_ge(sem("k_written"), 16 * HP)
                    do(V.memset(att[:], 0.0))
                    fold_gate(0)
                elif b == 2:
                    log_gate(0)
                    next_gate()
                elif b == 3:
                    fold_gate(1)
                elif b == 4:
                    log_gate(1)
                    next_gate()
                elif b == 5:
                    gate_decays(0)
                elif b == 6:
                    next_gate()
                    gate_decays(1)
                elif b == 7:
                    next_gate()
            dve.wait_ge(sem("sample_rows_ready"), 1)
            do(V.tensor_tensor(krep, B[5][0:NB * AH, :], ownhead[:], ALU.mult))
            do(V.tensor_copy(vrep, B[7][0:NB * AH, :]))
            do(V.tensor_tensor_reduce(kscr, B[4][0:NB * AH, :], krep, 1.0, 0.0, ALU.mult, ALU.add,
                                      sst[:, 1:2]))
            do(V.tensor_reduce(sst[:, 0:1], B[6][0:NB * AH, 0:NBR * P], AX, ALU.max))
            do(V.tensor_tensor(sst[:, 0:1], sst[:, 0:1], sst[:, 1:2], ALU.max))
            do(V.tensor_scalar(sst[:, 2:3], sst[:, 0:1], -1.0, None, ALU.mult), "sample_max")
            next_gate()
            dve.wait_ge(sem("sample_expd"), 1)
            do(V.scalar_tensor_tensor(sst[:, 5:6], sst[:, 4:5], float(NBR), sst[:, 3:4], ALU.mult, ALU.add))
            do(V.reciprocal(sst[:, 6:7], sst[:, 5:6]))
            do(V.scalar_tensor_tensor(sst[:, 7:8], sst[:, 4:5], float(NBR), sst[:, 6:7], ALU.mult, ALU.mult))
            do(V.tensor_scalar(sdiag[:], ident[0:NB * AH, 0:NB * AH], sst[:, 7:8], None, ALU.mult))
            do(V.tensor_scalar(flat(sexp[:]), flat(sexp[:]), sst[:, 6:7], None, ALU.mult), "sample_probs")
            dve.wait_ge(sem("sample_probs_turned"), 1)
            do(V.tensor_copy(flat(spt[:]), B[4][:, 0:NBR * NB * AH]), "spt_copied")
            dve.wait_ge(sem("sample_mixed"), 1)
            mixed = B[5][:, 0:HP * NB * 2].rearrange("p (a b e) -> p a b e", a=HP, b=NB)
            for e in range(2):
                rows = slice(AD * e, AD * e + AD)
                do(V.tensor_copy(mixT[rows, 0:HP, TP:T], mixed[rows, :, :, e]), "sample_out")

            def scaled(gp):
                for i in range(2):
                    n = T_GLA + 6 * gp + i
                    dve.wait_ge(copied[n % 2], turns_before(n) + 1)
                if gp:
                    dve.wait_ge(sem("gla_out"), gp)
                dve.wait_ge(sem("decays_ready"), gp + 1)
                do(V.tensor_tensor(gt[:, 0, 0:TP], qg[:, gp, 0:TP], flat(eb[:, gp]), ALU.mult))
                do(V.tensor_tensor(gt[:, 1, 0:TP], kg[:, gp, 0:TP], flat(enb[:, gp]), ALU.mult))
                do(V.tensor_tensor(flat(ee[:, gp]), kg[:, gp, 0:TP], flat(ee[:, gp]), ALU.mult), "k_end_ready")

            def gla(gp, after_tokens, after_chain, after_step, between_norms):
                if gp:
                    dve.wait_ge(sem("gla_prompt_out"), 16 * gp)
                dve.wait_ge(sem("gla_turned"), gp + 1)
                do(V.tensor_copy(flat(gvtok[:, 1]), B[4][:]))
                do(V.tensor_copy(flat(gsamp[:]), B[5][0:NB, 0:3 * P]))
                dve.wait_ge(sem("gla_tok_act"), gp + 1)
                for e2 in range(2):
                    do(V.tensor_tensor(vdiag[:, e2], gsamp[:, 1 + e2].unsqueeze(1).to_broadcast((NB, NB, P)),
                                       delta[:].unsqueeze(2).to_broadcast((NB, NB, P)), ALU.mult),
                       "gla_tokens_ready" if e2 else None)
                after_tokens()
                dve.wait_ge(sem("gla_att"), gp + 1)
                for e2 in range(2):
                    do(V.copy_predicated(att[:, e2], mask64[:].unsqueeze(1).to_broadcast((P, NT, P)), B[6 + e2][:].rearrange("p (t q) -> p t q", t=NT)),
                       "gla_masked" if e2 else None)
                dve.wait_ge(sem("gla_added"), gp + 1)
                for ch in range(NCH):
                    add = B[4 + ch % 2][:, (ch // 2) * P:(ch // 2 + 1) * P]
                    last = "gla_chained" if ch == NCH - 1 else None
                    if ch == 0:
                        do(V.tensor_copy(gst[:, 1], add))
                    else:
                        do(V.scalar_tensor_tensor(gst[:, ch + 1], gst[:, ch], eb[:, gp, ch, CH - 1:CH], add,
                                                  ALU.mult, ALU.add), last)
                after_chain()
                dve.wait_ge(sem("gla_sample_kv"), gp + 1)
                dve.wait_ge(sem("gla_state_in"), 16 * (gp + 1))
                for b in range(NB):
                    do(V.scalar_tensor_tensor(gs0[:, b], gs0[:, b], sdec[:, gp, b:b + 1],
                                              B[4 + b // 4][:, (b % 4) * P:(b % 4 + 1) * P], ALU.mult, ALU.add),
                       "gla_stepped" if b == NB - 1 else None)
                after_step()
                for e2 in range(2):
                    hd = 2 * gp + e2
                    dve.wait_ge(sem("gla_std"), hd + 1)
                    do(V.reciprocal(gt[:, 2 + e2], gt[:, 2 + e2]))
                    do(V.scalar_tensor_tensor(gt[:, 4 + e2], gt[:, 4 + e2], wonorm[:, 0:1], gt[:, 2 + e2],
                                              ALU.mult, ALU.mult))
                    if e2 == 0:
                        between_norms()
                    n = T_GLA + 6 * gp + 4 + e2
                    dve.wait_ge(copied[n % 2], turns_before(n) + 1)
                    do(V.scalar_tensor_tensor(mixT[:, HP + hd], gt[:, 4 + e2], 0.5, rg[:, hd], ALU.mult,
                                              ALU.mult), "gla_mixed")

            def residual(n, block_of_h, units, done=units_multiplied):
                dve.wait_ge(done, units)
                V.tensor_tensor(h[:, block_of_h, 0:LO], h[:, block_of_h, 0:LO], lo(n), ALU.add).then_inc(
                    sem("h_low"), 1)
                V.tensor_tensor(h[:, block_of_h, LO:T], h[:, block_of_h, LO:T], hi(n), ALU.add).then_inc(
                    copied[n % 2], 1)

            def mlp(r, t_norm, t_up, t_down, u_down, up_turns):
                norm(r, t_norm)
                with dve.Fori(0, FC // RING) as i:
                    for s in range(RING):
                        dve.wait_ge(copied[(t_up + s) % 2], i * (RING // 2) + (turns_before(t_up + s) + 1))
                        V.tensor_tensor(hid[:, i * RING + s], hid[:, i * RING + s], hid[:, i * RING + s],
                                        ALU.mult).then_inc(hidden, 1)
                do(V.memset(rstd[:], 0.0))
                with dve.Fori(0, DC // 2) as i:
                    for s in range(2):
                        residual(t_down + s, i * 2 + s, i * RING + (u_down + (s + 1) * (FF // D)))
                        add_square(r + 1, i * 2 + s)

            def halves(*blocks):
                for j in blocks:
                    residual(T_OUT0 + j, j, j + 1, sem("parts_multiplied"))

            scaled(0)

            def step0():
                next_gate()
                scaled(1)
                next_gate()

            gla(0, next_gate, next_gate, step0, lambda: halves(0, 1))
            gla(1, lambda: halves(2), lambda: halves(3, 4), lambda: halves(5, 6), lambda: halves(7))
            do(V.memset(rstd[:], 0.0))
            for j in range(DC):
                residual(T_OUT0B + j, j, U_OUT0 + j + 1)
                add_square(1, j)
            mlp(1, T_NORM1, T_UP0, T_DOWN0, U_DOWN0, FC)

            norm(2, T_NORM2)
            dve.wait_ge(sem("dt_summed"), 1)
            bank = B[2 * (T_DT % 2)]
            do(V.memset(dts[:, 0], 0.0))
            do(V.memset(xe[:, :, 0:TAPS - 1], 0.0), "pads_ready")
            do(V.tensor_tensor(dts[:, 0, 0:NT], bank[:, 0:NT * CH_ALL].rearrange("p (t k) -> p t k", t=NT),
                               dtb[:].unsqueeze(1).to_broadcast((P, NT, CH_ALL)), ALU.add))
            ins = V.tensor_tensor(dts[0:NB, 0, NT], bank[0:NB, NT * CH_ALL:(NT + 1) * CH_ALL], dtb[0:NB], ALU.add)
            ins.then_inc(copied[T_DT % 2], 1)
            dve.wait_ge(copied[T_DT % 2], turns_before(T_DT) + 1)
            f = lambda i: flat(dts[:, i])
            do(V.scalar_tensor_tensor(f(1), f(0), -1.0, f(0), ALU.mult, ALU.min), "dt_folded")
            dve.wait_ge(sem("dt_expd"), 1)
            log1p_tail(f(2), f(5), f(6), f(7), f(3))
            do(V.tensor_scalar(f(0), f(0), 0.0, None, ALU.max))
            do(V.scalar_tensor_tensor(f(0), f(7), 2.0, f(0), ALU.mult, ALU.add))
            do(V.scalar_tensor_tensor(dts[:, 1], dts[:, 0], -1.0,
                                      nega[:].unsqueeze(1).to_broadcast((P, NT + 1, CH_ALL)), ALU.mult, ALU.mult))

            steps_of = dts[:].rearrange("p i t (g j) -> p i t g j", g=CG)
            conv_tally, mix_tally = Tally(dve), Tally(dve)
            cstep, mstep = sem("vec_conv_step"), sem("vec_ssd_step")

            def cdo(ins, name=None):
                conv_tally.done(ins, cstep if name is None else sem(name))

            def mdo(ins, name=None):
                mix_tally.done(ins, mstep if name is None else sem(name))

            def prepare(g, d):
                conv_tally.start("conv", g)
                cdo(V.tensor_scalar(pg[:, d, 0:20], parm[:, g, 0:20], 0.5, None, ALU.mult))
                cdo(V.tensor_copy(pg[:, d, 20:24], parm[:, g, 20:24]))
                cdo(V.tensor_copy(xs[:, :, 0:3, :], parm[:, g, 24:120].rearrange("p (c t b) -> p c t b", c=4, t=3)))
                cdo(V.tensor_copy(dtg[:, d], steps_of[:, 0, :, g]))
                cdo(V.tensor_copy(dag[:, d], steps_of[:, 1, :, g]))
                cdo(V.tensor_tensor(sadg[:, d], dag[0:NB, d, NT].unsqueeze(1).to_broadcast((NB, NB, CJ)),
                                    deltac[:].unsqueeze(2).to_broadcast((NB, NB, CJ)), ALU.mult))

            def taps(g, d, j):
                n = T_SSD + j
                dve.wait_ge(copied[n % 2], g * (SSD_UNITS // 2) + (turns_before(n) + 1))
                out = conv[:, d, j, 0:TP]
                cdo(V.tensor_scalar(out, xe[:, j, 0:TP], pg[:, d, 4 * j:4 * j + 1], pg[:, d, 16 + j:17 + j],
                                    ALU.mult, ALU.add))
                for tap in range(1, TAPS):
                    cdo(V.scalar_tensor_tensor(out, xe[:, j, tap:tap + TP], pg[:, d, 4 * j + tap:4 * j + tap + 1],
                                               out, ALU.mult, ALU.add), "taps_done" if tap == TAPS - 1 else None)

            def finish(g, d, j):
                dve.wait_ge(sem("conv_tanh"), g * 4 + (j + 1))
                cdo(V.scalar_tensor_tensor(conv[:, d, j, 0:TP], th[:, j % 2, 0:TP], 1.0, conv[:, d, j, 0:TP],
                                           ALU.add, ALU.mult), "tanh_used")

            def sample_taps(g, d):
                w = pg[:, d, 0:16].rearrange("p (c t) -> p c t", c=4).unsqueeze(3).to_broadcast((P, 4, TAPS, NB))
                cdo(V.tensor_tensor(xsp[:], xs[:], w, ALU.mult))
                cdo(V.tensor_reduce(conv[:, d, :, TP:T], xsp[:].rearrange("p c t b -> p c b t"), AX, ALU.add))
                cdo(V.tensor_tensor(conv[:, d, :, TP:T], conv[:, d, :, TP:T],
                                    pg[:, d, 16:20].unsqueeze(2).to_broadcast((P, 4, NB)), ALU.add),
                    "sample_taps_done")
                cdo(V.tensor_copy(pconv[:, g], xe[:, :, TP:TP + 3]), "conv_kept")
                cdo(V.tensor_copy(sconv[:, g], xs[:, :, 1:4, :]), "conv_kept")

            def finish_samples(g, d):
                dve.wait_ge(sem("sample_conv_tanh"), g + 1)
                cdo(V.scalar_tensor_tensor(conv[:, d, :, TP:T], ths[:], 1.0, conv[:, d, :, TP:T], ALU.add,
                                           ALU.mult), "conv_ready")
                conv_tally.end()

            def gate(g, d, i):
                n = T_SSD + 4 + i
                dve.wait_ge(sem("z_tanh"), g * 2 + (i + 1))
                V.scalar_tensor_tensor(gz[:, d, i, 0:LO], gz[:, d, i, 0:LO], 1.0, lo(n), ALU.add,
                                       ALU.mult).then_inc(sem("z_low"), 1)
                V.scalar_tensor_tensor(gz[:, d, i, LO:T], gz[:, d, i, LO:T], 1.0, hi(n), ALU.add,
                                       ALU.mult).then_inc(copied[n % 2], 1)

            def normed(g, d):
                dve.wait_ge(sem("y_std"), g + 1)
                norm_tally.start("normed", g)
                norm_tally.done(V.reciprocal(yrstd[:], ystd[:]), nstep)
                for i in range(2):
                    norm_tally.done(V.scalar_tensor_tensor(yout[:, g * 2 + i], yT[:, i], pg[:, d, 22 + i:23 + i],
                                                           yrstd[:], ALU.mult, ALU.mult),
                                    sem("yout_ready") if i else nstep)
                norm_tally.end()

            norm_tally, nstep = Tally(dve), sem("vec_norm_step")
            norm_tally.per["normed"] = {id(nstep): 2, id(sem("yout_ready")): 1}

            def pair(i):
                return B[i][:].rearrange("p (t j q) -> p t j q", t=2, j=CJ)

            def mix(g, d, nxt, prev):
                mix_tally.start("mix", g)
                dve.wait_ge(sem("ssd_turned"), g + 1)
                if prev is not None:
                    dve.wait_ge(sem("ssd_added"), g)
                    dve.wait_ge(sem("ssm_outer"), g * 2)
                mdo(V.tensor_copy(flat(cum[:]), B[7][:, 0:32]), "small_read")
                mdo(V.tensor_copy(flat(ssamp[:]), B[7][0:NB, 32:416]), "ssamp_read")
                mdo(V.tensor_tensor(toend[:], cum[:, 1], cum[:, 0], ALU.subtract), "cum_left")
                for i in range(2):
                    mdo(V.tensor_tensor(xdt[:, 2 * i:2 * i + 2], pair(4 + i),
                                        dtg[:, d, 2 * i:2 * i + 2].unsqueeze(3).to_broadcast((P, 2, CJ, CHD)),
                                        ALU.mult), "xdt_ready" if i else None)
                mdo(V.tensor_tensor(sxdt[:], ssamp[:, 0:2].rearrange("b i (j q) -> b (i j) q", j=2),
                                    dtg[0:NB, d, NT].unsqueeze(2).to_broadcast((NB, CJ, CHD)), ALU.mult))
                mdo(V.tensor_tensor(sxdiag, flat(sxdt[:]).unsqueeze(1).to_broadcast((NB, NB, GW)),
                                    deltac[:].unsqueeze(2).to_broadcast((NB, NB, GW)), ALU.mult), "sxdiag_ready")
                if prev is not None:
                    normed(prev, 1 - d)
                for i in range(2):
                    mdo(V.tensor_scalar(yT[:, i], conv[:, d, i], pg[:, d, 20 + i:21 + i], None, ALU.mult))
                if nxt is not None:
                    prepare(nxt, 1 - d)
                    taps(nxt, 1 - d, 0)
                dve.wait_ge(sem("decay_exps"), g + 1)
                mdo(V.tensor_tensor(xde, xdt[:], toend[:].unsqueeze(3).to_broadcast((P, NT, CJ, CHD)),
                                    ALU.mult), "xde_ready")

                def step_states(half):
                    dve.wait_ge(sem("ssm_outer"), g * 2 + (half + 1))
                    dve.wait_ge(sem("ssm_decayed"), g * 2 + (half + 1))
                    for j in range(2):
                        b = 4 * half + 2 * j
                        s = ss0[:, b:b + 2].rearrange("p b j q -> p (b j q)")
                        mdo(V.tensor_tensor(s, s, B[4 + j][:], ALU.add), "ssm_stepped" if j else None)

                def differences(j):
                    for t in range(NT):
                        mdo(V.tensor_scalar(seg[:, j, t], B[4 + j][:, t * P:(t + 1) * P], cum[:, 0, t, j:j + 1],
                                            0.0, ALU.subtract, ALU.min), "decays_read" if t == NT - 1 else None)

                step_states(0)
                dve.wait_ge(sem("cb_ready"), g + 1)
                mdo(V.tensor_tensor(cbm[:], B[6][:].rearrange("p (t q) -> p t q", t=NT),
                                    tri[:].unsqueeze(1).to_broadcast((P, NT, P)), ALU.mult), "cbm_ready")
                if nxt is not None:
                    finish(nxt, 1 - d, 0)
                    taps(nxt, 1 - d, 1)
                step_states(1)
                for i, j in enumerate((2, 3)):
                    dve.wait_ge(sem("decays_spread"), g * 4 + (i + 1))
                    differences(j)
                if nxt is not None:
                    finish(nxt, 1 - d, 1)
                    taps(nxt, 1 - d, 2)
                for i, j in enumerate((0, 1)):
                    dve.wait_ge(sem("decays_spread"), g * 4 + (i + 3))
                    differences(j)
                for i, j in enumerate((2, 3, 0, 1)):
                    dve.wait_ge(sem("seg_expd"), g * 4 + (i + 1))
                    mdo(V.tensor_tensor(seg[:, j], seg[:, j], cbm[:], ALU.mult), "seg_ready")
                dve.wait_ge(sem("ssm_read"), g + 1)
                mdo(V.tensor_tensor(yT[:, :, TP:T], yT[:, :, TP:T],
                                    B[6][:, 0:2 * NB].rearrange("p (i b) -> p i b", i=2), ALU.add), "sample_y_read")
                if nxt is not None:
                    finish(nxt, 1 - d, 2)
                    taps(nxt, 1 - d, 3)
                    sample_taps(nxt, 1 - d)
                dve.wait_ge(sem("ssd_added"), g + 1)
                if prev is not None:
                    dve.wait_ge(sem("pssm_out"), g * 16)
                for t in range(NT):
                    add = pair(4 + t // 2)[:, t % 2]
                    if t == 0:
                        mdo(V.tensor_copy(st[:, 0], add))
                        continue
                    mdo(V.tensor_tensor(std1[:], st[:, t - 1], dec[:, t].unsqueeze(2).to_broadcast((P, CJ, CHD)),
                                        ALU.mult))
                    mdo(V.tensor_tensor(st[:, t] if t < NT - 1 else pssm[:], std1[:], add, ALU.add),
                        "states_kept" if t == NT - 1 else None)
                if nxt is not None:
                    finish(nxt, 1 - d, 3)
                    finish_samples(nxt, 1 - d)
                    gate(nxt, 1 - d, 0)
                for i in range(2):
                    mdo(V.tensor_tensor(yT[:, i, 0:TP], yT[:, i, 0:TP], B[6 + i][:], ALU.add),
                        "y_read" if i else None)
                dve.wait_ge(sem("y_inter"), g + 1)
                dve.wait_ge(sem("decays_featured"), g * 4 + 4)
                for i in range(2):
                    mdo(V.tensor_tensor(ytmp[:, i], B[4 + i][:, P:TP], efeat[:, i], ALU.mult),
                        "y_scaled" if i else None)
                for i in range(2):
                    mdo(V.tensor_tensor(yT[:, i, P:TP], yT[:, i, P:TP], ytmp[:, i], ALU.add))
                n = T_SSD + 5
                dve.wait_ge(copied[n % 2], g * (SSD_UNITS // 2) + (turns_before(n) + 1))
                for i in range(2):
                    mdo(V.scalar_tensor_tensor(yT[:, i], yT[:, i], 0.5, gz[:, d, i], ALU.mult, ALU.mult),
                        "y_gated" if i else None)
                dve.wait_ge(sem("y_squared"), g + 1)
                mdo(V.tensor_tensor(ysq[:, 0], ysq[:, 0], ysq[:, 1], ALU.add), "ysq_ready")
                if nxt is not None:
                    gate(nxt, 1 - d, 1)
                mix_tally.end()

            prepare(0, 0)
            for j in range(4):
                taps(0, 0, j)
                if j:
                    finish(0, 0, j - 1)
            sample_taps(0, 0)
            finish(0, 0, 3)
            finish_samples(0, 0)
            gate(0, 0, 0)
            gate(0, 0, 1)
            mix(0, 0, 1, None)
            with dve.Fori(0, (CG - 2) // 2) as i:
                mix(i * 2 + 1, 1, i * 2 + 2, i * 2)
                mix(i * 2 + 2, 0, i * 2 + 3, i * 2 + 1)
            mix(CG - 1, 1, None, CG - 2)
            normed(CG - 1, 1)
            do(V.memset(rstd[:], 0.0))
            for j in range(DC):
                residual(T_OUT1 + j, j, U_OUT1 + 2 * j + 2)
                add_square(3, j)
            mlp(3, T_NORM3, T_UP1, T_DOWN1, U_DOWN1, FC)
            norm(4, T_NORM4)



def _constants():
    k = np.arange(P)
    out = {}
    out["ident"] = np.eye(P)
    out["ones"] = np.ones((P, P))
    out["tri"] = k[:, None] <= k[None, :]
    out["eps"] = np.full((P, 1), EPS)
    half = AD // 2
    rot = np.zeros((P, P))
    for m in range(P):
        rot[m + half if m % AD < half else m - half, m] = -1.0 if m % AD < half else 1.0
    out["rotm"] = rot
    pos = np.concatenate([np.arange(TP), np.full(NB, WIN)]).astype(np.float32)
    freq = np.float32(10000.0) ** (-np.arange(half, dtype=np.float32) / np.float32(half))
    ang = (pos[None, :] * freq[k % half][:, None]).astype(np.float32)
    out["cos"], out["sin"] = np.cos(ang), np.sin(ang)
    dist = k[:, None] - np.arange(TP)[None, :] + (TP - P)
    count = sum(((dist >= 0) & (dist <= w) & (dist % d == 0)).astype(int) for w, d in BRANCHES)
    out["lncount"] = np.where(count > 0, np.log(np.maximum(count, 1)), NEVER)
    b = np.arange(NB)
    out["selb"] = np.broadcast_to((b[:, None] == b[None, :])[:, :, None], (NB, NB, P))
    out["rep"] = b[:, None] == np.arange(NB * AH)[None, :] // AH
    out["ownhead"] = np.arange(NB * AH)[:, None] % AH == np.arange(AW)[None, :] // AD
    out["delta"] = out["deltac"] = np.eye(NB)
    same = (k[:, None] // CH == k[None, :] // CH) & (k[:, None] <= k[None, :])
    out["tri64"] = same
    out = {n: np.ascontiguousarray(v, dtype=np.float32) for n, v in out.items()}
    out["mask64"] = np.ascontiguousarray(same.astype(np.uint32))
    return out


def _unit(w):
    return w.reshape(DC, P, P).transpose(1, 0, 2).reshape(P, DC * P)


def _columns(v):
    return v.reshape(-1, P).T


def kernel(**inputs):
    import concourse.bacc as bacc
    from concourse.bass_utils import run_bass_kernel_spmd

    x = {k: np.asarray(v) for k, v in inputs.items()}
    w_in, w_c = x["w_in_ab"][0], x["w_in_c"][0]
    q_b, g_low = 3 * AW, 3 * AW + 2 * BH * BK + BH * BV
    k_b, v_b, r_b = q_b + BH * BK, q_b + 2 * BH * BK, g_low + RANK
    starts = [i * AW + hp * P for hp in range(HP) for i in range(3)]
    for gp in range(GP):
        starts += [q_b + gp * P, k_b + gp * P, v_b + 2 * gp * P, v_b + (2 * gp + 1) * P,
                   r_b + 2 * gp * P, r_b + (2 * gp + 1) * P]
    units = [_unit(w_in[:, s:s + P]) for s in starts]
    units += [_unit(x["w_out_ab"][0][:, j * P:(j + 1) * P]) for j in range(DC)]

    def mlp(layer):
        up = [_unit(x["w_up"][layer][:, j * P:(j + 1) * P]) for j in range(FC)]
        return up + [_unit(x["w_down"][layer][q * D:(q + 1) * D, j * P:(j + 1) * P])
                     for j in range(DC) for q in range(FF // D)]

    units += mlp(0)
    for g in range(CG):
        for s in (CI + g * GW, CI + g * GW + P, 2 * CI + g * P, 2 * CI + CG * CN + g * P, g * GW, g * GW + P):
            units.append(_unit(w_c[:, s:s + P]))
    units += [_unit(x["w_out_c"][0][q * D:(q + 1) * D, j * P:(j + 1) * P])
              for j in range(DC) for q in range(CI // D)]
    units += mlp(1)
    arrays = {"units": np.stack(units)}
    assert len(units) == N_UNITS
    tokens = np.concatenate([x["x_prompt"][0], x["x_sample"][:, 0]])
    arrays["xT"] = tokens.T.reshape(DC, P, T).transpose(1, 0, 2)

    consts = _constants()
    consts["norms"] = np.stack([_columns(v) for v in (
        x["norm_mix"][0], x["norm_mlp"][0], x["norm_mix"][1], x["norm_mlp"][1], x["norm_final"])], axis=1)
    consts["wglow"] = w_in[:, g_low:g_low + RANK].reshape(DC, P, RANK).transpose(1, 0, 2)
    consts["wgate"] = x["w_gate_b"][0]
    consts["bgate"] = _columns(x["b_gate_b"][0])
    consts["wonorm"] = x["w_onorm_b"][0][:, None]
    consts["wdt"] = w_c[:, CI + 2 * CI:].reshape(DC, P, CH_ALL).transpose(1, 0, 2)
    consts["dtb"] = np.broadcast_to(x["dt_bias"][0], (P, CH_ALL))
    consts["nega"] = np.broadcast_to(x["a_log"][0], (P, CH_ALL))

    def grouped(v):
        xs, bs, cs = v[..., :CI], v[..., CI:CI + CG * CN], v[..., CI + CG * CN:]
        blocks = np.concatenate([xs.reshape(*v.shape[:-1], CG, 2, P), bs.reshape(*v.shape[:-1], CG, 1, P),
                                 cs.reshape(*v.shape[:-1], CG, 1, P)], axis=-2)
        return np.moveaxis(blocks, (-1, -3, -2), (0, 1, 2))

    two = lambda v: v.reshape(CG, 2, P).transpose(2, 0, 1)
    consts["parm"] = np.concatenate([
        grouped(x["conv_w"][0]).reshape(P, CG, 4 * TAPS), grouped(x["conv_b"][0]),
        two(np.repeat(x["d_skip"][0], CHD)), two(x["w_gnorm_c"][0]),
        grouped(x["state_conv"][0].transpose(1, 0, 2)).reshape(P, CG, 4 * 3 * NB)], axis=2)
    arrays.update({"const_" + n: v for n, v in consts.items()})
    arrays["cache_k"] = x["cache_win_k"][0].reshape(NB, WIN, AW)
    arrays["cache_v"] = x["cache_win_v"][0].reshape(NB, WIN, AW)
    arrays["gla0"] = x["state_gla"][0].reshape(NB, GP, P, BV).transpose(1, 2, 0, 3)
    arrays["ssm0"] = x["state_ssm"][0].reshape(NB, CG, CJ * CHD, CN).transpose(1, 3, 0, 2).reshape(CG, CN, NB * GW)

    outs = {"y": (P, DC, T), "pk": (HP, P, TP), "pv": (HP, P, TP), "win_k": (NB, WIN, AW), "win_v": (NB, WIN, AW),
            "pgla": (GP, P, BV), "gla1": (GP, P, NB, BV), "pconv": (P, CG * 4 * 3), "sconv": (P, CG * 4 * 3 * NB),
            "pssm": (CG, P, GW), "ssm1": (CG, CN, NB * GW)}
    nc = bacc.Bacc("TRN2", target_bir_lowering=False, num_devices=1)
    aps = {}
    arrays = {n: np.ascontiguousarray(v) for n, v in arrays.items()}
    for n, v in arrays.items():
        aps[n] = nc.dram_tensor(n, v.shape, mybir.dt.from_np(v.dtype), kind="ExternalInput").ap()
    for n, shape in outs.items():
        aps[n] = nc.dram_tensor("out_" + n, shape, F32, kind="ExternalOutput").ap()
    aps["consts"] = {n: aps["const_" + n] for n in consts}
    build(nc, aps)
    r = run_bass_kernel_spmd(nc, [arrays], core_ids=[0]).results[0]
    got = {n: np.asarray(r["out_" + n]) for n in outs}

    y = got["y"].transpose(2, 1, 0).reshape(T, D)
    cached = lambda v: v.reshape(AW, TP).T.reshape(1, 1, TP, AH, AD)
    window = lambda v: v.reshape(1, NB, WIN, AH, AD)

    def ungrouped(v):
        v = np.moveaxis(v, 0, -1)
        v = np.moveaxis(v, 2, 0)
        n = v.shape[0]
        return np.concatenate([v[:, :, 0:2].reshape(n, CI), v[:, :, 2].reshape(n, CG * CN),
                               v[:, :, 3].reshape(n, CG * CN)], axis=1)

    pconv = ungrouped(got["pconv"].reshape(P, CG, 4, 3))
    sconv = ungrouped(got["sconv"].reshape(P, CG, 4, 3 * NB)).reshape(3, NB, 2 * CI).transpose(1, 0, 2)
    pssm = got["pssm"].transpose(0, 2, 1).reshape(1, 1, CH_ALL, CHD, CN)
    sssm = got["ssm1"].reshape(CG, CN, NB, CJ, CHD).transpose(2, 0, 3, 4, 1).reshape(1, NB, CH_ALL, CHD, CN)
    pgla = got["pgla"].reshape(1, 1, BH, BK, BV)
    sgla = got["gla1"].reshape(GP, 2, BK, NB, BV).transpose(3, 0, 1, 2, 4).reshape(1, NB, BH, BK, BV)
    return (y[:TP][None], y[TP:][:, None], cached(got["pk"]), cached(got["pv"]), pgla, pconv[None, None], pssm,
            window(got["win_k"]), window(got["win_v"]), sgla, sconv[None], sssm)
```

```python
from contextlib import ExitStack

import numpy as np

import concourse.bass as bass
from concourse import mybir

F32 = mybir.dt.float32
U32 = mybir.dt.uint32
ALU = mybir.AluOpType
ACT = mybir.ActivationFunctionType
AX = mybir.AxisListType.X

P = 128
D = 1024
DC = D // P
TP = 512
NB = 8
T = TP + NB
LO, HI = 256, T - 256
NT = TP // P
EPS = 1e-5

AH, AD = 8, 64
AW = AH * AD
HP = AW // P
WIN = 2048
BRANCHES = ((128, 1), (512, 4), (2048, 16))
NBR = len(BRANCHES)
BH, BK, BV = 4, 64, 128
GP = BH // 2
RANK, TAU, CH = 16, 16.0, 64
NCH = TP // CH
FF = 4096
FC = FF // P

CI = 2048
CG, CHD, CN = 8, 64, 128
CJ = 4
CH_ALL = CG * CJ
TAPS = 4
GW = CI // CG
SCALE = AD ** -0.5

LATE_ROOT = (1, 3, 4)
HN_BEFORE = [sum(DC if r in LATE_ROOT else 2 * DC for r in range(n)) for n in range(5)]
Y_SHARE = 5
ORDERS = ((2, 3, 0, 1), (0, 1, 2, 3))
PT_AT = [sum(TP - k * P for k in range(kt)) for kt in range(NT)]
PT_COPIES = ((4, PT_AT[0], PT_AT[1]), (5, PT_AT[1], PT_AT[2]), (6, PT_AT[2], PT_AT[3] + P))
RING = 8
SLOTS = 2
SSD_UNITS = 6
U_ATT = 0
U_GLA = U_ATT + 3 * HP
U_OUT0 = U_GLA + 6 * GP
U_UP0 = U_OUT0 + DC
U_DOWN0 = U_UP0 + FC
U_SSD = U_DOWN0 + DC * (FF // D)
U_OUT1 = U_SSD + SSD_UNITS * CG
U_UP1 = U_OUT1 + DC * (CI // D)
U_DOWN1 = U_UP1 + FC
N_UNITS = U_DOWN1 + DC * (FF // D)
T_ATT = 0
T_GATE = T_ATT + 3 * HP
T_GLA = T_GATE + 1
T_OUT0 = T_GLA + 6 * GP
T_OUT0B = T_OUT0 + DC
T_UP0 = T_OUT0B + DC
T_DOWN0 = T_UP0 + FC
T_DT = T_DOWN0 + DC
T_SSD = T_DT + 1
T_OUT1 = T_SSD + SSD_UNITS * CG
AHEAD = RING // 2
T_UP1 = T_OUT1 + AHEAD + DC
T_DOWN1 = T_UP1 + FC

PW = 120
LEAST = -3.0e38
NEVER = -1.0e30
LOG1P = [1.0 / n for n in (15, 13, 11, 9, 7, 5, 3)]
COPIES = [("k", b) for b in range(NB)] + [("v", b) for b in range(NB)]


class Tally:

    def __init__(self, eng):
        self.eng, self.total, self.round, self.per, self.here = eng, {}, None, {}, {}

    def start(self, name, i):
        self.name, self.round, self.here = name, i, {}

    def end(self):
        known = self.per.setdefault(self.name, dict(self.here))
        assert known == self.here
        self.round = None

    def done(self, ins, sem):
        self.mark(ins, sem)
        if self.round is None:
            self.eng.wait_ge(sem, self.total[id(sem)])
        else:
            n = self.here[id(sem)]
            per = self.per.get(self.name)
            self.eng.wait_ge(sem, n if per is None else self.round * per[id(sem)] + n)

    def mark(self, ins, sem):
        ins.then_inc(sem, 1)
        where = self.total if self.round is None else self.here
        where[id(sem)] = where.get(id(sem), 0) + 1


def build(nc, A):
    ctx = ExitStack()
    with ctx:
        sems = {}

        def sem(name):
            if name not in sems:
                sems[name] = ctx.enter_context(nc.semaphore(name))
            return sems[name]

        def sb(name, shape, dt=F32, stack=ctx):
            return stack.enter_context(nc.sbuf_tensor(name, shape, dt))

        def flat(ap):
            names = "abcd"[:len(ap.shape) - 1]
            return ap.rearrange(f"p {' '.join(names)} -> p ({' '.join(names)})")

        B = [ctx.enter_context(nc.psum_tensor(f"bank{i}", [P, 512], F32)) for i in range(8)]

        ring = sb("ring", [P, RING, DC, P])
        h = sb("h", [P, DC, T])
        hn = sb("hn", [P, DC, T])
        std = sb("std", [P, T])
        rstd = sb("rstd", [P, T])
        ident = sb("ident", [P, P])
        tri = sb("tri", [P, P])
        normc = sb("normc", [P, P + 5 * DC + 1])
        ones = normc[:, 0:P]
        norms = normc[:, P:P + 5 * DC].rearrange("p (r k i) -> p r k i", r=5, i=1)
        eps = normc[:, P + 5 * DC:]

        wdt = sb("wdt", [P, DC, CH_ALL])
        dtb = sb("dtb", [P, CH_ALL])
        nega = sb("nega", [P, CH_ALL])
        parm = sb("parm", [P, CG, PW])
        deltac = sb("deltac", [NB, NB])

        a = ExitStack()
        rotm = sb("rotm", [P, P], stack=a)
        cos = sb("cos", [P, T], stack=a)
        sin = sb("sin", [P, T], stack=a)
        lncount = sb("lncount", [P, TP], stack=a)
        selb = sb("selb", [NB, NB, P], stack=a)
        rep = sb("rep", [NB, NB * AH], stack=a)
        ownhead = sb("ownhead", [NB * AH, AW], stack=a)
        delta = sb("delta", [NB, NB], stack=a)
        tri64 = sb("tri64", [P, P], stack=a)
        mask64 = sb("mask64", [P, P], U32, stack=a)
        wglow = sb("wglow", [P, DC, RANK], stack=a)
        wgate = sb("wgate", [RANK, BH * BK], stack=a)
        bgate = sb("bgate", [P, GP], stack=a)
        wonorm = sb("wonorm", [P, 1], stack=a)
        mixT = sb("mixT", [P, DC, T], stack=a)
        samp = sb("samp", [NB, 3, AW], stack=a)
        gath = sb("gath", [P, SLOTS, NBR, AW], stack=a)
        gprod = sb("gprod", [P, NBR, AW], stack=a)
        s3 = sb("s3", [P, NBR, NB * AH], stack=a)
        krep = gprod[0:NB * AH, 0]
        kscr = gprod[0:NB * AH, 1]
        vrep = gprod[0:NB * AH, 2]
        sexp = sb("sexp", [NB * AH, NBR, P], stack=a)
        sst = sb("sst", [NB * AH, 10], stack=a)
        sdiag = sb("sdiag", [NB * AH, NB * AH], stack=a)
        spt = sb("spt", [P, NBR, NB * AH], stack=a)
        glow = sb("glow", [RANK, T], stack=a)
        qg = sb("qg", [P, GP, T], stack=a)
        kg = sb("kg", [P, GP, T], stack=a)
        vg = sb("vg", [P, BH, T], stack=a)
        rg = sb("rg", [P, BH, T], stack=a)
        b0 = ExitStack()
        qraw = sb("qraw", [P, T], stack=b0)
        kraw = sb("kraw", [P, T], stack=b0)
        vraw = sb("vraw", [P, T], stack=b0)
        qr = sb("qr", [P, T], stack=b0)
        kr = sb("kr", [P, T], stack=b0)
        rt = sb("rt", [P, 2, T], stack=b0)
        vtok = sb("vtok", [P, NT, P], stack=b0)
        probs = sb("probs", [P, NT, TP], stack=b0)
        pstat = sb("pstat", [P, 4, NT], stack=b0)
        pt = sb("pt", [P, sum(TP - kt * P for kt in range(NT))], stack=b0)
        b0.close()
        b1 = ExitStack()
        gt = sb("gt", [P, 6, T], stack=b1)
        vdiag = sb("vdiag", [NB, 2, NB, P], stack=b1)
        loga = sb("loga", [P, GP, T], stack=b1)
        latok = gprod[:, 0].rearrange("p (t k) -> p t k", k=P)
        bT = gprod[:, 1].rearrange("p (c t) -> p c t", c=NCH)
        eb = sb("eb", [P, GP, NCH, CH], stack=b1)
        enb = sb("enb", [P, GP, NCH, CH], stack=b1)
        ee = sb("ee", [P, GP, NCH, CH], stack=b1)
        sdec = sb("sdec", [P, GP, NB], stack=b1)
        rows_left = flat(gath[:])
        gst = rows_left[:, 0:(NCH + 1) * P].rearrange("p (c v) -> p c v", v=P)
        ketok = rows_left[:, (NCH + 1) * P:(NCH + 1) * P + TP].rearrange("p (t k) -> p t k", k=P)
        gvtok = rows_left[:, (NCH + 1) * P + TP:(NCH + 1) * P + 3 * TP].rearrange("p (e t v) -> p e t v", e=2, v=P)
        gsamp = sb("gsamp", [NB, 3, P], stack=b1)
        att = sb("att", [P, 2, NT, P], stack=b1)
        gs0 = sb("gs0", [P, NB, P], stack=b1)
        b1.close()
        a.close()

        m = ExitStack()
        hid = sb("hid", [P, FC, T], stack=m)
        m.close()

        c = ExitStack()
        pg = sb("pg", [P, 2, 24], stack=c)
        dts = sb("dts", [P, 8, NT + 1, CH_ALL], stack=c)
        dtg = sb("dtg", [P, 2, NT + 1, CJ], stack=c)
        dag = sb("dag", [P, 2, NT + 1, CJ], stack=c)
        xe = sb("xe", [P, 4, TAPS - 1 + TP], stack=c)
        xs = sb("xs", [P, 4, TAPS, NB], stack=c)
        xsp = sb("xsp", [P, 4, TAPS, NB], stack=c)
        conv = sb("conv", [P, 2, 4, T], stack=c)
        th = sb("th", [P, 2, T], stack=c)
        gz = sb("gz", [P, 2, 2, T], stack=c)
        ths = sb("ths", [P, 4, NB], stack=c)
        root = sb("root", [P, 1], stack=c)
        ystd = sb("ystd", [P, T], stack=c)
        yrstd = sb("yrstd", [P, T], stack=c)
        cum = sb("cum", [P, 2, NT, CJ], stack=c)
        dec = sb("dec", [P, NT, CJ], stack=c)
        toend = sb("toend", [P, NT, CJ], stack=c)
        xdt = sb("xdt", [P, NT, CJ, CHD], stack=c)
        btok = sb("btok", [P, NT, P], stack=c)
        cbm = sb("cbm", [P, NT, P], stack=c)
        seg = sb("seg", [P, CJ, NT, P], stack=c)
        st = sb("st", [P, NT - 1, CJ, CHD], stack=c)
        std1 = sb("std1", [P, CJ, CHD], stack=c)
        turns3 = sb("turns3", [P, 2 * T], stack=c)
        xde = turns3[:, 0:NT * GW].rearrange("p (t j q) -> p t j q", j=CJ, q=CHD)
        ytmp = turns3[:, 0:2 * (TP - P)].rearrange("p (i t) -> p i t", i=2)
        ysq = turns3[:].rearrange("p (i t) -> p i t", i=2)
        efeat = sb("efeat", [P, 2, TP - P], stack=c)
        yT = sb("yT", [P, 2, T], stack=c)
        ssamp = sb("ssamp", [NB, 3, P], stack=c)
        sxdt = sb("sxdt", [NB, CJ, CHD], stack=c)
        sadg = sb("sadg", [NB, 2, NB, CJ], stack=c)
        sadec = sb("sadec", [P, NB, CJ], stack=c)
        sxdiag = seg[0:NB].rearrange("k j t q -> k (j t q)").rearrange("k (b c) -> k b c", b=NB)
        ss0 = sb("ss0", [P, NB, CJ, CHD], stack=c)
        yout = sb("yout", [P, 2 * CG, T], stack=c)
        pconv = sb("pconv", [P, CG, 4, TAPS - 1], stack=c)
        sconv = sb("sconv", [P, CG, 4, TAPS - 1, NB], stack=c)
        pssm = sb("pssm", [P, CJ, CHD], stack=c)
        c.close()

        x_in = [sem(f"x_in{i}") for i in range(DC // 2)]
        norm_consts_in = sem("norm_consts_in")
        consts_in = sem("consts_in")
        late_consts_in = sem("late_consts_in")
        units_multiplied = sem("units_multiplied")
        copied = [sem("pair0_copied"), sem("pair1_copied")]
        ring_in = [sem(f"ring{s}_in") for s in range(RING)]
        squares = sem("squares")
        squares_added = sem("squares_added")
        norm_summed = sem("norm_summed")
        std_ready = sem("std_ready")
        hn_ready = sem("hn_ready")
        hidden = sem("hidden")
        caches_written = sem("caches_written")

        def lo(n):
            return B[2 * (n % 2)][:, 0:LO]

        def hi(n):
            return B[2 * (n % 2) + 1][:, 0:HI]

        def turns_before(n):
            return n // 2

        MATMULS = [(slice(0, LO), lo), (slice(LO, T), hi)]

        NORM_CONSTS = ("normc",)
        FIRST_CONSTS = ("ident", "rotm", "cos", "sin", "lncount")
        LATE_CONSTS = [n for n in A["consts"] if n not in NORM_CONSTS + FIRST_CONSTS]
        const_tiles = dict(ident=ident, tri=tri, normc=normc, rotm=rotm, cos=cos, sin=sin,
                           lncount=lncount, selb=selb, rep=rep, ownhead=ownhead, delta=delta, tri64=tri64,
                           mask64=mask64, wglow=wglow, wgate=wgate, bgate=bgate, wonorm=wonorm, wdt=wdt,
                           dtb=dtb, nega=nega, parm=parm, deltac=deltac)
        block = ctx.enter_context(nc.Block())

        @block.sync
        def _(sp):
            for i in range(DC // 2):
                sp.dma_start(h[:, 2 * i:2 * i + 2], A["xT"][:, 2 * i:2 * i + 2]).then_inc(x_in[i], 16)

            def load(w, s):
                sp.dma_start(flat(ring[:, s]), A["units"][w]).then_inc(ring_in[s], 16)

            for s in range(RING):
                load(s, s)
                if s == 1:
                    for name in FIRST_CONSTS:
                        sp.dma_start(const_tiles[name][:], A["consts"][name]).then_inc(consts_in, 16)
            for name in LATE_CONSTS:
                sp.dma_start(const_tiles[name][:], A["consts"][name]).then_inc(late_consts_in, 16)
            with sp.Fori(1, U_SSD // RING) as i:
                for s in range(RING):
                    sp.wait_ge(units_multiplied, i * RING + (s + 1 - RING))
                    load(i * RING + s, s)
            for s in range(SSD_UNITS):
                sp.wait_ge(units_multiplied, U_SSD - RING + s + 1)
                load(U_SSD + s, s)
            with sp.Fori(1, CG) as g:
                for s in range(SSD_UNITS):
                    sp.wait_ge(units_multiplied, g * SSD_UNITS + (U_SSD - SSD_UNITS + s + 1))
                    load(g * SSD_UNITS + (U_SSD + s), s)
            for s in range(RING):
                if s < SSD_UNITS:
                    sp.wait_ge(units_multiplied, U_OUT1 - SSD_UNITS + s + 1)
                load(U_OUT1 + s, s)
            with sp.Fori(1, (N_UNITS - U_OUT1) // RING) as i:
                for s in range(RING):
                    sp.wait_ge(units_multiplied, i * RING + (U_OUT1 - RING + s + 1))
                    load(i * RING + (U_OUT1 + s), s)
            parts = 0
            for high, (cols, _) in enumerate(MATMULS):
                for first, end, scaled in ((0, 2, "y_scaled_vector"), (Y_SHARE, DC, "y_scaled_pool"),
                                           (2, Y_SHARE, "y_scaled_vector")):
                    own = Y_SHARE if scaled == "y_scaled_vector" else DC - Y_SHARE
                    sp.wait_ge(sem(scaled), high * own + (end if scaled == "y_scaled_vector" else own))
                    sp.dma_start(A["y"][:, first:end, cols], hn[:, first:end, cols]).then_inc(sem("y_written"), 16)
                    parts += 1
            sp.wait_ge(sem("y_written"), 16 * parts)

        @block.gpsimd
        def _(pool):
            copy_sent = [0]

            def cache_copy(units_done):
                kind, b = COPIES[copy_sent[0]]
                copy_sent[0] += 1
                if units_done:
                    pool.wait_ge(units_multiplied, units_done)
                src = A["cache_" + kind][b, 1:WIN].rearrange("t d -> (t d)")
                dst = A["win_" + kind][b, 0:WIN - 1].rearrange("t d -> (t d)")
                pool.dma_start(dst, src).then_inc(caches_written, 16)

            def gather(n):
                kind, b = COPIES[n]
                if n >= SLOTS:
                    if n - SLOTS < NB:
                        pool.wait_ge(sem("keys_scored"), n - SLOTS + 1)
                    else:
                        pool.wait_ge(sem("values_mixed"), n - SLOTS + 1 - NB)
                for i, (w, d) in enumerate(BRANCHES):
                    pool.dma_start(gath[:, n % SLOTS, i], A["cache_" + kind][b, WIN - w:WIN:d]).then_inc(
                        sem(f"gathered{n % SLOTS}"), 16)

            pool.wait_ge(x_in[DC // 2 - 1], 16)
            gather(0)
            gather(1)
            for hp in range(HP):
                pool.wait_ge(sem("rope_done"), 2 * hp + 2)
                pool.dma_start(A["pk"][hp], kr[:, 0:TP]).then_inc(sem("k_written"), 16)
                pool.wait_ge(copied[(T_ATT + 3 * hp + 2) % 2], turns_before(T_ATT + 3 * hp + 2) + 1)
                pool.dma_start(A["pv"][hp], vraw[:, 0:TP]).then_inc(sem("v_written"), 16)
            pool.wait_ge(sem("samp_ready"), HP)
            pool.dma_start(A["win_k"][:, WIN - 1, :], samp[:, 1, :]).then_inc(sem("samp_written"), 16)
            pool.dma_start(A["win_v"][:, WIN - 1, :], samp[:, 2, :]).then_inc(sem("samp_written"), 16)
            for n in range(SLOTS, 2 * NB):
                gather(n)
            for gp in range(GP):
                if gp:
                    pool.wait_ge(sem("gla_state_out"), 16)
                    pool.wait_ge(sem("gla_sample_out"), gp)
                else:
                    pool.wait_ge(sem("o_copied"), AH)
                    pool.wait_ge(sem("v_written"), 16 * HP)
                    pool.wait_ge(sem("k_written"), 16 * HP)
                pool.dma_start(gs0[:], A["gla0"][gp]).then_inc(sem("gla_state_in"), 16)
                pool.wait_ge(sem("gla_stepped"), gp + 1)
                pool.dma_start(A["gla1"][gp], gs0[:]).then_inc(sem("gla_state_out"), 16)
                pool.wait_ge(sem("gla_chained"), gp + 1)
                pool.dma_start(A["pgla"][gp], gst[:, NCH]).then_inc(sem("gla_prompt_out"), 16)
            for n in range(2 * NB - 4):
                cache_copy(U_UP0 + 5 * n)
            pool.wait_ge(units_multiplied, U_SSD)

            def states(g):
                pool.dma_start(flat(ss0[:]), A["ssm0"][g]).then_inc(sem("ssm_in"), 16)
                if g:
                    pool.wait_ge(sem("y_intra"), g)
                pool.wait_ge(sem("sxdt_ready"), g + 1)
                nc.gpsimd.tensor_tensor(sxdiag, flat(sxdt[:]).unsqueeze(1).to_broadcast((NB, NB, GW)),
                                        deltac[:].unsqueeze(2).to_broadcast((NB, NB, GW)), ALU.mult).then_inc(
                    sem("sxdiag_ready"), 1)
                pool.wait_ge(sem("ssm_in"), g * 16 + 16)
                pool.wait_ge(sem("sadec_ready"), g + 1)
                for half in (slice(0, NB // 2), slice(NB // 2, NB)):
                    s = ss0[:, half].rearrange("p b j q -> p (b j) q")
                    decays = sadec[:, half].rearrange("p b j -> p (b j)").unsqueeze(2)
                    nc.gpsimd.tensor_tensor(s, s, decays.to_broadcast((P, NB // 2 * CJ, CHD)), ALU.mult).then_inc(
                        sem("ssm_decayed"), 1)
                pool.wait_ge(sem("ssm_read"), g + 1)
                pool.dma_start(A["ssm1"][g], flat(ss0[:])).then_inc(sem("ssm_out"), 16)
                pool.wait_ge(sem("states_kept"), g + 1)
                pool.dma_start(A["pssm"][g], flat(pssm[:])).then_inc(sem("pssm_out"), 16)
                pool.wait_ge(sem("ssm_out"), g * 16 + 16)

            for g in range(CG):
                states(g)
            pool.wait_ge(sem("conv_kept"), 2 * CG)
            pool.dma_start(A["pconv"], flat(pconv[:])).then_inc(sem("layer1_out"), 16)
            pool.dma_start(A["sconv"], flat(sconv[:])).then_inc(sem("layer1_out"), 16)
            for n in range(4):
                cache_copy(U_UP1 + 4 * n)
            pool.wait_ge(hn_ready, HN_BEFORE[4] + DC)
            for high, (cols, _) in enumerate(MATMULS):
                pool.wait_ge(sem("last_root"), high + 1)
                for k in range(Y_SHARE, DC):
                    nc.gpsimd.tensor_tensor(hn[:, k, cols], hn[:, k, cols], rstd[:, cols], ALU.mult).then_inc(
                        sem("y_scaled_pool"), 1)
            pool.wait_ge(caches_written, 16 * len(COPIES))
            pool.wait_ge(sem("layer1_out"), 32)
            pool.wait_ge(sem("gla_prompt_out"), 16 * GP)
            pool.wait_ge(sem("gla_state_out"), 16 * GP)

        @block.tensor
        def _(pe):
            mm = nc.tensor.matmul

            def unit(w, n, s, count, src, first=0, last=True, start=True, ready=None, blocks=range(DC), used=True,
                     between=None):
                pe.wait_ge(ring_in[s], count * 16)
                for cols, half in MATMULS:
                    for k in blocks:
                        if ready is not None:
                            pe.wait_ge(*ready(k, cols.start > 0))
                        x = mm(half(n), ring[:, s, k], src[:, first + k, cols],
                               start=start and k == blocks[0], stop=last and k == blocks[-1])
                        if between is not None and not (cols.start and k == blocks[-1]):
                            between(k + DC * (cols.start > 0))
                x.then_inc(units_multiplied if used else sem("parts_multiplied"), 1)

            def bank_free(n, more=0):
                if n >= 2:
                    pe.wait_ge(copied[n % 2], turns_before(n) + more)

            def norm(r):
                pe.wait_ge(squares_added, (r + 1) * DC)
                for i, (cols, _) in enumerate(MATMULS):
                    mm(B[4 + i][:, 0:cols.stop - cols.start], ones, rstd[:, cols], start=True, stop=True).then_inc(
                        norm_summed, 1)

            def normed(r):
                return lambda k, high: (hn_ready, HN_BEFORE[r] + k + 1 + (0 if r in LATE_ROOT else DC * high))

            pe.wait_ge(norm_consts_in, 16 * len(NORM_CONSTS))
            norm(0)

            at = [0]

            def project():
                w = at[0]
                if w >= U_OUT0:
                    return
                at[0] += 1
                n = T_ATT + w if w < U_GLA else T_GLA + w - U_GLA
                if w == U_GLA:
                    gates()
                bank_free(n)
                unit(w, n, w % RING, w // RING + 1, hn,
                     ready=normed(0) if w == 0 else None)

            def gates():
                n = T_GATE
                bank_free(n)
                pe.wait_ge(late_consts_in, 16 * len(LATE_CONSTS))
                for cols, half in MATMULS:
                    for k in range(DC):
                        x = mm(half(n)[0:RANK], wglow[:, k], hn[:, k, cols], start=k == 0, stop=k == DC - 1)
                x.then_inc(sem("glow_summed"), 1)

            def rotate(hp):
                for i, (raw, n) in enumerate(((qraw, T_ATT + 3 * hp), (kraw, T_ATT + 3 * hp + 1))):
                    pe.wait_ge(copied[n % 2], turns_before(n) + 1)
                    if hp and not i:
                        pe.wait_ge(sem("pt_copied"), 2 * hp * len(PT_COPIES))
                    elif hp:
                        pe.wait_ge(sem("o_copied"), 2 * hp)
                    for j, cols in enumerate((slice(0, LO), slice(LO, T))):
                        x = mm(B[4 + 2 * i + j][:, 0:cols.stop - cols.start], rotm[:], raw[:, cols],
                               start=True, stop=True)
                    x.then_inc(sem("rotated"), 1)

            def to_tokens(hp):
                pe.wait_ge(sem("rope_done"), 2 * hp + 2)
                n = T_ATT + 3 * hp + 2
                pe.wait_ge(copied[n % 2], turns_before(n) + 1)
                for t in range(NT):
                    pe.transpose(B[4][:, t * P:(t + 1) * P], vraw[:, t * P:(t + 1) * P], ident[:])
                for i, src in enumerate((qr, kr, vraw)):
                    x = pe.transpose(B[5][0:NB, i * P:(i + 1) * P], src[:, TP:T], ident[:])
                x.then_inc(sem("v_turned"), 1)

            def scores(hp, e):
                hd = 2 * hp + e
                if e == 1:
                    pe.wait_ge(sem("pt_copied"), hd * len(PT_COPIES))
                rows = slice(AD * e, AD * e + AD)
                for i, j in enumerate(ORDERS[e]):
                    if e == 0 and i == 2:
                        pe.wait_ge(sem("samp_ready"), hp + 1)
                    if e == 1 and i == 3:
                        pe.wait_ge(sem("o_copied"), hd)
                    mm(B[4 + j][:, 0:(j + 1) * P], qr[rows, j * P:(j + 1) * P], kr[rows, 0:(j + 1) * P],
                       start=True, stop=True).then_inc(sem("scored"), 1)

            def mix_values(hp, e):
                hd = 2 * hp + e
                pe.wait_ge(sem("p_ready"), (hd + 1) * NT)
                for kt in range(NT):
                    bank, at = (4 + kt, 0) if kt < 3 else (6, TP - 2 * P)
                    for j in range(kt, NT):
                        x = pe.transpose(B[bank][:, at + (j - kt) * P:at + (j - kt + 1) * P],
                                         probs[:, j, kt * P:(kt + 1) * P], ident[:])
                    if kt != 2:
                        x.then_inc(sem("p_turned"), 1)
                for kt in range(NT):
                    pe.wait_ge(sem("pt_copied"), hd * len(PT_COPIES) + min(kt, 2) + 1)
                    mm(B[7][AD * e:AD * e + AD, kt * P:TP], vtok[:, kt, AD * e:AD * e + AD],
                       pt[:, PT_AT[kt]:PT_AT[kt] + TP - kt * P], start=kt == 0, stop=kt == NT - 1,
                       skip_group_check=True).then_inc(sem("pv_done"), 1)

            def sample_q(b):
                if b < 2:
                    pe.wait_ge(sem("pt_copied"), AH * len(PT_COPIES))
                    pe.wait_ge(sem("samp_ready"), HP)
                else:
                    pe.wait_ge(sem("keys_scored"), b - 1)
                mm(B[4 + b % 2][:, 0:AW], selb[:, b, :], samp[:, 0, :], start=True, stop=True).then_inc(
                    sem("sample_q_spread"), 1)

            def sample_rows():
                pe.wait_ge(sem("keys_scored"), NB)
                for i in range(NBR):
                    pe.transpose(B[6][0:NB * AH, i * P:(i + 1) * P], s3[:, i, :], ident[:])
                for i, bank in enumerate((4, 5, 7)):
                    x = mm(B[bank][0:NB * AH, 0:AW], rep[:], samp[:, i, :], start=True, stop=True)
                x.then_inc(sem("sample_rows_ready"), 1)

            def sample_cols():
                pe.wait_ge(sem("sample_probs"), 1)
                for i in range(NBR):
                    x = pe.transpose(B[4][:, i * NB * AH:(i + 1) * NB * AH], sexp[:, i, :],
                                     ident[0:NB * AH, 0:NB * AH])
                x.then_inc(sem("sample_probs_turned"), 1)

            def sample_mix():
                pe.wait_ge(sem("spt_copied"), 1)
                out = B[5][:, 0:HP * NB * 2].rearrange("p (a b e) -> p a b e", a=HP, b=NB)
                for b in range(NB):
                    n = NB + b
                    pe.wait_ge(sem(f"gathered{n % SLOTS}"), 16 * NBR * (n // SLOTS + 1))
                    for hp in range(HP):
                        for i in range(NBR):
                            x = mm(out[:, hp, b, :], gath[:, n % SLOTS, i, hp * P:(hp + 1) * P],
                                   spt[:, i, b * AH + 2 * hp:b * AH + 2 * hp + 2],
                                   start=b == 0 and hp == 0 and i == 0, stop=False, skip_group_check=True)
                    x.then_inc(sem("values_mixed"), 1)
                own = sdiag[:].rearrange("r (b k) -> r b k", b=NB)
                for hp in range(HP):
                    x = mm(out[:, hp, :, :], vrep[:, hp * P:(hp + 1) * P], own[:, :, 2 * hp:2 * hp + 2],
                           start=False, stop=hp == HP - 1, skip_group_check=True)
                x.then_inc(sem("sample_mixed"), 1)

            def gate_logits(gp):
                if gp == 0:
                    pe.wait_ge(copied[T_GATE % 2], turns_before(T_GATE) + 1)
                    pe.wait_ge(sem("pt_copied"), AH * len(PT_COPIES))
                    pe.wait_ge(sem("o_copied"), AH)
                else:
                    pe.wait_ge(sem("gate_folded"), gp)
                for j, cols in enumerate((slice(0, LO), slice(LO, T))):
                    x = mm(B[6 + j][:, 0:cols.stop - cols.start], wgate[:, gp * P:(gp + 1) * P], glow[:, cols],
                           start=True, stop=True)
                x.then_inc(sem("gate_logits"), 1)

            def gate_turn(gp):
                pe.wait_ge(sem("gate_folded"), GP)
                pe.wait_ge(sem("loga_ready"), gp + 1)
                for t in range(NT):
                    x = pe.transpose(B[6][:, t * P:(t + 1) * P], loga[:, gp, t * P:(t + 1) * P], ident[:])
                x.then_inc(sem("loga_turned"), 1)

            def gate_sums(gp):
                pe.wait_ge(sem("latok_ready"), gp + 1)
                if gp:
                    pe.wait_ge(sem("sums_copied"), gp)
                for t in range(NT):
                    x = mm(B[7][:, t * P:(t + 1) * P], latok[:, t, :], tri64[:], start=True, stop=True)
                x.then_inc(sem("gates_summed"), 1)

            def gla_tokens(gp):
                if gp == 0:
                    pe.wait_ge(sem("sample_out"), 2)
                    pe.wait_ge(sem("sums_copied"), GP)
                else:
                    pe.wait_ge(sem("gla_std"), 2 * gp)
                pe.wait_ge(sem("k_end_ready"), gp + 1)
                for i in range(2):
                    n = T_GLA + 6 * gp + 2 + i
                    pe.wait_ge(copied[n % 2], turns_before(n) + 1)
                for t in range(NT):
                    pe.transpose(B[6][:, t * P:(t + 1) * P], flat(ee[:, gp])[:, t * P:(t + 1) * P], ident[:])
                    pe.transpose(B[7][:, t * P:(t + 1) * P], vg[:, 2 * gp, t * P:(t + 1) * P], ident[:])
                    pe.transpose(B[4][:, t * P:(t + 1) * P], vg[:, 2 * gp + 1, t * P:(t + 1) * P], ident[:])
                for i, src in enumerate((kg[:, gp], vg[:, 2 * gp], vg[:, 2 * gp + 1])):
                    x = pe.transpose(B[5][0:NB, i * P:(i + 1) * P], src[:, TP:T], ident[:])
                x.then_inc(sem("gla_turned"), 1)

            def gla_att(gp):
                pe.wait_ge(sem("gla_tokens_ready"), gp + 1)
                for e in range(2):
                    rows = slice(BK * e, BK * e + BK)
                    for t in range(NT):
                        x = mm(B[6 + e][:, t * P:(t + 1) * P], gt[rows, 1, t * P:(t + 1) * P],
                               gt[rows, 0, t * P:(t + 1) * P], start=True, stop=True)
                x.then_inc(sem("gla_att"), 1)
                for ch in range(NCH):
                    for e in range(2):
                        rows = slice(CH * (ch % 2), CH * (ch % 2) + CH)
                        x = mm(B[4 + ch % 2][BK * e:BK * e + BK, (ch // 2) * P:(ch // 2 + 1) * P],
                               ketok[rows, ch // 2, BK * e:BK * e + BK], gvtok[rows, e, ch // 2, :],
                               start=True, stop=True, skip_group_check=True)
                x.then_inc(sem("gla_added"), 1)

            def gla_out(gp):
                pe.wait_ge(sem("gla_masked"), gp + 1)
                pe.wait_ge(sem("gla_chained"), gp + 1)
                for e in range(2):
                    rows = slice(BK * e, BK * e + BK)
                    for t in range(NT):
                        mm(B[6 + e][:, t * P:(t + 1) * P], gvtok[:, e, t, :], att[:, e, t, :],
                           start=True, stop=False, skip_group_check=True)
                        for ch in (2 * t, 2 * t + 1):
                            if ch:
                                x = mm(B[6 + e][:, ch * CH:(ch + 1) * CH], gst[rows, ch, :],
                                       gt[rows, 0, ch * CH:(ch + 1) * CH], start=False, stop=ch % 2 == 1,
                                       skip_group_check=True)
                x.then_inc(sem("gla_out"), 1)
                for bh in range(2):
                    for e in range(2):
                        x = mm(B[4 + bh][BK * e:BK * e + BK, :], gsamp[:, 0, BK * e:BK * e + BK],
                               vdiag[:, e, 4 * bh:4 * bh + 4, :].rearrange("k b v -> k (b v)"), start=True, stop=True,
                               skip_group_check=True)
                x.then_inc(sem("gla_sample_kv"), 1)

            def gla_sample_out(gp):
                pe.wait_ge(sem("gla_stepped"), gp + 1)
                for e in range(2):
                    rows = slice(BK * e, BK * e + BK)
                    for b in range(NB):
                        x = mm(B[4 + e][:, b:b + 1], gs0[rows, b, :], qg[rows, gp, TP + b:TP + b + 1],
                               start=True, stop=True, skip_group_check=True)
                x.then_inc(sem("gla_sample_out"), 1)

            def gla_norm(gp):
                pe.wait_ge(sem("gla_squares"), 2 * gp + 2)
                for e in range(2):
                    for j, cols in enumerate((slice(0, LO), slice(LO, T))):
                        x = mm(B[4 + 2 * e + j][:, 0:cols.stop - cols.start], ones, gt[:, 2 + e, cols],
                               start=True, stop=True)
                x.then_inc(sem("gla_squares_summed"), 1)

            for _ in range(3):
                project()
            pe.wait_ge(consts_in, 16 * len(FIRST_CONSTS))
            for hp in range(HP):
                rotate(hp)
                project()
                to_tokens(hp)
                scores(hp, 0)
                project()
                mix_values(hp, 0)
                scores(hp, 1)
                project()
                mix_values(hp, 1)
            for b in range(NB):
                sample_q(b)
                if b == 1:
                    gate_logits(0)
                if b % 2:
                    project()
            sample_rows()
            project()
            sample_cols()
            gate_logits(1)
            sample_mix()
            gate_turn(0)
            project()
            gate_sums(0)
            gate_turn(1)
            project()
            gate_sums(1)
            assert U_OUT0 % RING == 0

            def out_half(j, part):
                n, w = (T_OUT0, T_OUT0B)[part] + j, U_OUT0 + j
                bank_free(n)
                split = HP if j < DC // 2 else HP + 2
                if part == 0 and j == DC // 2:
                    pe.wait_ge(sem("gla_mixed"), 2)
                unit(w, n, w % RING, w // RING + 1, mixT, blocks=range(split) if part == 0 else range(split, DC),
                     used=part == 1)

            gla_tokens(0)
            project()
            gla_att(0)
            project()
            gla_out(0)
            out_half(0, 0)
            gla_sample_out(0)
            out_half(1, 0)
            gla_norm(0)
            out_half(2, 0)
            gla_tokens(1)
            out_half(3, 0)
            gla_att(1)
            out_half(4, 0)
            gla_out(1)
            out_half(5, 0)
            gla_sample_out(1)
            out_half(6, 0)
            gla_norm(1)
            out_half(7, 0)
            for j in range(2):
                bank_free(T_OUT0B + j)
            for heads in ((0, 1), (2,), (3,)):
                pe.wait_ge(sem("gla_mixed"), heads[-1] + 1)
                for j in range(2):
                    for cols, half in MATMULS:
                        for k in heads:
                            x = mm(half(T_OUT0B + j), ring[:, j, HP + k], mixT[:, HP + k, cols], start=k == 0,
                                   stop=k == BH - 1, skip_group_check=True)
                    if heads[-1] == BH - 1:
                        x.then_inc(units_multiplied, 1)
            for j in range(2, DC):
                out_half(j, 1)

            def mlp(layer, r, t_up, t_down, u_up, load_up):

                def up(i):
                    for s in range(RING):
                        bank_free(t_up + s, i * (RING // 2))
                        unit(i * RING + (u_up + s), t_up + s, s, i + (load_up[s] + 1), hn,
                             ready=normed(r) if isinstance(i, int) and s == 0 else None)
                        if isinstance(i, int) and s == 0:
                            norm(r)

                up(0)
                with pe.Fori(1, FC // RING) as i:
                    up(i)
                with pe.Fori(0, DC // 2) as i:
                    for s in range(RING):
                        part = s % (FF // D)
                        n = t_down + s // (FF // D)
                        if part == 0:
                            bank_free(n, i)
                        pe.wait_ge(hidden, layer * FC + (part + 1) * DC)
                        unit(None, n, s, i + (load_up[s] + FC // RING + 1), hid, first=part * DC,
                             start=part == 0, last=part == FF // D - 1)

            mlp(0, 1, T_UP0, T_DOWN0, U_UP0, [U_UP0 // RING] * RING)

            norm(2)

            def ssd_project(g, j, between=None, ready=None):
                n = T_SSD + j
                bank_free(n, g * (SSD_UNITS // 2))
                unit(None, n, j, g + (U_SSD // RING + 1), hn, between=between, ready=ready)

            def ssd_tokens(g, d):
                pe.wait_ge(sem("conv_ready"), g + 1)
                for t in range(NT):
                    pe.transpose(B[6][:, t * P:(t + 1) * P], conv[:, d, 2, t * P:(t + 1) * P], ident[:])
                for i in range(3):
                    pe.transpose(B[7][0:NB, 32 + i * P:32 + (i + 1) * P], conv[:, d, i, TP:T], ident[:])
                mm(B[7][:, 0:16], tri[:], flat(dag[:, d, 0:NT]), start=True, stop=True)
                mm(B[7][:, 16:32], ones, flat(dag[:, d, 0:NT]), start=True, stop=True)
                mm(B[7][:, 416:448], ones[0:NB], flat(sadg[:, d]), start=True, stop=True).then_inc(
                    sem("ssd_turned"), 1)
                for t in range(NT):
                    if t % 2 == 0 and (not isinstance(g, int) or g > 0):
                        pe.wait_ge(sem("y_std" if t else "y_std_low"), g)
                    for i in range(2):
                        x = pe.transpose(B[4 + t // 2][:, (t % 2) * GW + i * P:(t % 2) * GW + (i + 1) * P],
                                         conv[:, d, i, t * P:(t + 1) * P], ident[:])
                x.then_inc(sem("x_turned"), 1)

            def sample_outer(g, half):
                if half == 0:
                    pe.wait_ge(sem("xdt_ready"), g + 1)
                    pe.wait_ge(sem("sxdiag_ready"), g + 1)
                else:
                    pe.wait_ge(sem("ssm_stepped"), g * 2 + 1)
                for j in range(2):
                    b = 4 * half + 2 * j
                    x = mm(B[4 + j][:], ssamp[:, 2, :], sxdiag[:, b:b + 2, :].rearrange("k b c -> k (b c)"), start=True, stop=True)
                x.then_inc(sem("ssm_outer"), 1)

            def ssd_cb(g, d):
                pe.wait_ge(sem("btok_ready"), g + 1)
                for t in range(NT):
                    x = mm(B[6][:, t * P:(t + 1) * P], conv[:, d, 2, t * P:(t + 1) * P],
                           conv[:, d, 3, t * P:(t + 1) * P], start=True, stop=True)
                x.then_inc(sem("cb_ready"), 1)

            def ssd_spread(g, d, heads):
                for j in heads:
                    if j == 2:
                        pe.wait_ge(sem("cbm_ready"), g + 1)
                    if j == 3:
                        for read in ("small_read", "ssamp_read", "sadec_ready"):
                            pe.wait_ge(sem(read), g + 1)
                    if j == 0:
                        pe.wait_ge(sem("ssm_stepped"), g * 2 + 2)
                    for t in range(NT):
                        x = mm(B[4 + j][:, t * P:(t + 1) * P], dag[:, d, t, j:j + 1].to_broadcast((P, P)), tri[:],
                               start=True, stop=True)
                    x.then_inc(sem("decays_spread"), 1)

            def sample_y(g, d, products):
                pe.wait_ge(sem("decays_featured"), g * 4 + 1)
                pe.wait_ge(sem("ssm_stepped"), g * 2 + 2)

                def some(m):
                    for n in range(m * 2 * NB // (products - 1), (m + 1) * 2 * NB // (products - 1)):
                        i, b = n // NB, n % NB
                        x = mm(B[6][:, n:n + 1], flat(ss0[:, b, 2 * i:2 * i + 2, :]),
                               conv[:, d, 3, TP + b:TP + b + 1], start=True, stop=True, skip_group_check=True)
                        if n == 2 * NB - 1:
                            x.then_inc(sem("ssm_read"), 1)
                return some

            def ssd_intra(g):
                for j in (2, 3, 0, 1):
                    if j == 2:
                        pe.wait_ge(sem("seg_ready"), g * 4 + 2)
                    if j == 0:
                        pe.wait_ge(sem("seg_ready"), g * 4 + 4)
                        pe.wait_ge(sem("decays_featured"), g * 4 + 4)
                        pe.wait_ge(sem("sample_y_read"), g + 1)
                    for t in range(NT):
                        x = mm(B[6 + j // 2][CHD * (j % 2):CHD * (j % 2) + CHD, t * P:(t + 1) * P], xdt[:, t, j, :],
                               seg[:, j, t, :], start=True, stop=True, skip_group_check=True)
                x.then_inc(sem("y_intra"), 1)
                pe.wait_ge(sem("xde_ready"), g + 1)
                for t in range(NT):
                    x = mm(B[4 + t // 2][:, (t % 2) * GW:(t % 2 + 1) * GW], btok[:, t, :], xde[:, t].rearrange("p j q -> p (j q)"),
                           start=True, stop=True)
                x.then_inc(sem("ssd_added"), 1)

            def ssd_inter(g, d):
                pe.wait_ge(sem("states_kept"), g + 1)
                for t in range(1, NT):
                    for i in range(2):
                        x = mm(B[4 + i][:, t * P:(t + 1) * P], flat(st[:, t - 1, 2 * i:2 * i + 2]),
                               conv[:, d, 3, t * P:(t + 1) * P], start=True, stop=True)
                x.then_inc(sem("y_inter"), 1)

            def ssd_norm(g):
                pe.wait_ge(sem("ysq_ready"), g + 1)
                for j, cols in enumerate((slice(0, LO), slice(LO, T))):
                    x = mm(B[4 + j][:, 0:cols.stop - cols.start], ones, ysq[:, 0, cols], start=True, stop=True)
                x.then_inc(sem("ysq_summed"), 1)

            def ssd_mix(g, d, project, products=2 * DC):
                if not isinstance(g, int) or g > 0:
                    pe.wait_ge(sem("y_read"), g)
                ssd_tokens(g, d)
                project(0)
                sample_outer(g, 0)
                ssd_cb(g, d)
                project(1)
                sample_outer(g, 1)
                ssd_spread(g, d, (2, 3))
                project(2)
                ssd_spread(g, d, (0, 1))
                project(3, sample_y(g, d, products))
                ssd_intra(g)
                project(4)
                ssd_inter(g, d)
                project(5)
                ssd_norm(g)

            ssd_project(0, 0, ready=normed(2))
            n = T_DT
            bank_free(n)
            for t in range(NT + 1):
                cols = slice(t * P, (t + 1) * P) if t < NT else slice(TP, T)
                out = B[2 * (n % 2)][0:cols.stop - cols.start, t * CH_ALL:(t + 1) * CH_ALL]
                for k in range(DC):
                    x = mm(out, hn[:, k, cols], wdt[:, k, :], start=k == 0, stop=k == DC - 1)
            x.then_inc(sem("dt_summed"), 1)
            for j in range(1, SSD_UNITS):
                ssd_project(0, j)
            ssd_mix(0, 0, lambda j, between=None: ssd_project(1, j, between))
            with pe.Fori(0, (CG - 2) // 2) as i:
                ssd_mix(i * 2 + 1, 1, lambda j, between=None: ssd_project(i * 2 + 2, j, between))
                ssd_mix(i * 2 + 2, 0, lambda j, between=None: ssd_project(i * 2 + 3, j, between))

            def out_ahead(j, part, between=None):
                n, w = T_OUT1 + j, 2 * j + part
                if part == 0:
                    bank_free(n)
                else:
                    pe.wait_ge(sem("yout_ready"), CG - 1)
                pe.wait_ge(ring_in[w], 16 * (U_SSD // RING + (CG if w < SSD_UNITS else 0) + 1))
                blocks = range(DC if part == 0 else DC - 2)
                for cols, bank in MATMULS:
                    for k in blocks:
                        x = mm(bank(n), ring[:, w, k], yout[:, part * DC + k, cols], start=part == 0 and k == 0,
                               stop=part == 1 and k == DC - 3, skip_group_check=True)
                        m = k + len(blocks) * (cols.start > 0)
                        if between is not None and m < 2 * len(blocks) - 1:
                            between(m)
                if w == 0:
                    x.then_inc(units_multiplied, 1)
                elif part == 1:
                    x.then_inc(sem("parts_multiplied"), 1)

            def last_project(step, between=None):
                for j, part in (((0, 0),), ((1, 0),), ((0, 1),), ((1, 1),), ((2, 0),), ((2, 1), (3, 0)))[step]:
                    out_ahead(j, part, between)

            ssd_mix(CG - 1, 1, last_project, 2 * (DC - 2))
            out_ahead(3, 1)
            pe.wait_ge(sem("yout_ready"), CG)
            for j in range(AHEAD):
                n = T_OUT1 + AHEAD + j
                bank_free(n)
                for cols, bank in MATMULS:
                    for k in (DC - 2, DC - 1):
                        x = mm(bank(n), ring[:, 2 * j + 1, k], yout[:, DC + k, cols], start=k == DC - 2,
                               stop=k == DC - 1)
                x.then_inc(units_multiplied, 2 if j < AHEAD - 1 else 1)
            for j in range(AHEAD, DC):
                n = T_OUT1 + AHEAD + j
                bank_free(n)
                for part in range(CI // D):
                    w = U_OUT1 + 2 * j + part
                    s = (2 * j + part) % RING
                    load = U_SSD // RING + (CG if s < SSD_UNITS else 0)
                    unit(w, n, s, load + (2 * j + part) // RING + 1, yout, first=part * DC, start=part == 0,
                         last=part == 1)
            mlp(1, 3, T_UP1, T_DOWN1, U_UP1,
                [U_SSD // RING + (CG if s < SSD_UNITS else 0) + (U_UP1 - U_OUT1) // RING for s in range(RING)])
            norm(4)

        @block.scalar
        def _(act):
            run = nc.scalar.activation
            tally = Tally(act)
            step = sem("act_step")
            for name in NORM_CONSTS:
                act.dma_start(const_tiles[name][:], A["consts"][name]).then_inc(norm_consts_in, 16)

            def norm(r, t_written):
                for k in range(DC):
                    if r == 0:
                        act.wait_ge(x_in[k // 2], 16)
                    else:
                        act.wait_ge(copied[(t_written + k) % 2], turns_before(t_written + k) + 1)
                    run(hn[:, k], h[:, k], ACT.Square).then_inc(squares, 1)
                if r == 0:
                    act.wait_ge(norm_consts_in, 16 * len(NORM_CONSTS))
                tally.done(run(std[:, 0:1], eps[:, 0:1], ACT.Sqrt), step)
                act.wait_ge(norm_summed, 2 * r + 1)
                run(std[:, 0:LO], B[4][:, 0:LO], ACT.Sqrt, bias=eps[:, 0:1], scale=1.0 / D).then_inc(std_ready, 1)
                act.wait_ge(norm_summed, 2 * r + 2)
                run(std[:, LO:T], B[5][:, 0:HI], ACT.Sqrt, bias=eps[:, 0:1], scale=1.0 / D).then_inc(std_ready, 1)

            def copy_turn(n, dst, units=None, scale=1.0):
                if units is not None:
                    act.wait_ge(units_multiplied, units)
                run(dst[:, 0:LO], lo(n), ACT.Copy, scale=scale).then_inc(step, 1)
                run(dst[:, LO:T], hi(n), ACT.Copy, scale=scale).then_inc(copied[n % 2], 1)
                tally.total[id(step)] = tally.total.get(id(step), 0) + 1

            norm(0, None)
            at = [0]

            def copy_next():
                w = at[0]
                if w >= U_OUT0:
                    return
                at[0] += 1
                if w < U_GLA:
                    n, hp, i = T_ATT + w, w // 3, w % 3
                    if hp:
                        if i < 2:
                            act.wait_ge(sem("rotated"), 2 * hp)
                            act.wait_ge(sem("rope_done"), 2 * hp)
                        else:
                            act.wait_ge(sem("v_turned"), hp)
                            act.wait_ge(sem("v_written"), 16 * hp)
                    copy_turn(n, (qraw, kraw, vraw)[i], w + 1, SCALE if i == 0 else 1.0)
                    return
                n, gp, i = T_GLA + w - U_GLA, (w - U_GLA) // 6, (w - U_GLA) % 6
                if w == U_GLA:
                    act.wait_ge(sem("glow_summed"), 1)
                    run(glow[:, 0:LO], lo(T_GATE)[0:RANK], ACT.Copy).then_inc(step, 1)
                    tally.total[id(step)] += 1
                    run(glow[:, LO:T], hi(T_GATE)[0:RANK], ACT.Copy).then_inc(copied[T_GATE % 2], 1)
                if i < 4:
                    copy_turn(n, (qg[:, gp], kg[:, gp], vg[:, 2 * gp], vg[:, 2 * gp + 1])[i], w + 1,
                              BK ** -0.5 if i == 0 else 1.0)
                else:
                    act.wait_ge(units_multiplied, w + 1)
                    run(rg[:, 2 * gp + i - 4, 0:LO], lo(n), ACT.Tanh, scale=0.5).then_inc(step, 1)
                    tally.total[id(step)] += 1
                    run(rg[:, 2 * gp + i - 4, LO:T], hi(n), ACT.Tanh, scale=0.5).then_inc(sem("r_tanh"), 1)

            def exps(hd):
                for i, j in enumerate(ORDERS[hd % 2]):
                    act.wait_ge(sem("masked"), hd * NT + i + 1)
                    run(probs[:, j, 0:(j + 1) * P], probs[:, j, 0:(j + 1) * P], ACT.Exp, bias=pstat[:, 1, j:j + 1],
                        accum_out=pstat[:, 2, j:j + 1]).then_inc(sem("expd"), 1)

            def pt_copies(hd):
                if hd:
                    act.wait_ge(sem("pv_done"), hd * NT)
                for i, (bank, at, end) in enumerate(PT_COPIES):
                    act.wait_ge(sem("p_turned"), hd * len(PT_COPIES) + i + 1)
                    run(pt[:, at:end], B[bank][:, 0:end - at], ACT.Copy).then_inc(sem("pt_copied"), 1)

            for _ in range(3):
                copy_next()
            for hp in range(HP):
                copy_next()
                exps(2 * hp)
                copy_next()
                pt_copies(2 * hp)
                exps(2 * hp + 1)
                copy_next()
                pt_copies(2 * hp + 1)

            def gate_exp(gp):
                act.wait_ge(sem("gate_folded"), gp + 1)
                run(gt[:, 1, :], gt[:, 1, :], ACT.Exp).then_inc(sem("gate_expd"), 1)

            def gate_tokens(gp):
                act.wait_ge(sem("loga_turned"), gp + 1)
                run(flat(latok), B[6][:], ACT.Copy).then_inc(sem("latok_ready"), 1)

            def gate_decays(gp):
                act.wait_ge(sem("sums_copied"), gp + 1)
                tally.done(run(flat(eb[:, gp]), flat(bT), ACT.Exp), step)
                tally.done(run(flat(enb[:, gp]), flat(bT), ACT.Exp, scale=-1.0), step)
                tally.done(run(sdec[:, gp], loga[:, gp, TP:T], ACT.Exp), step)
                act.wait_ge(sem("gate_left"), gp + 1)
                run(flat(ee[:, gp]), flat(ee[:, gp]), ACT.Exp).then_inc(sem("decays_ready"), 1)

            gate_exp(0)
            for b in range(1, NB, 2):
                copy_next()
            copy_next()
            act.wait_ge(sem("sample_max"), 1)
            tally.done(run(flat(sexp[:]), B[6][0:NB * AH, 0:NBR * P], ACT.Exp, bias=sst[:, 2:3],
                           accum_out=sst[:, 3:4]), step)
            run(sst[:, 4:5], sst[:, 1:2], ACT.Exp, bias=sst[:, 2:3]).then_inc(sem("sample_expd"), 1)
            gate_exp(1)
            gate_tokens(0)
            copy_next()
            gate_decays(0)
            gate_tokens(1)
            copy_next()
            gate_decays(1)

            def gla(gp):
                act.wait_ge(sem("gla_turned"), gp + 1)
                tally.done(run(flat(ketok), B[6][:], ACT.Copy), step)
                run(flat(gvtok[:, 0]), B[7][:], ACT.Copy).then_inc(sem("gla_tok_act"), 1)
                copy_next()
                copy_next()
                act.wait_ge(sem("gla_sample_kv"), gp + 1)
                for e in range(2):
                    run(gt[:, 4 + e, 0:TP], B[6 + e][:], ACT.Copy).then_inc(sem("gla_o_copied"), 1)
                copy_next()
                act.wait_ge(sem("gla_sample_out"), gp + 1)
                for e in range(2):
                    tally.done(run(gt[:, 4 + e, TP:T], B[4 + e][:, 0:NB], ACT.Copy), step)
                act.wait_ge(sem("gla_o_copied"), 2 * gp + 2)
                for e in range(2):
                    run(gt[:, 2 + e, :], gt[:, 4 + e, :], ACT.Square).then_inc(sem("gla_squares"), 1)
                copy_next()
                act.wait_ge(sem("gla_squares_summed"), gp + 1)
                for e in range(2):
                    tally.done(run(gt[:, 2 + e, 0:LO], B[4 + 2 * e][:, 0:LO], ACT.Sqrt, bias=eps[:, 0:1],
                                   scale=1.0 / BV), step)
                    run(gt[:, 2 + e, LO:T], B[5 + 2 * e][:, 0:HI], ACT.Sqrt, bias=eps[:, 0:1],
                        scale=1.0 / BV).then_inc(sem("gla_std"), 1)

            for gp in range(GP):
                gla(gp)

            def mlp_squares(t_up):
                with act.Fori(0, FC // RING) as i:
                    for s in range(RING):
                        act.wait_ge(copied[(t_up + s) % 2], i * (RING // 2) + (turns_before(t_up + s) + 1))
                        run(hid[:, i * RING + s], hid[:, i * RING + s], ACT.Square).then_inc(hidden, 1)

            norm(1, T_OUT0B)
            mlp_squares(T_UP0)

            norm(2, T_DOWN0)
            act.wait_ge(sem("dt_folded"), 1)
            tally.done(run(nega[:], nega[:], ACT.Exp), step)
            run(flat(dts[:, 2]), flat(dts[:, 1]), ACT.Exp).then_inc(sem("dt_expd"), 1)

            ct = Tally(act)
            cstep, mstep = sem("act_conv_step"), sem("act_ssd_step")

            def conv_in(g, j):
                n = T_SSD + j
                act.wait_ge(units_multiplied, g * SSD_UNITS + (U_SSD + j + 1))
                if not (isinstance(g, int) and g == 0):
                    act.wait_ge(sem("conv_ready"), g)
                else:
                    act.wait_ge(sem("pads_ready"), 1)
                run(xe[:, j, 3:3 + LO], lo(n), ACT.Copy).then_inc(cstep, 1)
                run(xe[:, j, 3 + LO:3 + TP], hi(n)[:, 0:LO], ACT.Copy).then_inc(cstep, 1)
                run(xs[:, j, 3, :], hi(n)[:, LO:HI], ACT.Copy).then_inc(copied[n % 2], 1)

            def conv_tanh(g, d, j):
                act.wait_ge(sem("taps_done"), g * 4 + (j + 1))
                if not (isinstance(g, int) and g == 0 and j < 2):
                    act.wait_ge(sem("tanh_used"), g * 4 + (j - 1))
                run(th[:, j % 2, 0:TP], conv[:, d, j, 0:TP], ACT.Tanh).then_inc(sem("conv_tanh"), 1)

            def conv_tanh_samples(g, d):
                act.wait_ge(sem("sample_taps_done"), g + 1)
                run(ths[:], conv[:, d, :, TP:T], ACT.Tanh).then_inc(sem("sample_conv_tanh"), 1)

            def gate(g, d, i):
                n = T_SSD + 4 + i
                act.wait_ge(units_multiplied, g * SSD_UNITS + (U_SSD + 4 + i + 1))
                run(gz[:, d, i, 0:LO], lo(n), ACT.Tanh, scale=0.5).then_inc(cstep, 1)
                run(gz[:, d, i, LO:T], hi(n), ACT.Tanh, scale=0.5).then_inc(sem("z_tanh"), 1)

            def mix(g, d, nxt):
                act.wait_ge(sem("ssd_turned"), g + 1)
                if not (isinstance(g, int) and g == 0):
                    act.wait_ge(sem("ssm_decayed"), g * 2)
                    act.wait_ge(sem("states_kept"), g)
                    act.wait_ge(sem("y_scaled"), g)
                act.wait_ge(sem("ssamp_read"), g + 1)
                run(flat(sadec[:]), B[7][:, 416:448], ACT.Exp).then_inc(sem("sadec_ready"), 1)
                run(flat(btok[:]), B[6][:], ACT.Copy).then_inc(sem("btok_ready"), 1)
                act.wait_ge(sem("cum_left"), g + 1)
                run(flat(dec[:]), flat(cum[:, 1]), ACT.Exp).then_inc(mstep, 1)
                run(flat(toend[:]), flat(toend[:]), ACT.Exp).then_inc(sem("decay_exps"), 1)
                if nxt is not None:
                    conv_in(nxt, 0)
                    conv_tanh(nxt, 1 - d, 0)
                    conv_in(nxt, 1)
                    conv_tanh(nxt, 1 - d, 1)
                for i, j in enumerate((2, 3, 0, 1)):
                    act.wait_ge(sem("decays_read"), g * 4 + (i + 1))
                    rows = slice(CHD * (j % 2), CHD * (j % 2) + CHD)
                    run(efeat[rows, j // 2, :], B[4 + j][rows, P:TP], ACT.Exp).then_inc(sem("decays_featured"), 1)
                    run(flat(seg[:, j]), flat(seg[:, j]), ACT.Exp).then_inc(sem("seg_expd"), 1)
                    if i == 1 and nxt is not None:
                        conv_in(nxt, 2)
                        conv_tanh(nxt, 1 - d, 2)
                if nxt is not None:
                    conv_in(nxt, 3)
                    conv_tanh(nxt, 1 - d, 3)
                    conv_tanh_samples(nxt, 1 - d)
                    gate(nxt, 1 - d, 0)
                act.wait_ge(sem("y_gated"), g + 1)
                run(ysq[:, 0], yT[:, 0], ACT.Square).then_inc(mstep, 1)
                run(ysq[:, 1], yT[:, 1], ACT.Square).then_inc(sem("y_squared"), 1)
                if nxt is not None:
                    gate(nxt, 1 - d, 1)
                run(root[:], eps[:, 0:1], ACT.Sqrt).then_inc(mstep, 1)
                act.wait_ge(sem("ysq_summed"), g + 1)
                run(ystd[:, 0:LO], B[4][:, 0:LO], ACT.Sqrt, bias=eps[:, 0:1], scale=1.0 / GW).then_inc(
                    sem("y_std_low"), 1)
                run(ystd[:, LO:T], B[5][:, 0:HI], ACT.Sqrt, bias=eps[:, 0:1], scale=1.0 / GW).then_inc(
                    sem("y_std"), 1)

            conv_in(0, 0)
            for j in range(4):
                if j:
                    conv_in(0, j)
                conv_tanh(0, 0, j)
            conv_tanh_samples(0, 0)
            gate(0, 0, 0)
            gate(0, 0, 1)
            mix(0, 0, 1)
            with act.Fori(0, (CG - 2) // 2) as i:
                mix(i * 2 + 1, 1, i * 2 + 2)
                mix(i * 2 + 2, 0, i * 2 + 3)
            mix(CG - 1, 1, None)
            norm(3, T_OUT1 + AHEAD)
            mlp_squares(T_UP1)
            norm(4, T_DOWN1)

        @block.vector
        def _(dve):
            V = nc.vector
            tally = Tally(dve)
            step = sem("vec_step")
            do = lambda ins, name=None: tally.done(ins, step if name is None else sem(name))

            def add_square(r, k):
                dve.wait_ge(squares, k + (r * DC + 1))
                if not (r == 0 and isinstance(k, int) and k == 0):
                    dve.wait_ge(squares_added, k + r * DC)
                V.tensor_tensor(rstd[:], rstd[:], hn[:, k], ALU.add).then_inc(squares_added, 1)

            def add_and_weigh(r, k):
                add_square(r, k)
                dve.wait_ge(squares_added, k + (r * DC + 1))
                V.tensor_scalar(hn[:, k], h[:, k], norms[:, r, k], None, ALU.mult).then_inc(hn_ready, 1)

            def root(r, cols):
                dve.wait_ge(std_ready, 2 * r + (1 if cols.start == 0 else 2))
                do(V.reciprocal(rstd[:, cols], std[:, cols]), "last_root" if r == 4 else None)

            def norm(r):
                for cols, _ in MATMULS:
                    root(r, cols)
                    for k in range(DC):
                        V.scalar_tensor_tensor(hn[:, k, cols], h[:, k, cols], norms[:, r, k], rstd[:, cols],
                                               ALU.mult, ALU.mult).then_inc(hn_ready, 1)

            def log1p_tail(e, s, s2, p, den):
                do(V.tensor_scalar(den, e, 2.0, None, ALU.add))
                do(V.reciprocal(den, den))
                do(V.tensor_tensor(s, e, den, ALU.mult))
                do(V.tensor_tensor(s2, s, s, ALU.mult))
                do(V.tensor_scalar(p, s2, LOG1P[0], None, ALU.mult))
                for coefficient in LOG1P[1:]:
                    do(V.scalar_tensor_tensor(p, p, coefficient, s2, ALU.add, ALU.mult))
                do(V.scalar_tensor_tensor(p, p, 1.0, s, ALU.add, ALU.mult))

            do(V.memset(rstd[:], 0.0))
            for k in range(DC):
                add_square(0, k)
            dve.wait_ge(norm_consts_in, 16 * len(NORM_CONSTS))
            for i in range(DC // 2):
                dve.wait_ge(x_in[i], 16)
            norm(0)
            at = [3]

            def next_gate():
                w = at[0]
                if w >= U_OUT0:
                    return
                at[0] += 1
                i = (w - U_GLA) % 6
                if w < U_GLA or i < 4:
                    return
                n, tile = T_GLA + w - U_GLA, (w - U_GLA) // 6 * 2 + i - 4
                dve.wait_ge(sem("r_tanh"), tile + 1)
                V.scalar_tensor_tensor(rg[:, tile, 0:LO], rg[:, tile, 0:LO], 1.0, lo(n), ALU.add,
                                       ALU.mult).then_inc(sem("r_gated"), 1)
                V.scalar_tensor_tensor(rg[:, tile, LO:T], rg[:, tile, LO:T], 1.0, hi(n), ALU.add,
                                       ALU.mult).then_inc(copied[n % 2], 1)

            def rope(hp):
                if hp:
                    dve.wait_ge(sem("k_written"), 16 * hp)
                for i, (raw, out) in enumerate(((qraw, qr), (kraw, kr))):
                    dve.wait_ge(sem("rotated"), 2 * hp + i + 1)
                    V.tensor_tensor(rt[:, 0, 0:LO], B[4 + 2 * i][:, 0:LO], sin[:, 0:LO], ALU.mult).then_inc(
                        sem("rope_part"), 1)
                    V.tensor_tensor(rt[:, 0, LO:T], B[5 + 2 * i][:, 0:HI], sin[:, LO:T], ALU.mult).then_inc(
                        sem("rope_part"), 1)
                    do(V.tensor_tensor(rt[:, 1], raw[:], cos[:], ALU.mult))
                    do(V.tensor_tensor(out[:], rt[:, 0], rt[:, 1], ALU.add), "rope_done")

            def tokens(hp):
                dve.wait_ge(sem("v_turned"), hp + 1)
                if hp:
                    dve.wait_ge(sem("pv_done"), 2 * hp * NT)
                do(V.tensor_copy(flat(vtok[:]), B[4][:]))
                do(V.tensor_copy(samp[:, :, hp * P:(hp + 1) * P],
                                 B[5][0:NB, 0:3 * P].rearrange("b (i d) -> b i d", i=3)), "samp_ready")

            def mask(hd):
                if hd:
                    dve.wait_ge(sem("p_turned"), hd * len(PT_COPIES))
                for i, j in enumerate(ORDERS[hd % 2]):
                    w = (j + 1) * P
                    dve.wait_ge(sem("scored"), hd * NT + i + 1)
                    do(V.tensor_tensor_reduce(probs[:, j, 0:w], B[4 + j][:, 0:w], lncount[:, TP - w:TP], 1.0,
                                              LEAST, ALU.add, ALU.max, pstat[:, 0, j:j + 1]))
                    do(V.tensor_scalar(pstat[:, 1, j:j + 1], pstat[:, 0, j:j + 1], -1.0, None, ALU.mult), "masked")

            def normalise(hd):
                for i, j in enumerate(ORDERS[hd % 2]):
                    dve.wait_ge(sem("expd"), hd * NT + i + 1)
                    do(V.reciprocal(pstat[:, 3, j:j + 1], pstat[:, 2, j:j + 1]))
                    do(V.tensor_scalar(probs[:, j, 0:(j + 1) * P], probs[:, j, 0:(j + 1) * P],
                                       pstat[:, 3, j:j + 1], None, ALU.mult), "p_ready")

            def take_out(hp, e):
                dve.wait_ge(sem("pv_done"), (2 * hp + e + 1) * NT)
                rows = slice(AD * e, AD * e + AD)
                do(V.tensor_copy(mixT[rows, hp, 0:TP], B[7][rows, :]), "o_copied")

            dve.wait_ge(consts_in, 16 * len(FIRST_CONSTS))
            for hp in range(HP):
                rope(hp)
                next_gate()
                tokens(hp)
                mask(2 * hp)
                normalise(2 * hp)
                next_gate()
                take_out(hp, 0)
                mask(2 * hp + 1)
                normalise(2 * hp + 1)
                next_gate()
                take_out(hp, 1)

            def fold_gate(gp):
                dve.wait_ge(sem("gate_logits"), gp + 1)
                x, e = gt[:, 0], gt[:, 1]
                do(V.tensor_scalar(x[:, 0:LO], B[6][:, 0:LO], bgate[:, gp:gp + 1], None, ALU.add))
                do(V.tensor_scalar(x[:, LO:T], B[7][:, 0:HI], bgate[:, gp:gp + 1], None, ALU.add))
                do(V.scalar_tensor_tensor(e, x, -1.0, x, ALU.mult, ALU.min), "gate_folded")

            def log_gate(gp):
                x, e, s, s2, p, t = (gt[:, i] for i in range(6))
                dve.wait_ge(sem("gate_expd"), gp + 1)
                log1p_tail(e, s, s2, p, t)
                do(V.tensor_scalar(x, x, 0.0, 1.0 / TAU, ALU.min, ALU.mult))
                do(V.scalar_tensor_tensor(loga[:, gp], p, -2.0 / TAU, x, ALU.mult, ALU.add), "loga_ready")

            def gate_decays(gp):
                dve.wait_ge(sem("gates_summed"), gp + 1)
                if gp:
                    dve.wait_ge(sem("decays_ready"), gp)
                do(V.tensor_copy(flat(bT), B[7][:]), "sums_copied")
                do(V.tensor_tensor(ee[:, gp], bT[:, :, CH - 1:CH].to_broadcast((P, NCH, CH)), bT, ALU.subtract),
                   "gate_left")

            dve.wait_ge(late_consts_in, 16 * len(LATE_CONSTS))
            for b in range(NB):
                dve.wait_ge(sem("sample_q_spread"), b + 1)
                dve.wait_ge(sem(f"gathered{b % SLOTS}"), 16 * NBR * (b // SLOTS + 1))
                do(V.tensor_tensor(gprod[:], gath[:, b % SLOTS], B[4 + b % 2][:].unsqueeze(1).to_broadcast((P, NBR, AW)),
                                   ALU.mult))
                do(V.tensor_reduce(s3[:, :, b * AH:(b + 1) * AH],
                                   gprod[:].rearrange("p i (k d) -> p i k d", k=AH), AX, ALU.add), "keys_scored")
                if b == 1:
                    dve.wait_ge(sem("v_written"), 16 * HP)
                    dve.wait_ge(sem("k_written"), 16 * HP)
                    do(V.memset(att[:], 0.0))
                    fold_gate(0)
                if b in (2, 4, 6, 7):
                    next_gate()
            dve.wait_ge(sem("sample_rows_ready"), 1)
            do(V.tensor_tensor(krep, B[5][0:NB * AH, :], ownhead[:], ALU.mult))
            do(V.tensor_copy(vrep, B[7][0:NB * AH, :]))
            do(V.tensor_tensor_reduce(kscr, B[4][0:NB * AH, :], krep, 1.0, 0.0, ALU.mult, ALU.add,
                                      sst[:, 1:2]))
            do(V.tensor_reduce(sst[:, 0:1], B[6][0:NB * AH, 0:NBR * P], AX, ALU.max))
            do(V.tensor_tensor(sst[:, 0:1], sst[:, 0:1], sst[:, 1:2], ALU.max))
            do(V.tensor_scalar(sst[:, 2:3], sst[:, 0:1], -1.0, None, ALU.mult), "sample_max")
            next_gate()
            dve.wait_ge(sem("sample_expd"), 1)
            do(V.scalar_tensor_tensor(sst[:, 5:6], sst[:, 4:5], float(NBR), sst[:, 3:4], ALU.mult, ALU.add))
            do(V.reciprocal(sst[:, 6:7], sst[:, 5:6]))
            do(V.scalar_tensor_tensor(sst[:, 7:8], sst[:, 4:5], float(NBR), sst[:, 6:7], ALU.mult, ALU.mult))
            do(V.tensor_scalar(sdiag[:], ident[0:NB * AH, 0:NB * AH], sst[:, 7:8], None, ALU.mult))
            do(V.tensor_scalar(flat(sexp[:]), flat(sexp[:]), sst[:, 6:7], None, ALU.mult), "sample_probs")
            dve.wait_ge(sem("sample_probs_turned"), 1)
            do(V.tensor_copy(flat(spt[:]), B[4][:, 0:NBR * NB * AH]), "spt_copied")
            log_gate(0)
            fold_gate(1)
            log_gate(1)
            dve.wait_ge(sem("sample_mixed"), 1)
            mixed = B[5][:, 0:HP * NB * 2].rearrange("p (a b e) -> p a b e", a=HP, b=NB)
            for e in range(2):
                rows = slice(AD * e, AD * e + AD)
                do(V.tensor_copy(mixT[rows, 0:HP, TP:T], mixed[rows, :, :, e]), "sample_out")

            def scaled(gp):
                for i in range(2):
                    n = T_GLA + 6 * gp + i
                    dve.wait_ge(copied[n % 2], turns_before(n) + 1)
                if gp:
                    dve.wait_ge(sem("gla_out"), gp)
                dve.wait_ge(sem("decays_ready"), gp + 1)
                do(V.tensor_tensor(gt[:, 0, 0:TP], qg[:, gp, 0:TP], flat(eb[:, gp]), ALU.mult))
                do(V.tensor_tensor(gt[:, 1, 0:TP], kg[:, gp, 0:TP], flat(enb[:, gp]), ALU.mult))
                do(V.tensor_tensor(flat(ee[:, gp]), kg[:, gp, 0:TP], flat(ee[:, gp]), ALU.mult), "k_end_ready")

            def gla_tokens(gp):
                dve.wait_ge(sem("gla_turned"), gp + 1)
                do(V.tensor_copy(flat(gvtok[:, 1]), B[4][:]))
                do(V.tensor_copy(flat(gsamp[:]), B[5][0:NB, 0:3 * P]))
                dve.wait_ge(sem("gla_tok_act"), gp + 1)
                for e2 in range(2):
                    do(V.tensor_tensor(vdiag[:, e2], gsamp[:, 1 + e2].unsqueeze(1).to_broadcast((NB, NB, P)),
                                       delta[:].unsqueeze(2).to_broadcast((NB, NB, P)), ALU.mult),
                       "gla_tokens_ready" if e2 else None)

            def gla_states(gp):
                if gp:
                    dve.wait_ge(sem("gla_prompt_out"), 16 * gp)
                dve.wait_ge(sem("gla_att"), gp + 1)
                for e2 in range(2):
                    do(V.copy_predicated(att[:, e2], mask64[:].unsqueeze(1).to_broadcast((P, NT, P)), B[6 + e2][:].rearrange("p (t q) -> p t q", t=NT)),
                       "gla_masked" if e2 else None)
                dve.wait_ge(sem("gla_added"), gp + 1)
                for ch in range(NCH):
                    add = B[4 + ch % 2][:, (ch // 2) * P:(ch // 2 + 1) * P]
                    last = "gla_chained" if ch == NCH - 1 else None
                    if ch == 0:
                        do(V.tensor_copy(gst[:, 1], add))
                    else:
                        do(V.scalar_tensor_tensor(gst[:, ch + 1], gst[:, ch], eb[:, gp, ch, CH - 1:CH], add,
                                                  ALU.mult, ALU.add), last)

            def gla_step(gp):
                dve.wait_ge(sem("gla_sample_kv"), gp + 1)
                dve.wait_ge(sem("gla_state_in"), 16 * (gp + 1))
                for b in range(NB):
                    do(V.scalar_tensor_tensor(gs0[:, b], gs0[:, b], sdec[:, gp, b:b + 1],
                                              B[4 + b // 4][:, (b % 4) * P:(b % 4 + 1) * P], ALU.mult, ALU.add),
                       "gla_stepped" if b == NB - 1 else None)

            def gla_normed(gp, e2):
                hd = 2 * gp + e2
                dve.wait_ge(sem("gla_std"), hd + 1)
                do(V.reciprocal(gt[:, 2 + e2], gt[:, 2 + e2]))
                do(V.scalar_tensor_tensor(gt[:, 4 + e2], gt[:, 4 + e2], wonorm[:, 0:1], gt[:, 2 + e2],
                                          ALU.mult, ALU.mult))
                n = T_GLA + 6 * gp + 4 + e2
                dve.wait_ge(copied[n % 2], turns_before(n) + 1)
                do(V.scalar_tensor_tensor(mixT[:, HP + hd], gt[:, 4 + e2], 0.5, rg[:, hd], ALU.mult,
                                          ALU.mult), "gla_mixed")

            def residual(n, block_of_h, units, done=units_multiplied):
                dve.wait_ge(done, units)
                V.tensor_tensor(h[:, block_of_h, 0:LO], h[:, block_of_h, 0:LO], lo(n), ALU.add).then_inc(
                    sem("h_low"), 1)
                V.tensor_tensor(h[:, block_of_h, LO:T], h[:, block_of_h, LO:T], hi(n), ALU.add).then_inc(
                    copied[n % 2], 1)

            def mlp(r, t_up, t_down, u_up, u_down):
                for cols, _ in MATMULS:
                    root(r, cols)
                with dve.Fori(0, FC // RING) as i:
                    for s in range(RING):
                        dve.wait_ge(units_multiplied, i * RING + (u_up + s + 1))
                        V.scalar_tensor_tensor(hid[:, i * RING + s, 0:LO], lo(t_up + s), 0.0, rstd[:, 0:LO],
                                               ALU.max, ALU.mult).then_inc(sem("relu_low"), 1)
                        V.scalar_tensor_tensor(hid[:, i * RING + s, LO:T], hi(t_up + s), 0.0, rstd[:, LO:T],
                                               ALU.max, ALU.mult).then_inc(copied[(t_up + s) % 2], 1)
                for n in (t_up + FC - 2, t_up + FC - 1):
                    dve.wait_ge(copied[n % 2], turns_before(n) + 1)
                do(V.memset(rstd[:], 0.0))
                with dve.Fori(0, DC // 2) as i:
                    for s in range(2):
                        residual(t_down + s, i * 2 + s, i * RING + (u_down + (s + 1) * (FF // D)))
                        (add_and_weigh if r + 1 in LATE_ROOT else add_square)(r + 1, i * 2 + s)

            def halves(*blocks):
                for j in blocks:
                    residual(T_OUT0 + j, j, j + 1, sem("parts_multiplied"))

            next_gate()
            gate_decays(0)
            scaled(0)
            next_gate()
            gate_decays(1)
            gla_tokens(0)
            next_gate()
            gla_states(0)
            next_gate()
            gla_step(0)
            scaled(1)
            halves(0)
            gla_normed(0, 0)
            halves(1)
            gla_tokens(1)
            gla_normed(0, 1)
            halves(2, 3)
            gla_states(1)
            halves(4)
            gla_step(1)
            halves(5, 6)
            gla_normed(1, 0)
            halves(7)
            gla_normed(1, 1)
            do(V.memset(rstd[:], 0.0))
            for j in range(DC):
                residual(T_OUT0B + j, j, U_OUT0 + j + 1)
                add_and_weigh(1, j)
            dve.wait_ge(sem("gla_prompt_out"), 16 * GP)
            dve.wait_ge(sem("gla_state_out"), 16 * GP)
            dve.wait_ge(sem("samp_written"), 32)
            mlp(1, T_UP0, T_DOWN0, U_UP0, U_DOWN0)

            norm(2)
            dve.wait_ge(sem("dt_summed"), 1)
            bank = B[2 * (T_DT % 2)]
            do(V.memset(dts[:, 0], 0.0))
            do(V.memset(xe[:, :, 0:TAPS - 1], 0.0), "pads_ready")
            do(V.tensor_tensor(dts[:, 0, 0:NT], bank[:, 0:NT * CH_ALL].rearrange("p (t k) -> p t k", t=NT),
                               dtb[:].unsqueeze(1).to_broadcast((P, NT, CH_ALL)), ALU.add))
            ins = V.tensor_tensor(dts[0:NB, 0, NT], bank[0:NB, NT * CH_ALL:(NT + 1) * CH_ALL], dtb[0:NB], ALU.add)
            ins.then_inc(copied[T_DT % 2], 1)
            dve.wait_ge(copied[T_DT % 2], turns_before(T_DT) + 1)
            f = lambda i: flat(dts[:, i])
            do(V.scalar_tensor_tensor(f(1), f(0), -1.0, f(0), ALU.mult, ALU.min), "dt_folded")
            dve.wait_ge(sem("dt_expd"), 1)
            log1p_tail(f(2), f(5), f(6), f(7), f(3))
            do(V.tensor_scalar(f(0), f(0), 0.0, None, ALU.max))
            do(V.scalar_tensor_tensor(f(0), f(7), 2.0, f(0), ALU.mult, ALU.add))
            do(V.scalar_tensor_tensor(dts[:, 1], dts[:, 0], -1.0,
                                      nega[:].unsqueeze(1).to_broadcast((P, NT + 1, CH_ALL)), ALU.mult, ALU.mult))

            steps_of = dts[:].rearrange("p i t (g j) -> p i t g j", g=CG)
            conv_tally, mix_tally = Tally(dve), Tally(dve)
            cstep, mstep = sem("vec_conv_step"), sem("vec_ssd_step")

            def cdo(ins, name=None):
                conv_tally.done(ins, cstep if name is None else sem(name))

            def mdo(ins, name=None):
                mix_tally.done(ins, mstep if name is None else sem(name))

            def prepare(g, d):
                conv_tally.start("conv", g)
                cdo(V.tensor_scalar(pg[:, d, 0:20], parm[:, g, 0:20], 0.5, None, ALU.mult))
                cdo(V.tensor_copy(pg[:, d, 20:24], parm[:, g, 20:24]))
                cdo(V.tensor_copy(xs[:, :, 0:3, :], parm[:, g, 24:120].rearrange("p (c t b) -> p c t b", c=4, t=3)))
                cdo(V.tensor_copy(dtg[:, d], steps_of[:, 0, :, g]))
                cdo(V.tensor_copy(dag[:, d], steps_of[:, 1, :, g]))
                cdo(V.tensor_tensor(sadg[:, d], dag[0:NB, d, NT].unsqueeze(1).to_broadcast((NB, NB, CJ)),
                                    deltac[:].unsqueeze(2).to_broadcast((NB, NB, CJ)), ALU.mult))

            def taps(g, d, j):
                n = T_SSD + j
                dve.wait_ge(copied[n % 2], g * (SSD_UNITS // 2) + (turns_before(n) + 1))
                out = conv[:, d, j, 0:TP]
                cdo(V.tensor_scalar(out, xe[:, j, 0:TP], pg[:, d, 4 * j:4 * j + 1], pg[:, d, 16 + j:17 + j],
                                    ALU.mult, ALU.add))
                for tap in range(1, TAPS):
                    cdo(V.scalar_tensor_tensor(out, xe[:, j, tap:tap + TP], pg[:, d, 4 * j + tap:4 * j + tap + 1],
                                               out, ALU.mult, ALU.add), "taps_done" if tap == TAPS - 1 else None)

            def finish(g, d, j):
                dve.wait_ge(sem("conv_tanh"), g * 4 + (j + 1))
                cdo(V.scalar_tensor_tensor(conv[:, d, j, 0:TP], th[:, j % 2, 0:TP], 1.0, conv[:, d, j, 0:TP],
                                           ALU.add, ALU.mult), "tanh_used")

            def sample_taps(g, d):
                w = pg[:, d, 0:16].rearrange("p (c t) -> p c t", c=4).unsqueeze(3).to_broadcast((P, 4, TAPS, NB))
                cdo(V.tensor_tensor(xsp[:], xs[:], w, ALU.mult))
                cdo(V.tensor_reduce(conv[:, d, :, TP:T], xsp[:].rearrange("p c t b -> p c b t"), AX, ALU.add))
                cdo(V.tensor_tensor(conv[:, d, :, TP:T], conv[:, d, :, TP:T],
                                    pg[:, d, 16:20].unsqueeze(2).to_broadcast((P, 4, NB)), ALU.add),
                    "sample_taps_done")
                cdo(V.tensor_copy(pconv[:, g], xe[:, :, TP:TP + 3]), "conv_kept")
                cdo(V.tensor_copy(sconv[:, g], xs[:, :, 1:4, :]), "conv_kept")

            def finish_samples(g, d):
                dve.wait_ge(sem("sample_conv_tanh"), g + 1)
                cdo(V.scalar_tensor_tensor(conv[:, d, :, TP:T], ths[:], 1.0, conv[:, d, :, TP:T], ALU.add,
                                           ALU.mult), "conv_ready")
                conv_tally.end()

            def gate(g, d, i):
                n = T_SSD + 4 + i
                dve.wait_ge(sem("z_tanh"), g * 2 + (i + 1))
                V.scalar_tensor_tensor(gz[:, d, i, 0:LO], gz[:, d, i, 0:LO], 1.0, lo(n), ALU.add,
                                       ALU.mult).then_inc(sem("z_low"), 1)
                V.scalar_tensor_tensor(gz[:, d, i, LO:T], gz[:, d, i, LO:T], 1.0, hi(n), ALU.add,
                                       ALU.mult).then_inc(copied[n % 2], 1)

            def normed(g, d):
                dve.wait_ge(sem("y_std"), g + 1)
                norm_tally.start("normed", g)
                norm_tally.done(V.reciprocal(yrstd[:], ystd[:]), nstep)
                for i in range(2):
                    norm_tally.done(V.scalar_tensor_tensor(yout[:, g * 2 + i], yT[:, i], pg[:, d, 22 + i:23 + i],
                                                           yrstd[:], ALU.mult, ALU.mult),
                                    sem("yout_ready") if i else nstep)
                norm_tally.end()

            norm_tally, nstep = Tally(dve), sem("vec_norm_step")
            norm_tally.per["normed"] = {id(nstep): 2, id(sem("yout_ready")): 1}

            def pair(i):
                return B[i][:].rearrange("p (t j q) -> p t j q", t=2, j=CJ)

            def ahead(j):
                residual(T_OUT1 + j, j, DC + j + 1, sem("parts_multiplied"))

            def mix(g, d, nxt, prev):
                mix_tally.start("mix", g)
                dve.wait_ge(sem("ssd_turned"), g + 1)
                if prev is not None:
                    dve.wait_ge(sem("ssd_added"), g)
                    dve.wait_ge(sem("ssm_outer"), g * 2)
                mdo(V.tensor_copy(flat(cum[:]), B[7][:, 0:32]), "small_read")
                mdo(V.tensor_copy(flat(ssamp[:]), B[7][0:NB, 32:416]), "ssamp_read")
                mdo(V.tensor_tensor(toend[:], cum[:, 1], cum[:, 0], ALU.subtract), "cum_left")
                mdo(V.tensor_tensor(sxdt[:], ssamp[:, 0:2].rearrange("b i (j q) -> b (i j) q", j=2),
                                    dtg[0:NB, d, NT].unsqueeze(2).to_broadcast((NB, CJ, CHD)), ALU.mult),
                    "sxdt_ready")
                dve.wait_ge(sem("x_turned"), g + 1)
                for i in range(2):
                    mdo(V.tensor_tensor(xdt[:, 2 * i:2 * i + 2], pair(4 + i),
                                        dtg[:, d, 2 * i:2 * i + 2].unsqueeze(3).to_broadcast((P, 2, CJ, CHD)),
                                        ALU.mult), "xdt_ready" if i else None)
                if prev is not None:
                    normed(prev, 1 - d)
                def step_states(half):
                    dve.wait_ge(sem("ssm_outer"), g * 2 + (half + 1))
                    dve.wait_ge(sem("ssm_decayed"), g * 2 + (half + 1))
                    for j in range(2):
                        b = 4 * half + 2 * j
                        s = ss0[:, b:b + 2].rearrange("p b j q -> p (b j q)")
                        mdo(V.tensor_tensor(s, s, B[4 + j][:], ALU.add), "ssm_stepped" if j else None)

                def differences(j):
                    for t in range(NT):
                        mdo(V.tensor_scalar(seg[:, j, t], B[4 + j][:, t * P:(t + 1) * P], cum[:, 0, t, j:j + 1],
                                            0.0, ALU.subtract, ALU.min), "decays_read" if t == NT - 1 else None)

                step_states(0)
                for i in range(2):
                    mdo(V.tensor_scalar(yT[:, i], conv[:, d, i], pg[:, d, 20 + i:21 + i], None, ALU.mult))
                if nxt is not None:
                    prepare(nxt, 1 - d)
                    taps(nxt, 1 - d, 0)
                dve.wait_ge(sem("decay_exps"), g + 1)
                mdo(V.tensor_tensor(xde, xdt[:], toend[:].unsqueeze(3).to_broadcast((P, NT, CJ, CHD)),
                                    ALU.mult), "xde_ready")
                dve.wait_ge(sem("cb_ready"), g + 1)
                mdo(V.tensor_tensor(cbm[:], B[6][:].rearrange("p (t q) -> p t q", t=NT),
                                    tri[:].unsqueeze(1).to_broadcast((P, NT, P)), ALU.mult), "cbm_ready")
                if nxt is not None:
                    finish(nxt, 1 - d, 0)
                    taps(nxt, 1 - d, 1)
                step_states(1)
                for i, j in enumerate((2, 3)):
                    dve.wait_ge(sem("decays_spread"), g * 4 + (i + 1))
                    differences(j)
                if nxt is not None:
                    finish(nxt, 1 - d, 1)
                    taps(nxt, 1 - d, 2)
                for i, j in enumerate((0, 1)):
                    dve.wait_ge(sem("decays_spread"), g * 4 + (i + 3))
                    differences(j)
                for i, j in enumerate((2, 3, 0, 1)):
                    dve.wait_ge(sem("seg_expd"), g * 4 + (i + 1))
                    mdo(V.tensor_tensor(seg[:, j], seg[:, j], cbm[:], ALU.mult), "seg_ready")
                dve.wait_ge(sem("ssm_read"), g + 1)
                mdo(V.tensor_tensor(yT[:, :, TP:T], yT[:, :, TP:T],
                                    B[6][:, 0:2 * NB].rearrange("p (i b) -> p i b", i=2), ALU.add), "sample_y_read")
                if nxt is not None:
                    finish(nxt, 1 - d, 2)
                    taps(nxt, 1 - d, 3)
                    sample_taps(nxt, 1 - d)
                else:
                    ahead(0)
                dve.wait_ge(sem("ssd_added"), g + 1)
                if prev is not None:
                    dve.wait_ge(sem("pssm_out"), g * 16)
                for t in range(NT):
                    add = pair(4 + t // 2)[:, t % 2]
                    if t == 0:
                        mdo(V.tensor_copy(st[:, 0], add))
                        continue
                    mdo(V.tensor_tensor(std1[:], st[:, t - 1], dec[:, t].unsqueeze(2).to_broadcast((P, CJ, CHD)),
                                        ALU.mult))
                    mdo(V.tensor_tensor(st[:, t] if t < NT - 1 else pssm[:], std1[:], add, ALU.add),
                        "states_kept" if t == NT - 1 else None)
                if nxt is not None:
                    finish(nxt, 1 - d, 3)
                    finish_samples(nxt, 1 - d)
                else:
                    ahead(1)
                for i in range(2):
                    mdo(V.tensor_tensor(yT[:, i, 0:TP], yT[:, i, 0:TP], B[6 + i][:], ALU.add),
                        "y_read" if i else None)
                dve.wait_ge(sem("y_inter"), g + 1)
                dve.wait_ge(sem("decays_featured"), g * 4 + 4)
                for i in range(2):
                    mdo(V.tensor_tensor(ytmp[:, i], B[4 + i][:, P:TP], efeat[:, i], ALU.mult),
                        "y_scaled" if i else None)
                for i in range(2):
                    mdo(V.tensor_tensor(yT[:, i, P:TP], yT[:, i, P:TP], ytmp[:, i], ALU.add))
                n = T_SSD + 5
                dve.wait_ge(copied[n % 2], g * (SSD_UNITS // 2) + (turns_before(n) + 1))
                for i in range(2):
                    mdo(V.scalar_tensor_tensor(yT[:, i], yT[:, i], 0.5, gz[:, d, i], ALU.mult, ALU.mult),
                        "y_gated" if i else None)
                if nxt is not None:
                    gate(nxt, 1 - d, 0)
                dve.wait_ge(sem("y_squared"), g + 1)
                mdo(V.tensor_tensor(ysq[:, 0], ysq[:, 0], ysq[:, 1], ALU.add), "ysq_ready")
                if nxt is not None:
                    gate(nxt, 1 - d, 1)
                mix_tally.end()

            prepare(0, 0)
            for j in range(4):
                taps(0, 0, j)
                if j:
                    finish(0, 0, j - 1)
            sample_taps(0, 0)
            finish(0, 0, 3)
            finish_samples(0, 0)
            gate(0, 0, 0)
            gate(0, 0, 1)
            mix(0, 0, 1, None)
            with dve.Fori(0, (CG - 2) // 2) as i:
                mix(i * 2 + 1, 1, i * 2 + 2, i * 2)
                mix(i * 2 + 2, 0, i * 2 + 3, i * 2 + 1)
            mix(CG - 1, 1, None, CG - 2)
            normed(CG - 1, 1)
            ahead(2)
            ahead(3)
            do(V.memset(rstd[:], 0.0))
            for j in range(DC):
                residual(T_OUT1 + AHEAD + j, j, U_OUT1 + 2 * j + 2)
                add_and_weigh(3, j)
            dve.wait_ge(sem("layer1_out"), 32)
            dve.wait_ge(sem("pssm_out"), 16 * CG)
            dve.wait_ge(sem("ssm_out"), 16 * CG)
            mlp(3, T_UP1, T_DOWN1, U_UP1, U_DOWN1)
            dve.wait_ge(hn_ready, HN_BEFORE[4] + DC)
            for cols, _ in MATMULS:
                root(4, cols)
                for k in range(Y_SHARE):
                    V.tensor_tensor(hn[:, k, cols], hn[:, k, cols], rstd[:, cols], ALU.mult).then_inc(
                        sem("y_scaled_vector"), 1)



def _constants():
    k = np.arange(P)
    out = {}
    out["ident"] = np.eye(P)
    out["tri"] = k[:, None] <= k[None, :]
    half = AD // 2
    rot = np.zeros((P, P))
    for m in range(P):
        rot[m + half if m % AD < half else m - half, m] = -1.0 if m % AD < half else 1.0
    out["rotm"] = rot
    pos = np.concatenate([np.arange(TP), np.full(NB, WIN)]).astype(np.float32)
    freq = np.float32(10000.0) ** (-np.arange(half, dtype=np.float32) / np.float32(half))
    ang = (pos[None, :] * freq[k % half][:, None]).astype(np.float32)
    out["cos"], out["sin"] = np.cos(ang), np.sin(ang)
    dist = k[:, None] - np.arange(TP)[None, :] + (TP - P)
    count = sum(((dist >= 0) & (dist <= w) & (dist % d == 0)).astype(int) for w, d in BRANCHES)
    out["lncount"] = np.where(count > 0, np.log(np.maximum(count, 1)), NEVER)
    b = np.arange(NB)
    out["selb"] = np.broadcast_to((b[:, None] == b[None, :])[:, :, None], (NB, NB, P))
    out["rep"] = b[:, None] == np.arange(NB * AH)[None, :] // AH
    out["ownhead"] = np.arange(NB * AH)[:, None] % AH == np.arange(AW)[None, :] // AD
    out["delta"] = out["deltac"] = np.eye(NB)
    same = (k[:, None] // CH == k[None, :] // CH) & (k[:, None] <= k[None, :])
    out["tri64"] = same
    out = {n: np.ascontiguousarray(v, dtype=np.float32) for n, v in out.items()}
    out["mask64"] = np.ascontiguousarray(same.astype(np.uint32))
    return out


def _unit(w):
    return w.reshape(DC, P, P).transpose(1, 0, 2).reshape(P, DC * P)


def _columns(v):
    return v.reshape(-1, P).T


def kernel(**inputs):
    import concourse.bacc as bacc
    from concourse.bass_utils import run_bass_kernel_spmd

    x = {k: np.asarray(v) for k, v in inputs.items()}
    w_in, w_c = x["w_in_ab"][0], x["w_in_c"][0]
    q_b, g_low = 3 * AW, 3 * AW + 2 * BH * BK + BH * BV
    k_b, v_b, r_b = q_b + BH * BK, q_b + 2 * BH * BK, g_low + RANK
    starts = [i * AW + hp * P for hp in range(HP) for i in range(3)]
    for gp in range(GP):
        starts += [q_b + gp * P, k_b + gp * P, v_b + 2 * gp * P, v_b + (2 * gp + 1) * P,
                   r_b + 2 * gp * P, r_b + (2 * gp + 1) * P]
    units = [_unit(w_in[:, s:s + P]) for s in starts]
    units += [_unit(x["w_out_ab"][0][:, j * P:(j + 1) * P]) for j in range(DC)]

    def mlp(layer):
        up = [_unit(x["w_up"][layer][:, j * P:(j + 1) * P]) for j in range(FC)]
        return up + [_unit(x["w_down"][layer][q * D:(q + 1) * D, j * P:(j + 1) * P])
                     for j in range(DC) for q in range(FF // D)]

    units += mlp(0)
    for g in range(CG):
        for s in (CI + g * GW, CI + g * GW + P, 2 * CI + g * P, 2 * CI + CG * CN + g * P, g * GW, g * GW + P):
            units.append(_unit(w_c[:, s:s + P]))
    units += [_unit(x["w_out_c"][0][q * D:(q + 1) * D, j * P:(j + 1) * P])
              for j in range(DC) for q in range(CI // D)]
    units += mlp(1)
    arrays = {"units": np.stack(units)}
    assert len(units) == N_UNITS
    tokens = np.concatenate([x["x_prompt"][0], x["x_sample"][:, 0]])
    arrays["xT"] = tokens.T.reshape(DC, P, T).transpose(1, 0, 2)

    consts = _constants()
    norms = [_columns(v) for v in (x["norm_mix"][0], x["norm_mlp"][0], x["norm_mix"][1], x["norm_mlp"][1],
                                   x["norm_final"])]
    consts["normc"] = np.concatenate([np.ones((P, P), np.float32), *norms, np.full((P, 1), EPS, np.float32)], axis=1)
    consts["wglow"] = w_in[:, g_low:g_low + RANK].reshape(DC, P, RANK).transpose(1, 0, 2)
    consts["wgate"] = x["w_gate_b"][0]
    consts["bgate"] = _columns(x["b_gate_b"][0])
    consts["wonorm"] = x["w_onorm_b"][0][:, None]
    consts["wdt"] = w_c[:, CI + 2 * CI:].reshape(DC, P, CH_ALL).transpose(1, 0, 2)
    consts["dtb"] = np.broadcast_to(x["dt_bias"][0], (P, CH_ALL))
    consts["nega"] = np.broadcast_to(x["a_log"][0], (P, CH_ALL))

    def grouped(v):
        xs, bs, cs = v[..., :CI], v[..., CI:CI + CG * CN], v[..., CI + CG * CN:]
        blocks = np.concatenate([xs.reshape(*v.shape[:-1], CG, 2, P), bs.reshape(*v.shape[:-1], CG, 1, P),
                                 cs.reshape(*v.shape[:-1], CG, 1, P)], axis=-2)
        return np.moveaxis(blocks, (-1, -3, -2), (0, 1, 2))

    two = lambda v: v.reshape(CG, 2, P).transpose(2, 0, 1)
    consts["parm"] = np.concatenate([
        grouped(x["conv_w"][0]).reshape(P, CG, 4 * TAPS), grouped(x["conv_b"][0]),
        two(np.repeat(x["d_skip"][0], CHD)), two(x["w_gnorm_c"][0]),
        grouped(x["state_conv"][0].transpose(1, 0, 2)).reshape(P, CG, 4 * 3 * NB)], axis=2)
    arrays.update({"const_" + n: v for n, v in consts.items()})
    arrays["cache_k"] = x["cache_win_k"][0].reshape(NB, WIN, AW)
    arrays["cache_v"] = x["cache_win_v"][0].reshape(NB, WIN, AW)
    arrays["gla0"] = x["state_gla"][0].reshape(NB, GP, P, BV).transpose(1, 2, 0, 3)
    arrays["ssm0"] = x["state_ssm"][0].reshape(NB, CG, CJ * CHD, CN).transpose(1, 3, 0, 2).reshape(CG, CN, NB * GW)

    outs = {"y": (P, DC, T), "pk": (HP, P, TP), "pv": (HP, P, TP), "win_k": (NB, WIN, AW), "win_v": (NB, WIN, AW),
            "pgla": (GP, P, BV), "gla1": (GP, P, NB, BV), "pconv": (P, CG * 4 * 3), "sconv": (P, CG * 4 * 3 * NB),
            "pssm": (CG, P, GW), "ssm1": (CG, CN, NB * GW)}
    nc = bacc.Bacc("TRN2", target_bir_lowering=False, num_devices=1)
    aps = {}
    arrays = {n: np.ascontiguousarray(v) for n, v in arrays.items()}
    for n, v in arrays.items():
        aps[n] = nc.dram_tensor(n, v.shape, mybir.dt.from_np(v.dtype), kind="ExternalInput").ap()
    for n, shape in outs.items():
        aps[n] = nc.dram_tensor("out_" + n, shape, F32, kind="ExternalOutput").ap()
    aps["consts"] = {n: aps["const_" + n] for n in consts}
    build(nc, aps)
    r = run_bass_kernel_spmd(nc, [arrays], core_ids=[0]).results[0]
    got = {n: np.asarray(r["out_" + n]) for n in outs}

    y = got["y"].transpose(2, 1, 0).reshape(T, D)
    cached = lambda v: v.reshape(AW, TP).T.reshape(1, 1, TP, AH, AD)
    window = lambda v: v.reshape(1, NB, WIN, AH, AD)

    def ungrouped(v):
        v = np.moveaxis(v, 0, -1)
        v = np.moveaxis(v, 2, 0)
        n = v.shape[0]
        return np.concatenate([v[:, :, 0:2].reshape(n, CI), v[:, :, 2].reshape(n, CG * CN),
                               v[:, :, 3].reshape(n, CG * CN)], axis=1)

    pconv = ungrouped(got["pconv"].reshape(P, CG, 4, 3))
    sconv = ungrouped(got["sconv"].reshape(P, CG, 4, 3 * NB)).reshape(3, NB, 2 * CI).transpose(1, 0, 2)
    pssm = got["pssm"].transpose(0, 2, 1).reshape(1, 1, CH_ALL, CHD, CN)
    sssm = got["ssm1"].reshape(CG, CN, NB, CJ, CHD).transpose(2, 0, 3, 4, 1).reshape(1, NB, CH_ALL, CHD, CN)
    pgla = got["pgla"].reshape(1, 1, BH, BK, BV)
    sgla = got["gla1"].reshape(GP, 2, BK, NB, BV).transpose(3, 0, 1, 2, 4).reshape(1, NB, BH, BK, BV)
    return (y[:TP][None], y[TP:][:, None], cached(got["pk"]), cached(got["pv"]), pgla, pconv[None, None], pssm,
            window(got["win_k"]), window(got["win_v"]), sgla, sconv[None], sssm)
```
